# Optimizing a Trainium2 kernel written in Bass

```python
import jax, jax.numpy as jnp
from jax import lax
import numpy as np

D_MODEL = 1024
BATCH = 1
SEQ = 512
DEPTH = 1

D_MIX = D_MODEL
ATT_HEADS = 8
ATT_HEAD_DIM = 64
ATT_WIDTH = ATT_HEADS * ATT_HEAD_DIM
DILATED_PATTERNS = ((128, 1), (512, 4), (2048, 16))
Q_BLOCK = 128
ROPE_THETA = 10000.0
GLA_HEADS = 4
GLA_KEY_DIM = 64
GLA_VAL_DIM = 128
GLA_KEY_WIDTH = GLA_HEADS * GLA_KEY_DIM
GLA_VAL_WIDTH = GLA_HEADS * GLA_VAL_DIM
GLA_GATE_RANK = 16
GLA_GATE_NORMALIZER = 16.0
GLA_CHUNK = 64
IN_SPLITS = (ATT_WIDTH, ATT_WIDTH, ATT_WIDTH, GLA_KEY_WIDTH, GLA_KEY_WIDTH,
             GLA_VAL_WIDTH, GLA_VAL_WIDTH, GLA_GATE_RANK)
D_IN = sum(IN_SPLITS)
N_EXPERTS = 32
TOP_K = 4
D_FF = D_MODEL
SWIGLU_LIMIT = 7.0
SWIGLU_ALPHA = 1.702
MOE_BLOCK = 128
NORM_EPS = 1e-6
N_MOD = 6


def rms_norm(x, g):
    xf = x.astype(jnp.float32)
    y = xf * lax.rsqrt(jnp.mean(xf * xf, axis=-1, keepdims=True) + NORM_EPS)
    return (y * g.astype(jnp.float32)).astype(x.dtype)

def rope(x, positions):
    half = x.shape[-1] // 2
    inv_freq = ROPE_THETA ** (-jnp.arange(half, dtype=jnp.float32) / half)
    ang = positions.astype(jnp.float32)[:, None] * inv_freq[None, :]
    cos, sin = jnp.cos(ang), jnp.sin(ang)
    xf = x.astype(jnp.float32)
    x1, x2 = xf[..., :half], xf[..., half:]
    return jnp.concatenate([x1 * cos - x2 * sin, x2 * cos + x1 * sin], axis=-1).astype(x.dtype)

def dilated_attention(q, k, v):
    B, H, S, hd = q.shape
    n_blk = S // Q_BLOCK

    def block(i):
        q0 = i * Q_BLOCK
        qb = lax.dynamic_slice_in_dim(q, q0, Q_BLOCK, axis=2).astype(jnp.float32)
        t = q0 + jnp.arange(Q_BLOCK)
        outs, lses = [], []
        for window, dil in DILATED_PATTERNS:
            offs = jnp.arange(window // dil + 1) * dil
            idx = t[:, None] - offs[None, :]
            valid = idx >= 0
            idx = jnp.maximum(idx, 0)
            kg = jnp.take(k, idx, axis=2).astype(jnp.float32)
            vg = jnp.take(v, idx, axis=2).astype(jnp.float32)
            s = jnp.einsum('bhqd,bhqjd->bhqj', qb, kg)
            s = jnp.where(valid, s, -jnp.inf)
            m = jnp.max(s, axis=-1, keepdims=True)
            p = jnp.exp(s - m)
            l = jnp.sum(p, axis=-1, keepdims=True)
            outs.append(jnp.einsum('bhqj,bhqjd->bhqd', p, vg) / l)
            lses.append(m + jnp.log(l))
        w = jax.nn.softmax(jnp.stack(lses, axis=0), axis=0)
        return jnp.sum(w * jnp.stack(outs, axis=0), axis=0)

    o = lax.map(block, jnp.arange(n_blk))
    o = o.transpose(1, 0, 3, 2, 4).reshape(B, S, H * hd)
    return o.astype(q.dtype)

def gated_linear_attention(q, k, v, log_a):
    B, H, S, dk = q.shape
    dv = v.shape[-1]
    C = GLA_CHUNK
    N = S // C
    qf = q.astype(jnp.float32).reshape(B, H, N, C, dk) * (dk ** -0.5)
    kf = k.astype(jnp.float32).reshape(B, H, N, C, dk)
    vf = v.astype(jnp.float32).reshape(B, H, N, C, dv)
    b = jnp.cumsum(log_a.reshape(B, H, N, C, dk), axis=3)
    b_last = b[:, :, :, -1:, :]
    q_dec = qf * jnp.exp(b)
    att = jnp.einsum('bhncd,bhnjd->bhncj', q_dec, kf * jnp.exp(-b))
    causal = jnp.tril(jnp.ones((C, C), dtype=bool))
    att = jnp.where(causal, att, 0.0)
    o_intra = jnp.einsum('bhncj,bhnje->bhnce', att, vf)
    u = jnp.einsum('bhncd,bhnce->nbhde', kf * jnp.exp(b_last - b), vf)
    a = jnp.exp(b_last[:, :, :, 0, :]).transpose(2, 0, 1, 3)

    def step(state, inp):
        a_n, u_n = inp
        return a_n[..., None] * state + u_n, state

    _, s_prev = lax.scan(step, jnp.zeros((B, H, dk, dv), jnp.float32), (a, u))
    o_inter = jnp.einsum('bhncd,nbhde->bhnce', q_dec, s_prev)
    return (o_intra + o_inter).reshape(B, H, S, dv)

def hybrid_mixer(h, w_in, w_gate_lr, b_gate, g_gla, w_out):
    B, S, _ = h.shape
    proj = h @ w_in
    split_points = [int(s) for s in np.cumsum(IN_SPLITS)[:-1]]
    q_a, k_a, v_a, q_g, k_g, v_g, r_g, g_lr = jnp.split(proj, split_points, axis=-1)

    def heads(t, n):
        return t.reshape(B, S, n, -1).transpose(0, 2, 1, 3)

    pos = jnp.arange(S)
    qa = rope(heads(q_a, ATT_HEADS), pos) * (ATT_HEAD_DIM ** -0.5)
    ka = rope(heads(k_a, ATT_HEADS), pos)
    o_att = dilated_attention(qa, ka, heads(v_a, ATT_HEADS))
    gate_logit = (g_lr @ w_gate_lr + b_gate).astype(jnp.float32)
    log_a = jax.nn.log_sigmoid(gate_logit) / GLA_GATE_NORMALIZER
    o_g = gated_linear_attention(heads(q_g, GLA_HEADS), heads(k_g, GLA_HEADS),
                                 heads(v_g, GLA_HEADS), heads(log_a, GLA_HEADS))
    o_g = rms_norm(o_g, g_gla)
    o_g = o_g.transpose(0, 2, 1, 3).reshape(B, S, GLA_VAL_WIDTH).astype(h.dtype) * jax.nn.silu(r_g)
    return jnp.concatenate([o_att, o_g], axis=-1) @ w_out

def moe_ffn(h, router_w, router_b, w_gate_up, b_gate_up, w_down, b_down):
    B, S, D = h.shape
    T = B * S
    xt = h.reshape(T, D)
    logits = (xt @ router_w + router_b).astype(jnp.float32)
    top_v, top_i = lax.top_k(logits, TOP_K)
    gates = jax.nn.softmax(top_v, axis=-1)
    A = T * TOP_K
    e_flat = top_i.reshape(A)
    tok_flat = jnp.arange(A, dtype=jnp.int32) // TOP_K
    g_flat = gates.reshape(A)
    order = jnp.argsort(e_flat)
    e_sorted = e_flat[order]
    counts = jnp.bincount(e_flat, length=N_EXPERTS)
    start = jnp.cumsum(counts) - counts
    padded = (counts + MOE_BLOCK - 1) // MOE_BLOCK * MOE_BLOCK
    pend = jnp.cumsum(padded)
    pstart = pend - padded
    dest = pstart[e_sorted] + jnp.arange(A, dtype=jnp.int32) - start[e_sorted]
    n_blocks = -(-(A + N_EXPERTS * (MOE_BLOCK - 1)) // MOE_BLOCK)
    P = n_blocks * MOE_BLOCK
    tok_buf = jnp.full((P,), T, dtype=jnp.int32).at[dest].set(tok_flat[order])
    gate_buf = jnp.zeros((P,), jnp.float32).at[dest].set(g_flat[order])
    blk_e = jnp.minimum(jnp.searchsorted(pend, jnp.arange(n_blocks) * MOE_BLOCK, side='right'),
                        N_EXPERTS - 1)
    xpad = jnp.concatenate([xt, jnp.zeros((1, D), xt.dtype)], axis=0)

    def expert_block(args):
        idx, e = args
        xb = xpad[idx]
        gu = xb @ w_gate_up[e] + b_gate_up[e]
        x_glu = jnp.minimum(gu[:, ::2], SWIGLU_LIMIT)
        x_lin = jnp.clip(gu[:, 1::2], -SWIGLU_LIMIT, SWIGLU_LIMIT)
        act = x_glu * jax.nn.sigmoid(SWIGLU_ALPHA * x_glu) * (x_lin + 1.0)
        return act @ w_down[e] + b_down[e]

    out_buf = lax.map(expert_block, (tok_buf.reshape(n_blocks, MOE_BLOCK), blk_e))
    out_buf = out_buf.reshape(P, D) * gate_buf[:, None].astype(out_buf.dtype)
    out = jnp.zeros((T + 1, D), out_buf.dtype).at[tok_buf].add(out_buf)
    return out[:T].reshape(B, S, D)

def first_inputs(seed: int = 0) -> dict:
    key = jax.random.key(seed)
    ks = jax.random.split(key, 20)
    L = DEPTH

    def nrm(k, shape, scale):
        return jax.random.normal(k, shape, jnp.float32) * scale

    return {
        "x": nrm(ks[0], (BATCH, SEQ, D_MODEL), 1.0),
        "c": nrm(ks[1], (BATCH, D_MODEL), 1.0),
        "w_mod": nrm(ks[2], (L, D_MODEL, N_MOD * D_MODEL), 0.5 * D_MODEL ** -0.5),
        "b_mod": nrm(ks[3], (L, N_MOD * D_MODEL), 0.02),
        "g_pre_mix": 1.0 + nrm(ks[4], (L, D_MODEL), 0.05),
        "w_in": nrm(ks[5], (L, D_MODEL, D_IN), D_MODEL ** -0.5),
        "w_gate_lr": nrm(ks[6], (L, GLA_GATE_RANK, GLA_KEY_WIDTH), GLA_GATE_RANK ** -0.5),
        "b_gate": nrm(ks[7], (L, GLA_KEY_WIDTH), 0.1),
        "g_gla": 1.0 + nrm(ks[8], (L, GLA_VAL_DIM), 0.05),
        "w_out": nrm(ks[9], (L, D_MIX, D_MODEL), D_MIX ** -0.5),
        "g_post_mix": 1.0 + nrm(ks[10], (L, D_MODEL), 0.05),
        "g_pre_ffn": 1.0 + nrm(ks[11], (L, D_MODEL), 0.05),
        "router_w": nrm(ks[12], (L, D_MODEL, N_EXPERTS), D_MODEL ** -0.5),
        "router_b": nrm(ks[13], (L, N_EXPERTS), 0.01),
        "w_gate_up": nrm(ks[14], (L, N_EXPERTS, D_MODEL, 2 * D_FF), D_MODEL ** -0.5),
        "b_gate_up": nrm(ks[15], (L, N_EXPERTS, 2 * D_FF), 0.02),
        "w_down": nrm(ks[16], (L, N_EXPERTS, D_FF, D_MODEL), D_FF ** -0.5),
        "b_down": nrm(ks[17], (L, N_EXPERTS, D_MODEL), 0.02),
        "g_post_ffn": 1.0 + nrm(ks[18], (L, D_MODEL), 0.05),
    }

def first_block(x, c, w_mod, b_mod, g_pre_mix, w_in, w_gate_lr, b_gate, g_gla, w_out,
              g_post_mix, g_pre_ffn, router_w, router_b, w_gate_up, b_gate_up,
              w_down, b_down, g_post_ffn):
    for l in range(DEPTH):
        mod = jax.nn.silu(c) @ w_mod[l] + b_mod[l]
        shift1, scale1, gate1, shift2, scale2, gate2 = jnp.split(mod[:, None, :], N_MOD, axis=-1)
        h = rms_norm(x, g_pre_mix[l]) * (1.0 + scale1) + shift1
        y = hybrid_mixer(h, w_in[l], w_gate_lr[l], b_gate[l], g_gla[l], w_out[l])
        x = x + gate1 * rms_norm(y, g_post_mix[l])
        h = rms_norm(x, g_pre_ffn[l]) * (1.0 + scale2) + shift2
        y = moe_ffn(h, router_w[l], router_b[l], w_gate_up[l], b_gate_up[l], w_down[l], b_down[l])
        x = x + gate2 * rms_norm(y, g_post_ffn[l])
    return x


CHUNK = 64
D_MIX_2 = D_MODEL
D_POOL = D_MIX_2 // 2
POOL_WINDOWS = (2, 4, 8, 16)
N_POOL_GROUPS = len(POOL_WINDOWS)
POOL_GROUP = D_POOL // N_POOL_GROUPS
D_RWKV = D_MIX_2 - D_POOL
RWKV_HEAD = 64
N_RWKV_HEADS = D_RWKV // RWKV_HEAD
DECAY_LORA = 64
AAA_LORA = 64
D_SHIFT = 3 * D_RWKV + DECAY_LORA + AAA_LORA
D_IN_2 = 2 * D_POOL + D_SHIFT + D_RWKV
GN_EPS = 64e-5


def rmsnorm(x, gain):
    x32 = x.astype(jnp.float32)
    inv = lax.rsqrt(jnp.mean(x32 * x32, axis=-1, keepdims=True) + NORM_EPS)
    return (x32 * inv * gain.astype(jnp.float32)).astype(x.dtype)

def multi_scale_pool(u, pool_w, pool_scale):
    B, S, _ = u.shape
    u32 = u.astype(jnp.float32).reshape(B, S, N_POOL_GROUPS, POOL_GROUP)
    cs = jnp.cumsum(u32, axis=1)
    cs0 = jnp.concatenate([jnp.zeros_like(cs[:, :1]), cs], axis=1)
    pos = jnp.arange(S)
    outs = []
    for g, w in enumerate(POOL_WINDOWS):
        hi = cs[:, :, g]
        lo = jnp.concatenate([jnp.zeros((B, w - 1, POOL_GROUP), jnp.float32),
                              cs0[:, :S + 1 - w, g]], axis=1)
        cnt = jnp.minimum(pos + 1, w).astype(jnp.float32)[None, :, None]
        outs.append((hi - lo) / cnt - u32[:, :, g])
    pooled = jnp.stack(outs, axis=2)
    mixed = jnp.einsum('bsgc,gcd->bsgd', pooled, pool_w.astype(jnp.float32))
    return (mixed.reshape(B, S, D_POOL) * pool_scale.astype(jnp.float32)).astype(u.dtype)

def rwkv7_time_mix(feat, w0, w_up, a0, a_up, k_k, k_a, r_k, gn_gain, gn_bias):
    B, S, _ = feat.shape
    H, N = N_RWKV_HEADS, RWKV_HEAD
    f = feat.astype(jnp.float32)
    r = f[..., :D_RWKV]
    k = f[..., D_RWKV:2 * D_RWKV]
    v = f[..., 2 * D_RWKV:3 * D_RWKV]
    w_lr = f[..., 3 * D_RWKV:3 * D_RWKV + DECAY_LORA]
    a_lr = f[..., 3 * D_RWKV + DECAY_LORA:]
    ww = w0.astype(jnp.float32) + jnp.tanh(w_lr) @ w_up.astype(jnp.float32)
    decay = jnp.exp(-jnp.exp(-jax.nn.softplus(-ww) - 0.5))
    a = jax.nn.sigmoid(a0.astype(jnp.float32) + a_lr @ a_up.astype(jnp.float32))
    heads = lambda t: t.reshape(B, S, H, N)
    kk = heads(k * k_k.astype(jnp.float32))
    kk = kk / jnp.maximum(jnp.sqrt(jnp.sum(kk * kk, axis=-1, keepdims=True)), 1e-12)
    k = k * (1.0 + (a - 1.0) * k_a.astype(jnp.float32))
    r, k, v, decay, a = heads(r), heads(k), heads(v), heads(decay), heads(a)

    def step(state, inp):
        r_t, k_t, v_t, w_t, kk_t, a_t = inp
        sa = jnp.einsum('bhvk,bhk->bhv', state, -kk_t)
        state = (state * w_t[:, :, None, :]
                 + sa[..., None] * (kk_t * a_t)[:, :, None, :]
                 + v_t[..., None] * k_t[:, :, None, :])
        y_t = jnp.einsum('bhvk,bhk->bhv', state, r_t)
        return state, y_t

    tm = lambda t: jnp.moveaxis(t, 1, 0)
    state0 = jnp.zeros((B, H, N, N), jnp.float32)
    _, y = lax.scan(step, state0, (tm(r), tm(k), tm(v), tm(decay), tm(kk), tm(a)))
    y = jnp.moveaxis(y, 0, 1)
    mu = jnp.mean(y, axis=-1, keepdims=True)
    var = jnp.mean(jnp.square(y - mu), axis=-1, keepdims=True)
    y = (y - mu) * lax.rsqrt(var + GN_EPS)
    y = y * gn_gain.astype(jnp.float32).reshape(H, N) + gn_bias.astype(jnp.float32).reshape(H, N)
    bonus = jnp.sum(r * k * r_k.astype(jnp.float32), axis=-1, keepdims=True) * v
    return (y + bonus).reshape(B, S, D_RWKV)

def second_inputs(seed: int = 0) -> dict:
    key = jax.random.key(seed)
    ks = jax.random.split(key, 20)
    f32 = jnp.float32
    nrm = lambda k, shape, s: jax.random.normal(k, shape, f32) * s
    x = jax.random.normal(ks[0], (BATCH, SEQ, D_MODEL), f32)
    norm_gain = 1.0 + nrm(ks[1], (DEPTH, D_MODEL), 0.05)
    w_in = nrm(ks[2], (DEPTH, D_MODEL, D_IN_2), D_MODEL ** -0.5)
    pool_w = nrm(ks[3], (DEPTH, N_POOL_GROUPS, POOL_GROUP, POOL_GROUP), POOL_GROUP ** -0.5)
    pool_scale = 1.0 + nrm(ks[4], (DEPTH, D_POOL), 0.05)
    shift_mu = jax.random.uniform(ks[5], (DEPTH, D_SHIFT), f32, 0.0, 1.0)
    w0 = jax.random.uniform(ks[6], (DEPTH, D_RWKV), f32, -4.0, 2.0)
    w_up = nrm(ks[7], (DEPTH, DECAY_LORA, D_RWKV), 0.1)
    a0 = nrm(ks[8], (DEPTH, D_RWKV), 0.1)
    a_up = nrm(ks[9], (DEPTH, AAA_LORA, D_RWKV), 0.5 * AAA_LORA ** -0.5)
    k_k = 0.85 + nrm(ks[10], (DEPTH, D_RWKV), 0.05)
    k_a = 1.0 + nrm(ks[11], (DEPTH, D_RWKV), 0.05)
    r_k = nrm(ks[12], (DEPTH, N_RWKV_HEADS, RWKV_HEAD), 0.1)
    gn_gain = 1.0 + nrm(ks[13], (DEPTH, D_RWKV), 0.05)
    gn_bias = nrm(ks[14], (DEPTH, D_RWKV), 0.02)
    w_out = nrm(ks[15], (DEPTH, D_MIX_2, D_MODEL), D_MIX_2 ** -0.5)
    final_gain = 1.0 + nrm(ks[16], (D_MODEL,), 0.05)
    return {"x": x, "norm_gain": norm_gain, "w_in": w_in, "pool_w": pool_w,
            "pool_scale": pool_scale, "shift_mu": shift_mu, "w0": w0, "w_up": w_up,
            "a0": a0, "a_up": a_up, "k_k": k_k, "k_a": k_a, "r_k": r_k,
            "gn_gain": gn_gain, "gn_bias": gn_bias, "w_out": w_out, "final_gain": final_gain}

def second_block(x, norm_gain, w_in, pool_w, pool_scale, shift_mu, w0, w_up, a0, a_up,
              k_k, k_a, r_k, gn_gain, gn_bias, w_out, final_gain):
    for l in range(DEPTH):
        h = rmsnorm(x, norm_gain[l])
        z = h @ w_in[l]
        u_a = z[..., :D_POOL]
        g_a = z[..., D_POOL:2 * D_POOL]
        sh = z[..., 2 * D_POOL:2 * D_POOL + D_SHIFT]
        g_b = z[..., 2 * D_POOL + D_SHIFT:]
        sh_prev = jnp.pad(sh, ((0, 0), (1, 0), (0, 0)))[:, :-1]
        sh = sh + shift_mu[l] * (sh_prev - sh)
        y_a = multi_scale_pool(u_a, pool_w[l], pool_scale[l])
        y_b = rwkv7_time_mix(sh, w0[l], w_up[l], a0[l], a_up[l], k_k[l], k_a[l],
                             r_k[l], gn_gain[l], gn_bias[l]).astype(x.dtype)
        y = jnp.concatenate([y_a * jax.nn.silu(g_a), y_b * jax.nn.silu(g_b)], axis=-1)
        x = x + y @ w_out[l]
    return rmsnorm(x, final_gain)


def setup_inputs(seed=0):
    out = dict(first_inputs(seed))
    for name, value in second_inputs(seed + 1).items():
        if name != "x":
            out[name + "_2"] = value
    return out


def reference(
    x, c, w_mod, b_mod, g_pre_mix, w_in, w_gate_lr, b_gate, g_gla, w_out, g_post_mix, g_pre_ffn,
    router_w, router_b, w_gate_up, b_gate_up, w_down, b_down, g_post_ffn, norm_gain_2, w_in_2,
    pool_w_2, pool_scale_2, shift_mu_2, w0_2, w_up_2, a0_2, a_up_2, k_k_2, k_a_2, r_k_2,
    gn_gain_2, gn_bias_2, w_out_2, final_gain_2,
):
    x = first_block(
        x, c, w_mod, b_mod, g_pre_mix, w_in, w_gate_lr, b_gate, g_gla, w_out, g_post_mix,
        g_pre_ffn, router_w, router_b, w_gate_up, b_gate_up, w_down, b_down, g_post_ffn,
    )
    return second_block(
        x, norm_gain_2, w_in_2, pool_w_2, pool_scale_2, shift_mu_2, w0_2, w_up_2, a0_2, a_up_2,
        k_k_2, k_a_2, r_k_2, gn_gain_2, gn_bias_2, w_out_2, final_gain_2,
    )


_drawn_inputs = setup_inputs


def setup_inputs(seed=0):
    import zlib

    import numpy as np

    out = dict(_drawn_inputs(seed))
    spreads = {}
    factors = {'b_gate_up': 6.79,
     'b_down': 8.0,
     'g_post_ffn': 3.218,
     'pool_scale_2': 3.828,
     'a0_2': 3.377,
     'k_k_2': 7.205,
     'k_a_2': 2.739,
     'gn_gain_2': 3.206,
     'gn_bias_2': 7.855}
    for name, (base, spread) in spreads.items():
        noise = np.random.default_rng([zlib.crc32(name.encode()), seed]).standard_normal(out[name].shape)
        drawn = base * np.exp(spread * noise) if base else spread * noise
        out[name] = __import__('jax').numpy.asarray(drawn.astype(out[name].dtype))
    for name, factor in factors.items():
        out[name] = (out[name] * factor).astype(out[name].dtype)
    return out
```

```python
from contextlib import ExitStack

import numpy as np
import concourse.bass as bass
from concourse import mybir

F32 = mybir.dt.float32
I32 = mybir.dt.int32
U32 = mybir.dt.uint32
ALU = mybir.AluOpType
ACT = mybir.ActivationFunctionType
AX = mybir.AxisListType

P = 128
S = 512
NT = S // P
D = 1024
KT = D // P
HA, DA = 8, 64
HG, DK, DV = 4, 64, 128
RANK = 16
D_IN = 3 * HA * DA + 2 * HG * DK + 2 * HG * DV + RANK
QA, KA, VA = 0, 512, 1024
QG, KG, VG, RG, LR = 1536, 1792, 2048, 2560, 3072
NE, TOPK = 32, 4
SLOTS = 128
EXTRA = (S * TOPK) // (SLOTS + 1)
NBLK = NE + EXTRA
NM = 8
GN_EPS = 64e-5
EPS = 1e-6
LIMIT, ALPHA = 7.0, 1.702
CH = 64
D_IN2 = 3200
NF2 = D_IN2 // P
LOG_DECAY = float(np.exp(-0.5))
WINDOWS = (2, 4, 8, 16)

MU0, W00, A00, KK0, KA0, RK0, GG0, GB0, PS0, C0 = 0, 13, 17, 21, 25, 29, 33, 37, 41, 45
NCOL = 53

IDENT, ONES, BLOCK, CUM, SUF, BEFORE, LT, LE = range(8)
LEVEL0 = 8
NSQ = LEVEL0 + 7
NSQ_KEPT = 8


def square_constants():
    i = np.arange(P)[:, None]
    j = np.arange(P)[None, :]
    same = i // CH == j // CH
    m = np.zeros((NSQ, P, P), np.float32)
    m[IDENT] = i == j
    m[ONES] = 1.0
    m[BLOCK] = same
    m[CUM] = (same & (i <= j)) / 16.0
    m[SUF] = (same & (i > j)) / 16.0
    m[BEFORE] = i < j
    m[LT] = same & (i < j)
    m[LE] = same & (i <= j)
    for n in range(5):
        s = 2 << n
        m[LEVEL0 + n] = (i // (2 * s) == j // (2 * s)) & (i // s < j // s)
    m[LEVEL0 + 5] = (i // 2 == j // 2) & (i < j)
    m[LEVEL0 + 6] = (i // 2 == j // 2) & (i > j)
    return np.ascontiguousarray(m.transpose(1, 0, 2))


def attention_constant():
    t = np.arange(S)[:, None]
    j = np.arange(S)[None, :]
    d = t - j
    n = sum(((d >= 0) & (d % dil == 0) & (d <= window)).astype(np.float64)
            for window, dil in ((128, 1), (512, 4), (2048, 16)))
    m = np.where(n > 0, np.log(np.maximum(n, 1)), -1e30).astype(np.float32)
    return np.ascontiguousarray(m.reshape(NT, P, S).transpose(1, 0, 2))


def rope_constant():
    half = DA // 2
    freq = (10000.0 ** (-np.arange(half, dtype=np.float32) / half)).astype(np.float32)
    ang = np.arange(S, dtype=np.float32)[:, None] * freq[None, :]
    cs = np.stack([np.cos(ang), np.sin(ang)], 1).astype(np.float32)
    both = np.stack([cs * DA ** -0.5, cs], 1)
    return np.ascontiguousarray(both.reshape(NT, P, 2, 2, half).transpose(1, 0, 2, 3, 4))


def route_constant():
    m = np.zeros((5, NE), np.float32)
    m[0] = np.arange(NE)
    m[1] = np.arange(NE) * SLOTS
    m[2] = np.arange(NE)
    m[3] = (NE - 1) * SLOTS
    return np.ascontiguousarray(np.broadcast_to(m, (P, 5, NE)))


def pool_constant():
    pos = np.arange(16)
    m = np.stack([1.0 / np.minimum(pos + 1, w) for w in WINDOWS]).astype(np.float32)
    return np.ascontiguousarray(np.broadcast_to(m, (P, 4, 16)))


class Chain:

    def __init__(self, sem):
        self.sem, self.n = sem, 0

    def on(self, eng):
        def chained(ins):
            self.n += 1
            ins.then_inc(self.sem, 1)
            eng.wait_ge(self.sem, self.n)
        return chained


class Core:

    def __init__(self, nc, ctx, dram):
        self.nc, self.ctx, self.d = nc, ctx, dram
        self.sb = lambda n, s, dt=F32, at=None: (at or ctx).enter_context(nc.sbuf_tensor(n, s, dt))
        self.sem = lambda n: ctx.enter_context(nc.semaphore(n))
        self.pp = [ctx.enter_context(nc.psum_tensor(f"banks{j}", [P, 1024], F32)) for j in range(4)]
        self.dve_chain = Chain(self.sem("dve_chain"))
        self.act_chain = Chain(self.sem("act_chain"))
        self.pool_chain = Chain(self.sem("pool_chain"))

    def stage_semaphores(self, ctx):
        own = []

        def give_back():
            self.nc.clear_and_free_semaphores(own)
            self.nc.all_engine_barrier()

        def sem(name):
            own.append(self.nc.alloc_semaphore(name))
            return own[-1]

        ctx.callback(give_back)
        return sem

    def bank(self, n):
        return self.pp[n // 2][:, (n % 2) * 512:(n % 2) * 512 + 512]


def flat(ap):
    return ap.rearrange("p a b -> p (a b)")


def stage_front(k, front):
    nc, d = k.nc, k.d
    k.x = k.sb("x", [P, NT, D])
    k.eps = k.sb("eps", [P, 2])
    k.gate2 = k.sb("gate2", [P, D])
    k.sq = k.sb("sq", [P, NSQ_KEPT, P])
    k.dest = k.sb("dest", [P, NT, TOPK], I32)
    k.gates = k.sb("gates", [P, NT, TOPK])
    k.gateT = k.sb("gateT", [NE, S])
    k.table = k.sb("table", [1, 2 * NE + 1], I32)
    k.mod = k.sb("mod", [P, 6, D], at=front)
    k.proj = k.sb("proj", [P, NT, D_IN], at=front)
    with ExitStack() as ctx:
        sb = lambda n, s, dt=F32: k.sb(n, s, dt, at=ctx)
        sem = k.stage_semaphores(ctx)
        hT = sb("hT", [P, KT, S])
        stage = sb("stage", [P, 3, KT, 512])
        gain = sb("gain", [P, 2, D])
        col = sb("col_c", [P, KT])
        ccol = sb("ccol", [P, 3, KT])
        cb = sb("cb", [P, KT, P])
        h = sb("h", [P, 2, D])
        sumsq = sb("sumsq", [P, NT])
        rstd = sb("rstd", [P, NT])
        small_in = sem("small_in")
        eps_set = sem("eps_set")
        x_in = sem("x_in")
        gain_in = [sem(f"gain_in{i}") for i in range(2)]
        gain_used = sem("gain_used")
        stage_in = [sem(f"stage_in{i}") for i in range(3)]
        stage_used = sem("stage_used")
        c_exp = sem("c_exp")
        c_ready = sem("c_ready")
        mod_ps = sem("mod_ps")
        mod_done = sem("mod_done")
        sumsq_ready = sem("sumsq_ready")
        root_ready = sem("root_ready")
        h_ready = sem("h_ready")
        h_turned = sem("h_turned")
        hT_ready = sem("hT_ready")
        proj_ps = sem("proj_ps")
        proj_done = sem("proj_done")
        w_in = d["w_in"].rearrange("(k p) n -> p k n", p=P)
        w_mod = d["w_mod"].rearrange("(k p) n -> p k n", p=P)
        items = [("mod", j) for j in range(4)] + [("in", j) for j in range(7)] + \
                [("mod", j) for j in range(4, 12)]
        gains = ["g_pre_mix", "g_post_mix", "g_pre_ffn", "g_post_ffn"]

        with nc.Block() as block:
            @block.sync
            def _(sp):
                sp.dma_start(col[:], d["cols"][:, C0:C0 + KT]).then_inc(small_in, 16)
                for n, (kind, j) in enumerate(items):
                    if n >= 3:
                        sp.wait_ge(stage_used, n - 2)
                    w = w_mod[:, :, j * 512:(j + 1) * 512] if kind == "mod" else \
                        w_in[:, :, j * 512:min((j + 1) * 512, D_IN)]
                    sp.dma_start(stage[:, n % 3, :, 0:w.shape[2]], w).then_inc(stage_in[n % 3], 16)

            @block.scalar
            def _(act):
                chain = k.act_chain.on(act)
                act.dma_start(k.sq[:], d["square"][:, 0:NSQ_KEPT, :]).then_inc(small_in, 16)
                act.dma_start(flat(k.mod[:]), d["b_mod"][0:1, :].partition_broadcast(P).rearrange(
                    "p a n -> p (a n)")).then_inc(small_in, 16)
                act.dma_start(k.x[:], d["x"].rearrange("(t p) n -> p t n", p=P)).then_inc(x_in, 16)
                act.wait_ge(small_in, 48)
                act.activation(ccol[:, 0, :], col[:], ACT.Exp, scale=-1.0).then_inc(c_exp, 1)
                act.wait_ge(eps_set, 2)
                act.wait_ge(x_in, 16)
                for t in range(NT):
                    act.activation(k.proj[:, t, 0:D], k.x[:, t, :], ACT.Square,
                                   accum_out=sumsq[:, t:t + 1]).then_inc(sumsq_ready, 1)
                act.wait_ge(sumsq_ready, NT)
                act.activation(rstd[:], sumsq[:], ACT.Sqrt, scale=1.0 / D,
                               bias=k.eps[:, 0:1]).then_inc(root_ready, 1)
                for t in range(NT):
                    for half in range(2):
                        act.wait_ge(h_turned, 2 * t + half + 1)
                        act.activation(hT[:, 4 * half:4 * half + 4, t * P:(t + 1) * P],
                                       k.bank(2 + half).rearrange("p (a b) -> p a b", b=P),
                                       ACT.Copy).then_inc(hT_ready, 1)
                for j in range(7):
                    n = min(512, D_IN - j * 512)
                    for t in range(NT):
                        act.wait_ge(proj_ps, j * NT + t + 1)
                        act.activation(k.proj[:, t, j * 512:j * 512 + n], k.bank(4 + t)[:, 0:n],
                                       ACT.Copy).then_inc(proj_done, 1)

            @block.gpsimd
            def _(pool):
                for n in range(2):
                    pool.dma_start(gain[:, n, :], d[gains[n]][0:1, :].partition_broadcast(P).rearrange(
                        "p a n -> p (a n)")).then_inc(gain_in[n], 16)
                for n in range(2):
                    pool.wait_ge(gain_used, n + 1)
                    pool.dma_start(gain[:, n, :], d[gains[2 + n]][0:1, :].partition_broadcast(P).rearrange(
                        "p a n -> p (a n)")).then_inc(gain_in[n], 16)

            @block.tensor
            def _(pe):
                def mod_chunk(n, j):
                    pe.wait_ge(stage_in[n % 3], 16 * (n // 3 + 1))
                    if j >= 2:
                        pe.wait_ge(mod_done, j - 1)
                    for q in range(KT):
                        mm = pe.matmul(k.bank(j % 2), cb[:, q, :], stage[:, n % 3, q, :],
                                       start=(q == 0), stop=(q == KT - 1))
                    mm.then_inc(mod_ps, 1)
                    pe.wait_ge(mod_ps, j + 1)
                    pe.sem_inc(stage_used, 1)

                pe.wait_ge(c_ready, 1)
                pe.wait_ge(small_in, 48)
                for n in range(4):
                    mod_chunk(n, n)
                for t in range(NT):
                    pe.wait_ge(h_ready, t + 1)
                    if t:
                        pe.wait_ge(hT_ready, 2 * t)
                    for q in range(KT):
                        mm = pe.transpose(k.bank(2 + q // 4)[:, (q % 4) * P:(q % 4 + 1) * P],
                                          h[:, t % 2, q * P:(q + 1) * P], k.sq[:, IDENT, :])
                        if q % 4 == 3:
                            mm.then_inc(h_turned, 1)
                pe.wait_ge(hT_ready, 2 * NT)
                for n in range(4, 11):
                    j = n - 4
                    w = min(512, D_IN - j * 512)
                    pe.wait_ge(stage_in[n % 3], 16 * (n // 3 + 1))
                    for t in range(NT):
                        if j:
                            pe.wait_ge(proj_done, (j - 1) * NT + t + 1)
                        for q in range(KT):
                            mm = pe.matmul(k.bank(4 + t)[:, 0:w], hT[:, q, t * P:(t + 1) * P],
                                           stage[:, n % 3, q, 0:w], start=(q == 0), stop=(q == KT - 1))
                        mm.then_inc(proj_ps, 1)
                    pe.wait_ge(proj_ps, (j + 1) * NT)
                    pe.sem_inc(stage_used, 1)
                for n in range(11, 19):
                    mod_chunk(n, n - 7)

            @block.vector
            def _(dve):
                chain = k.dve_chain.on(dve)
                dve.memset(k.eps[:, 0:1], EPS).then_inc(eps_set, 1)
                dve.memset(k.eps[:, 1:2], GN_EPS).then_inc(eps_set, 1)
                dve.wait_ge(c_exp, 1)
                chain(dve.tensor_scalar(ccol[:, 1, :], ccol[:, 0, :], 1.0, None, ALU.add))
                chain(dve.reciprocal(ccol[:, 2, :], ccol[:, 1, :]))
                chain(dve.tensor_tensor(ccol[:, 1, :], ccol[:, 2, :], col[:], ALU.mult))
                dve.tensor_copy(cb[:], ccol[:, 1, :].unsqueeze(2).broadcast_to([P, KT, P])).then_inc(c_ready, 1)

                def mod_add(j):
                    dve.wait_ge(mod_ps, j + 1)
                    part = flat(k.mod[:])[:, j * 512:(j + 1) * 512]
                    dve.tensor_tensor(part, part, k.bank(j % 2), ALU.add).then_inc(mod_done, 1)

                for j in range(4):
                    mod_add(j)
                dve.wait_ge(mod_done, 4)
                dve.wait_ge(gain_in[0], 16)
                dve.scalar_tensor_tensor(k.mod[:, 1, :], k.mod[:, 1, :], 1.0, gain[:, 0, :],
                                         ALU.add, ALU.mult).then_inc(gain_used, 1)
                dve.wait_ge(root_ready, 1)
                chain(dve.reciprocal(rstd[:], rstd[:]))
                dve.wait_ge(gain_used, 1)
                for t in range(NT):
                    if t >= 2:
                        dve.wait_ge(h_turned, 2 * (t - 1))
                    chain(dve.scalar_tensor_tensor(h[:, t % 2, :], k.x[:, t, :], rstd[:, t:t + 1],
                                                   k.mod[:, 1, :], ALU.mult, ALU.mult))
                    dve.tensor_tensor(h[:, t % 2, :], h[:, t % 2, :], k.mod[:, 0, :],
                                      ALU.add).then_inc(h_ready, 1)
                for j in range(4, 12):
                    mod_add(j)
                    if j == 5:
                        dve.wait_ge(gain_in[1], 16)
                        dve.wait_ge(mod_done, 6)
                        dve.tensor_tensor(k.mod[:, 2, :], k.mod[:, 2, :], gain[:, 1, :],
                                          ALU.mult).then_inc(gain_used, 1)
                dve.wait_ge(mod_done, 12)
                dve.wait_ge(gain_in[0], 32)
                dve.scalar_tensor_tensor(k.mod[:, 4, :], k.mod[:, 4, :], 1.0, gain[:, 0, :],
                                         ALU.add, ALU.mult).then_inc(gain_used, 1)
                dve.wait_ge(gain_in[1], 32)
                dve.tensor_tensor(k.gate2[:], k.mod[:, 5, :], gain[:, 1, :], ALU.mult).then_inc(gain_used, 1)


def stage_mixers(k, front):
    k.cat = k.sb("cat", [P, NT, D], at=front)
    k.w_out = k.sb("w_out", [P, KT, D], at=front)
    k.w_out_in = k.sem("w_out_in")
    attention(k)
    linear_attention(k)


def attention(k):
    nc, d = k.nc, k.d
    half = DA // 2
    units = [(i, h) for i in range(NT) for h in range(HA)]
    NU = len(units)
    with ExitStack() as ctx:
        sb = lambda n, s, dt=F32: k.sb(n, s, dt, at=ctx)
        sem = k.stage_semaphores(ctx)
        log_count = sb("log_count", [P, NT, S])
        zeros = sb("zero_rows", [P, D])
        table = sb("rope_table", [P, NT, 2, 2, half])
        turned = sb("turned", [P, 2, 2 * HA, 2, half])
        cross = sb("cross", [P, 2, 2 * HA, half])
        qkT = sb("qkT", [P, 8, S])
        scores = sb("scores", [P, 2, S])
        probs = sb("probs", [P, 2, S])
        probsT = sb("probsT", [P, 2, S])
        negmax = sb("negmax", [P, NU])
        rowsum = sb("rowsum", [P, NU])
        inv = sb("inv", [P, NU])
        const_in = sem("attn_const_in")
        zeros_set = sem("zeros_set")
        zeros_out = sem("zeros_out")
        rope_done = sem("rope_done")
        turn_ps = sem("turn_ps")
        qkT_ready = sem("qkT_ready")
        scores_ps = sem("scores_ps")
        scores_masked = sem("scores_masked")
        probs_ready = sem("probs_ready")
        probsT_ps = sem("probsT_ps")
        probsT_ready = sem("probsT_ready")
        pv_done = sem("pv_done")
        cat_ready = sem("cat_ready")

        with nc.Block() as block:
            @block.sync
            def _(sp):
                sp.dma_start(table[:], d["rope"]).then_inc(const_in, 16)
                sp.dma_start(log_count[:], d["log_count"]).then_inc(const_in, 16)
                sp.wait_ge(zeros_set, 1)
                sp.dma_start(d["expert_rows"].rearrange("(b p) n -> p b n", p=P)[:, NE:, :],
                             zeros[:].unsqueeze(1).broadcast_to([P, EXTRA, D])).then_inc(zeros_out, 16)
                sp.dma_start(k.w_out[:], d["w_out"].rearrange("(k p) n -> p k n", p=P)).then_inc(k.w_out_in, 16)
                sp.wait_ge(zeros_out, 16)

            @block.vector
            def _(dve):
                chain = k.dve_chain.on(dve)
                dve.memset(zeros[:], 0.0).then_inc(zeros_set, 1)

                def finish_tile(dve, chain, i):
                    a, b = i * HA, (i + 1) * HA
                    dve.wait_ge(pv_done, b)
                    chain(dve.reciprocal(inv[:, a:b], rowsum[:, a:b]))
                    dve.tensor_tensor(k.cat[:, i, 0:HA * DA].rearrange("p (h n) -> p h n", h=HA),
                                      k.bank(6 + i % 2).rearrange("p (h n) -> p h n", h=HA),
                                      inv[:, a:b].unsqueeze(2).broadcast_to([P, HA, DA]),
                                      ALU.mult).then_inc(cat_ready, 1)

                dve.wait_ge(const_in, 32)
                for t in range(NT):
                    if t >= 2:
                        dve.wait_ge(turn_ps, 2 * (t - 1))
                    x = k.proj[:, t, 0:2 * HA * DA].rearrange("p (h two n) -> p h two n", two=2, n=half)
                    cs = [table[:, t, :, c, :].unsqueeze(2).broadcast_to([P, 2, HA, half]) for c in range(2)]
                    grouped = lambda ap: ap.rearrange("p (q h) n -> p q h n", q=2)
                    out = turned[:, t % 2]
                    dve.tensor_tensor(grouped(out[:, :, 0, :]), grouped(x[:, :, 0, :]), cs[0], ALU.mult)
                    dve.tensor_tensor(grouped(cross[:, 0]), grouped(x[:, :, 1, :]), cs[1], ALU.mult)
                    dve.tensor_tensor(grouped(out[:, :, 1, :]), grouped(x[:, :, 1, :]), cs[0], ALU.mult)
                    chain(dve.tensor_tensor(grouped(cross[:, 1]), grouped(x[:, :, 0, :]), cs[1], ALU.mult))
                    dve.tensor_tensor(out[:, :, 0, :], out[:, :, 0, :], cross[:, 0], ALU.subtract)
                    chain(dve.tensor_tensor(out[:, :, 1, :], out[:, :, 1, :], cross[:, 1], ALU.add))
                    dve.sem_inc(rope_done, 1)
                for u, (i, h) in enumerate(units):
                    n = (i + 1) * P
                    dve.wait_ge(scores_ps, u + 1)
                    if u >= 2:
                        dve.wait_ge(probs_ready, u - 1)
                    dve.tensor_tensor_reduce(scores[:, u % 2, 0:n], k.bank(2 + u % 2)[:, 0:n],
                                             log_count[:, i, 0:n], -1.0, 1e30, ALU.add, ALU.min,
                                             negmax[:, u:u + 1]).then_inc(scores_masked, 1)
                    if h == 1 and i:
                        finish_tile(dve, chain, i - 1)
                finish_tile(dve, chain, NT - 1)

            @block.scalar
            def _(act):
                for t in range(NT):
                    for part in range(2):
                        act.wait_ge(turn_ps, 2 * t + part + 1)
                        act.activation(qkT[:, 4 * part:4 * part + 4, t * P:(t + 1) * P],
                                       k.bank(part).rearrange("p (a b) -> p a b", b=P),
                                       ACT.Copy).then_inc(qkT_ready, 1)
                for u in range(NU + 1):
                    if u < NU:
                        n = (units[u][0] + 1) * P
                        act.wait_ge(scores_masked, u + 1)
                        if u >= 2:
                            act.wait_ge(probsT_ps, u - 1)
                        act.activation(probs[:, u % 2, 0:n], scores[:, u % 2, 0:n], ACT.Exp, scale=-1.0,
                                       bias=negmax[:, u:u + 1],
                                       accum_out=rowsum[:, u:u + 1]).then_inc(probs_ready, 1)
                    if u >= 1:
                        v = u - 1
                        n = (units[v][0] + 1) * P
                        act.wait_ge(probsT_ps, v + 1)
                        if v >= 2:
                            act.wait_ge(pv_done, v - 1)
                        act.activation(probsT[:, v % 2, 0:n], k.bank(4 + v % 2)[:, 0:n],
                                       ACT.Copy).then_inc(probsT_ready, 1)

            @block.tensor
            def _(pe):
                for t in range(NT):
                    pe.wait_ge(rope_done, t + 1)
                    for part in range(2):
                        if t:
                            pe.wait_ge(qkT_ready, 2 * (t - 1) + part + 1)
                        for q in range(4):
                            c = 4 * part + q
                            src = turned[:, t % 2].rearrange("p h two n -> p (h two n)")[:, c * P:(c + 1) * P]
                            mm = pe.transpose(k.bank(part)[:, q * P:(q + 1) * P], src, k.sq[:, IDENT, :])
                        mm.then_inc(turn_ps, 1)
                pe.wait_ge(qkT_ready, 2 * NT)
                for u in range(NU + 2):
                    if u < NU:
                        i, h = units[u]
                        r = (h % 2) * DA
                        if u >= 2:
                            pe.wait_ge(scores_masked, u - 1)
                        pe.matmul(k.bank(2 + u % 2)[:, 0:(i + 1) * P],
                                  qkT[r:r + DA, h // 2, i * P:(i + 1) * P],
                                  qkT[r:r + DA, 4 + h // 2, 0:(i + 1) * P],
                                  start=True, stop=True).then_inc(scores_ps, 1)
                    if 1 <= u <= NU:
                        v = u - 1
                        i = units[v][0]
                        pe.wait_ge(probs_ready, v + 1)
                        if v >= 2:
                            pe.wait_ge(probsT_ready, v - 1)
                        for j in range(i + 1):
                            mm = pe.transpose(k.bank(4 + v % 2)[:, j * P:(j + 1) * P],
                                              probs[:, v % 2, j * P:(j + 1) * P], k.sq[:, IDENT, :])
                        mm.then_inc(probsT_ps, 1)
                    if u >= 2:
                        v = u - 2
                        i, h = units[v]
                        pe.wait_ge(probsT_ready, v + 1)
                        if h == 0 and i >= 2:
                            pe.wait_ge(cat_ready, i - 1)
                        for j in range(i + 1):
                            mm = pe.matmul(k.bank(6 + i % 2)[:, h * DA:(h + 1) * DA],
                                           probsT[:, v % 2, j * P:(j + 1) * P],
                                           k.proj[:, j, VA + h * DA:VA + (h + 1) * DA],
                                           start=(j == 0), stop=(j == i))
                        mm.then_inc(pv_done, 1)


def linear_attention(k):
    nc, d = k.nc, k.d
    KW, VW = HG * DK, HG * DV
    NCH = S // CH
    with ExitStack() as ctx:
        sb = lambda n, s, dt=F32: k.sb(n, s, dt, at=ctx)
        sem = k.stage_semaphores(ctx)
        lrT = sb("lrT", [32, S])
        w_lr = sb("w_lr", [32, KW])
        g_gla = sb("g_gla", [P, DV])
        la = sb("la", [P, NT, KW])
        tmp = sb("gla_tmp", [P, NT * KW])
        grow = sb("grow", [P, 3, NT * KW])
        qd = sb("qd", [P, NT, KW])
        kd = sb("kd", [P, NT, KW])
        kl = sb("kl", [P, NT, KW])
        qkdT = sb("qkdT", [P, 4, S])
        decay = sb("decay", [P, 2, NCH])
        att = sb("gla_att", [P, 2, HG, P])
        state = sb("gla_state", [P, NCH, 2, DV])
        junk = sb("gla_junk", [P, DV])
        sumsq = sb("gla_sumsq", [P, NT * HG])
        rstd = sb("gla_rstd", [P, NT * HG])
        const_in = sem("gla_const_in")
        lr_set = sem("lr_set")
        lr_ps = sem("lr_ps")
        lr_ready = sem("lr_ready")
        logit_ps = sem("logit_ps")
        abs_ready = sem("abs_ready")
        log_ready = sem("log_ready")
        la_ready = sem("la_ready")
        cum_ps = sem("cum_ps")
        grow_ready = sem("grow_ready")
        qk_ready = sem("qk_ready")
        qkT_ps = sem("qkdT_ps")
        qkT_ready = sem("qkdT_ready")
        att_ps = sem("att_ps")
        att_ready = sem("att_ready")
        u_ps = sem("u_ps")
        state_ready = sem("state_ready")
        o_ps = sem("o_ps")
        o_read = sem("o_read")
        root_ready = sem("gla_root")
        silu_ready = sem("silu_ready")

        with nc.Block() as block:
            @block.sync
            def _(sp):
                sp.dma_start(w_lr[0:RANK + 1, :], d["w_gate_lr"]).then_inc(const_in, 16)
                sp.dma_start(g_gla[:], d["g_gla"][0:1, :].partition_broadcast(P).rearrange(
                    "p a n -> p (a n)")).then_inc(const_in, 16)

            @block.tensor
            def _(pe):
                for t in range(NT):
                    mm = pe.transpose(k.bank(0)[0:RANK, t * P:(t + 1) * P], k.proj[:, t, LR:LR + RANK],
                                      k.sq[:, IDENT, :])
                mm.then_inc(lr_ps, 1)
                pe.wait_ge(lr_ready, 1)
                pe.wait_ge(const_in, 32)
                for t in range(NT):
                    mm = pe.matmul(k.pp[1][:, t * KW:(t + 1) * KW], lrT[0:RANK + 1, t * P:(t + 1) * P],
                                   w_lr[0:RANK + 1, :], start=True, stop=True)
                mm.then_inc(logit_ps, 1)
                pe.wait_ge(la_ready, 1)
                for t in range(NT):
                    mm = pe.matmul(k.pp[0][:, t * KW:(t + 1) * KW], k.sq[:, CUM, :], la[:, t, :],
                                   start=True, stop=True)
                mm.then_inc(cum_ps, 1)
                for t in range(NT):
                    mm = pe.matmul(k.pp[2][:, t * KW:(t + 1) * KW], k.sq[:, SUF, :], la[:, t, :],
                                   start=True, stop=True)
                mm.then_inc(cum_ps, 1)
                for t in range(NT):
                    for p in range(2):
                        c = p * NCH + 2 * t
                        mm = pe.matmul(k.bank(6)[:, c:c + 2], la[:, t, p * P:(p + 1) * P],
                                       k.sq[:, BLOCK, 0:P:CH], start=True, stop=True)
                mm.then_inc(cum_ps, 1)
                for t in range(NT):
                    pe.wait_ge(qk_ready, 1)
                    if t >= 2:
                        pe.wait_ge(qkT_ready, t - 1)
                    for q in range(4):
                        src = (qd, kd)[q // 2][:, t, (q % 2) * P:(q % 2 + 1) * P]
                        mm = pe.transpose(k.bank(2 + t % 2)[:, q * P:(q + 1) * P], src, k.sq[:, IDENT, :])
                    mm.then_inc(qkT_ps, 1)
                for t in range(NT):
                    pe.wait_ge(qkT_ready, t + 1)
                    pe.wait_ge(grow_ready, 4)
                    if t:
                        pe.wait_ge(att_ready, 2 * t)
                    for h in range(HG):
                        r = (h % 2) * DK
                        mm = pe.matmul(k.bank(6 + h % 2)[:, h // 2 * P:(h // 2 + 1) * P],
                                       qkdT[r:r + DK, 2 + h // 2, t * P:(t + 1) * P],
                                       qkdT[r:r + DK, h // 2, t * P:(t + 1) * P], start=True, stop=True)
                    mm.then_inc(att_ps, 1)
                    if t:
                        pe.wait_ge(state_ready, 2 * t)
                    for c in range(2):
                        for h in range(HG):
                            r = c * CH
                            o = (h % 2) * DK
                            col = h // 2 * DV
                            mm = pe.matmul(k.bank(4 + c)[o:o + DK, col:col + DV],
                                           kl[r:r + CH, t, h * DK:(h + 1) * DK],
                                           k.proj[r:r + CH, t, VG + h * DV:VG + (h + 1) * DV],
                                           start=True, stop=True)
                    mm.then_inc(u_ps, 1)
                    pe.wait_ge(att_ready, 2 * (t + 1))
                    pe.wait_ge(state_ready, 2 * t + 1)
                    if t:
                        pe.wait_ge(o_read, t)
                    for h in range(HG):
                        out = k.bank(h % 2)[:, h // 2 * DV:(h // 2 + 1) * DV]
                        pe.matmul(out, att[:, t % 2, h, :],
                                  k.proj[:, t, VG + h * DV:VG + (h + 1) * DV], start=True, stop=True)
                        for c in range(2):
                            r = (h % 2) * DK
                            mm = pe.matmul(out[c * CH:(c + 1) * CH, :],
                                           qkdT[r:r + DK, h // 2, t * P + c * CH:t * P + (c + 1) * CH],
                                           state[r:r + DK, 2 * t + c, h // 2, :], start=False,
                                           stop=True, skip_group_check=True)
                    mm.then_inc(o_ps, 1)

            @block.scalar
            def _(act):
                chain = k.act_chain.on(act)
                act.wait_ge(lr_ps, 1)
                act.wait_ge(lr_set, 1)
                act.activation(lrT[0:RANK, :], k.bank(0)[0:RANK, :], ACT.Copy).then_inc(lr_ready, 1)
                act.wait_ge(abs_ready, 1)
                chain(act.activation(tmp[:], tmp[:], ACT.Exp))
                act.activation(tmp[:], tmp[:], ACT.Ln, bias=1.0).then_inc(log_ready, 1)
                act.wait_ge(cum_ps, 1)
                act.activation(grow[:, 0, :], k.pp[0][:, :], ACT.Exp).then_inc(grow_ready, 1)
                act.activation(grow[:, 1, :], k.pp[0][:, :], ACT.Exp, scale=-1.0).then_inc(grow_ready, 1)
                act.wait_ge(cum_ps, 2)
                act.activation(grow[:, 2, :], k.pp[2][:, :], ACT.Exp).then_inc(grow_ready, 1)
                act.wait_ge(cum_ps, 3)
                act.activation(decay[:], k.bank(6)[:, 0:2 * NCH].rearrange("p (a c) -> p a c", a=2), ACT.Exp,
                               scale=1.0 / 16).then_inc(grow_ready, 1)
                for t in range(NT):
                    act.wait_ge(qkT_ps, t + 1)
                    act.activation(qkdT[:, :, t * P:(t + 1) * P],
                                   k.bank(2 + t % 2).rearrange("p (a b) -> p a b", b=P),
                                   ACT.Copy).then_inc(qkT_ready, 1)
                for t in range(NT):
                    act.wait_ge(o_ps, t + 1)
                    for h in range(HG):
                        chain(act.activation(junk[:], k.bank(h % 2)[:, h // 2 * DV:(h // 2 + 1) * DV],
                                             ACT.Square, accum_out=sumsq[:, t * HG + h:t * HG + h + 1]))
                    for b in range(2):
                        ins = act.activation(
                            k.cat[:, t, VW:2 * VW].rearrange("p (h n) -> p h n", h=HG)[:, b::2, :],
                            k.bank(b)[:, 0:2 * DV].rearrange("p (h n) -> p h n", n=DV), ACT.Copy)
                    chain(ins)
                    act.sem_inc(o_read, 1)
                act.activation(rstd[:], sumsq[:], ACT.Sqrt, scale=1.0 / DV,
                               bias=k.eps[:, 0:1]).then_inc(root_ready, 1)
                for t in range(NT):
                    act.activation(k.proj[:, t, RG:RG + VW], k.proj[:, t, RG:RG + VW],
                                   ACT.Silu).then_inc(silu_ready, 1)

            @block.vector
            def _(dve):
                chain = k.dve_chain.on(dve)
                dve.memset(lrT[:], 1.0).then_inc(lr_set, 1)
                dve.memset(state[:, 0], 0.0)
                chain(dve.memset(att[:], 0.0))
                dve.wait_ge(logit_ps, 1)
                chain(dve.tensor_scalar(tmp[:], k.pp[1][:, :], -1.0, None, ALU.mult))
                dve.tensor_tensor(tmp[:], tmp[:], k.pp[1][:, :], ALU.min).then_inc(abs_ready, 1)
                dve.wait_ge(log_ready, 1)
                dve.scalar_tensor_tensor(flat(la[:]), k.pp[1][:, :], 0.0, tmp[:], ALU.min,
                                         ALU.subtract).then_inc(la_ready, 1)
                part = lambda n: grow[:, n, :].rearrange("p (t n) -> p t n", t=NT)
                dve.wait_ge(grow_ready, 1)
                dve.scalar_tensor_tensor(qd[:], k.proj[:, :, QG:QG + KW], DK ** -0.5, part(0),
                                         ALU.mult, ALU.mult)
                dve.wait_ge(grow_ready, 2)
                chain(dve.tensor_tensor(kd[:], k.proj[:, :, KG:KG + KW], part(1), ALU.mult))
                dve.wait_ge(grow_ready, 3)
                dve.tensor_tensor(kl[:], k.proj[:, :, KG:KG + KW], part(2), ALU.mult).then_inc(qk_ready, 1)
                mask = k.sq[:, LE, :].bitcast(U32).unsqueeze(1).broadcast_to([P, HG // 2, P])
                dve.wait_ge(grow_ready, 4)
                for t in range(NT):
                    dve.wait_ge(att_ps, t + 1)
                    if t >= 2:
                        dve.wait_ge(o_ps, t - 1)
                    for b in range(2):
                        dve.copy_predicated(att[:, t % 2, b::2, :], mask,
                                            k.bank(6 + b)[:, 0:2 * P].rearrange("p (a b) -> p a b", b=P)
                                            ).then_inc(att_ready, 1)
                    dve.wait_ge(u_ps, t + 1)
                    for c in range(2):
                        n = 2 * t + c
                        if n + 1 < NCH:
                            for p in range(2):
                                ins = dve.scalar_tensor_tensor(
                                    state[:, n + 1, p, :], state[:, n, p, :], decay[:, p, n:n + 1],
                                    k.bank(4 + c)[:, p * DV:(p + 1) * DV],
                                    ALU.mult, ALU.add)
                            chain(ins)
                            dve.sem_inc(state_ready, 1)
                dve.wait_ge(root_ready, 1)
                chain(dve.reciprocal(rstd[:], rstd[:]))
                for t in range(NT):
                    o = k.cat[:, t, VW:2 * VW].rearrange("p (h n) -> p h n", h=HG)
                    scale = rstd[:, t * HG:(t + 1) * HG].unsqueeze(2).broadcast_to([P, HG, DV])
                    gain = g_gla[:].unsqueeze(1).broadcast_to([P, HG, DV])
                    chain(dve.tensor_tensor(o, o, scale, ALU.mult))
                    chain(dve.tensor_tensor(o, o, gain, ALU.mult))
                    dve.wait_ge(silu_ready, t + 1)
                    chain(dve.tensor_tensor(k.cat[:, t, VW:2 * VW], k.cat[:, t, VW:2 * VW],
                                            k.proj[:, t, RG:RG + VW], ALU.mult))


def row(ap):
    return ap.partition_broadcast(P).rearrange("p a n -> p (a n)")


def stage_router(k, front):
    nc, d = k.nc, k.d
    with ExitStack() as ctx:
        sb = lambda n, s, dt=F32: k.sb(n, s, dt, at=ctx)
        sem = k.stage_semaphores(ctx)
        turned = sb("catT", [P, KT, S])
        h2 = sb("h2", [P, NT, D])
        scaled = sb("scaled", [P, D])
        junk = sb("router_junk", [P, D])
        sumsq = sb("router_sumsq", [P, 2, NT])
        rstd = sb("router_rstd", [P, 2, NT])
        w_router = sb("w_router", [P, KT, NE])
        b_router = sb("b_router", [P, NE])
        route = sb("route_const", [P, 5, NE])
        token = sb("token", [P, NT], I32)
        none = sb("none", [P, NBLK + 1], I32)
        logits = sb("logits", [P, NT, NE])
        top = sb("top", [P, NT, 8])
        index = sb("index", [P, NT, 8], U32)
        indexf = sb("indexf", [P, NT, 8])
        onehot = sb("onehot", [P, NT, TOPK, NE])
        work = sb("route_work", [P, NT, TOPK, NE])
        chosen = sb("chosen", [P, NT, NE])
        gate_e = sb("gate_e", [P, NT, NE])
        gsum = sb("gsum", [P, NT])
        rank = sb("rank", [P, NT, NE])
        over = sb("over", [P, NT, NE])
        cnt = sb("cnt", [P, 6, NE])
        cmp = sb("cmp", [P, NE, NE])
        destf = sb("destf", [P, NT, TOPK])
        ends = sb("ends", [P, 2 * NE + 1])
        const_in = sem("router_const_in")
        cat_ps = sem("cat_ps")
        catT_ready = sem("catT_ready")
        y_ps = sem("y_ps")
        y_sumsq = sem("y_sumsq")
        x_ready = sem("resid_ready")
        x_sumsq = sem("x_sumsq")
        y_read = sem("y_read")
        h2_ready = sem("h2_ready")
        h2_out = sem("h2_out")
        h2_ps = sem("h2_ps")
        h2T_ready = sem("h2T_ready")
        logits_ps = sem("logits_ps")
        gate_diff = sem("gate_diff")
        gate_exp = sem("gate_exp")
        chosen_ready = sem("chosen_ready")
        rank_ps = sem("rank_ps")
        gateT_ps = sem("gateT_ps")
        none_set = sem("none_set")
        none_out = sem("none_out")
        dest_ready = sem("dest_ready")
        table_ready = sem("table_ready")
        lists_out = sem("lists_out")
        gateT_ready = sem("gateT_ready")

        with nc.Block() as block:
            @block.sync
            def _(sp):
                sp.dma_start(w_router[:], d["router_w"].rearrange("(k p) n -> p k n", p=P)).then_inc(const_in, 16)
                sp.dma_start(b_router[:], row(d["router_b"][0:1, :])).then_inc(const_in, 16)
                sp.dma_start(route[:], d["route"]).then_inc(const_in, 16)
                sp.dma_start(token[:], d["token"]).then_inc(const_in, 16)
                sp.wait_ge(none_set, 1)
                sp.dma_start(d["slot_token"].rearrange("(p n) one -> p (n one)", p=P),
                             none[:]).then_inc(none_out, 16)
                for t in range(NT):
                    sp.wait_ge(h2_ready, t + 1)
                    sp.dma_start(d["h2"][t * P:(t + 1) * P, :], h2[:, t, :]).then_inc(h2_out, 16)
                sp.wait_ge(h2_out, 16 * NT)

            @block.gpsimd
            def _(pool):
                pool.memset(none[:], 0).then_inc(none_set, 1)
                pool.wait_ge(none_out, 16)
                pool.wait_ge(const_in, 64)
                pool.wait_ge(dest_ready, 1)
                for t in range(NT):
                    for c in range(TOPK):
                        pool.indirect_dma_start(
                            out=d["slot_token"],
                            out_offset=bass.IndirectOffsetOnAxis(ap=k.dest[:, t, c:c + 1], axis=0),
                            in_=token[:, t:t + 1], in_offset=None).then_inc(lists_out, 16)
                pool.wait_ge(lists_out, 16 * NT * TOPK)

            @block.tensor
            def _(pe):
                ident = k.sq[:, IDENT, :]

                def turn_and_project(t):
                    if t:
                        pe.wait_ge(catT_ready, 2 * t)
                    for q in range(KT):
                        mm = pe.transpose(k.bank(q // 4)[:, (q % 4) * P:(q % 4 + 1) * P],
                                          k.cat[:, t, q * P:(q + 1) * P], ident)
                        if q % 4 == 3:
                            mm.then_inc(cat_ps, 1)
                    pe.wait_ge(catT_ready, 2 * (t + 1))
                    if t >= 2:
                        pe.wait_ge(y_read, t - 1)
                    for n in range(2):
                        for q in range(KT):
                            mm = pe.matmul(k.pp[1 + t % 2][:, n * 512:(n + 1) * 512],
                                           turned[:, q, t * P:(t + 1) * P],
                                           k.w_out[:, q, n * 512:(n + 1) * 512],
                                           start=(q == 0), stop=(q == KT - 1))
                    mm.then_inc(y_ps, 1)

                def turn_h2(t):
                    pe.wait_ge(h2_ready, t + 1)
                    if t:
                        pe.wait_ge(h2T_ready, 2 * t)
                    for q in range(KT):
                        mm = pe.transpose(k.bank(6 + q // 4)[:, (q % 4) * P:(q % 4 + 1) * P],
                                          h2[:, t, q * P:(q + 1) * P], ident)
                        if q % 4 == 3:
                            mm.then_inc(h2_ps, 1)

                pe.wait_ge(k.w_out_in, 16)
                turn_and_project(0)
                for t in range(1, NT):
                    turn_and_project(t)
                    turn_h2(t - 1)
                turn_h2(NT - 1)
                pe.wait_ge(h2T_ready, 2 * NT)
                pe.wait_ge(const_in, 64)
                for t in range(NT):
                    for q in range(KT):
                        mm = pe.matmul(k.bank(0)[:, t * NE:(t + 1) * NE], turned[:, q, t * P:(t + 1) * P],
                                       w_router[:, q, :], start=(q == 0), stop=(q == KT - 1))
                mm.then_inc(logits_ps, 1)
                pe.wait_ge(chosen_ready, 1)
                for t in range(NT):
                    for s in range(t + 1):
                        pe.matmul(k.bank(1)[:, t * NE:(t + 1) * NE],
                                  k.sq[:, BEFORE if s == t else ONES, :], chosen[:, s, :],
                                  start=(s == 0), stop=(s == t))
                for s in range(NT):
                    mm = pe.matmul(k.bank(1)[:, NT * NE:(NT + 1) * NE], k.sq[:, ONES, :], chosen[:, s, :],
                                   start=(s == 0), stop=(s == NT - 1))
                mm.then_inc(rank_ps, 1)
                pe.wait_ge(gateT_ready, 1)
                for t in range(NT):
                    mm = pe.transpose(k.bank(2)[0:NE, t * P:(t + 1) * P], gate_e[:, t, :], ident)
                mm.then_inc(gateT_ps, 1)

            @block.scalar
            def _(act):
                def root(part, t):
                    chain(act.activation(rstd[:, part, t:t + 1], sumsq[:, part, t:t + 1], ACT.Sqrt,
                                         scale=1.0 / D, bias=k.eps[:, 0:1]))

                def evac(bank0, ps, ready, t):
                    for part in range(2):
                        act.wait_ge(ps, 2 * t + part + 1)
                        act.activation(turned[:, 4 * part:4 * part + 4, t * P:(t + 1) * P],
                                       k.bank(bank0 + part).rearrange("p (a b) -> p a b", b=P),
                                       ACT.Copy).then_inc(ready, 1)

                chain = k.act_chain.on(act)
                for t in range(NT + 1):
                    if t < NT:
                        evac(0, cat_ps, catT_ready, t)
                    if t < NT:
                        act.wait_ge(y_ps, t + 1)
                        chain(act.activation(junk[:], k.pp[1 + t % 2][:, :], ACT.Square,
                                             accum_out=sumsq[:, 0, t:t + 1]))
                        root(0, t)
                        act.sem_inc(y_sumsq, 1)
                        act.wait_ge(x_ready, t + 1)
                        chain(act.activation(junk[:], k.x[:, t, :], ACT.Square,
                                             accum_out=sumsq[:, 1, t:t + 1]))
                        root(1, t)
                        act.sem_inc(x_sumsq, 1)
                    if t:
                        evac(6, h2_ps, h2T_ready, t - 1)
                act.wait_ge(gate_diff, 1)
                act.activation(k.gates[:], k.gates[:], ACT.Exp).then_inc(gate_exp, 1)
                act.wait_ge(gateT_ps, 1)
                act.activation(k.gateT[:], k.bank(2)[0:NE, :], ACT.Copy)

            @block.vector
            def _(dve):
                chain = k.dve_chain.on(dve)
                for t in range(NT):
                    dve.wait_ge(y_sumsq, t + 1)
                    chain(dve.reciprocal(rstd[:, 0, t:t + 1], rstd[:, 0, t:t + 1]))
                    chain(dve.scalar_tensor_tensor(scaled[:], k.pp[1 + t % 2][:, :], rstd[:, 0, t:t + 1],
                                                   k.mod[:, 2, :], ALU.mult, ALU.mult))
                    dve.sem_inc(y_read, 1)
                    dve.tensor_tensor(k.x[:, t, :], k.x[:, t, :], scaled[:], ALU.add).then_inc(x_ready, 1)
                    dve.wait_ge(x_sumsq, t + 1)
                    chain(dve.reciprocal(rstd[:, 1, t:t + 1], rstd[:, 1, t:t + 1]))
                    chain(dve.scalar_tensor_tensor(h2[:, t, :], k.x[:, t, :], rstd[:, 1, t:t + 1],
                                                   k.mod[:, 4, :], ALU.mult, ALU.mult))
                    dve.tensor_tensor(h2[:, t, :], h2[:, t, :], k.mod[:, 3, :], ALU.add).then_inc(h2_ready, 1)
                dve.wait_ge(const_in, 64)
                dve.wait_ge(logits_ps, 1)
                over_t = lambda ap, n=NT: ap.unsqueeze(1).broadcast_to([P, n, NE])
                chain(dve.tensor_tensor(logits[:], k.bank(0)[:, 0:NT * NE].rearrange("p (t e) -> p t e", e=NE),
                                        over_t(b_router[:]), ALU.add))
                for t in range(NT):
                    ins = dve.max(top[:, t, :], logits[:, t, :])
                chain(ins)
                for t in range(NT):
                    ins = dve.max_index(index[:, t, :], top[:, t, :], logits[:, t, :])
                chain(ins)
                chain(dve.tensor_copy(indexf[:], index[:]))
                for t in range(NT):
                    ins = dve.tensor_tensor(onehot[:, t], over_t(route[:, 0, :], TOPK),
                                            indexf[:, t, 0:TOPK].unsqueeze(2).broadcast_to([P, TOPK, NE]),
                                            ALU.is_equal)
                dve.tensor_tensor(k.gates[:], top[:, :, 0:TOPK], top[:, :, 0:1].broadcast_to([P, NT, TOPK]),
                                  ALU.subtract).then_inc(gate_diff, 1)
                chain(dve.memset(over[:], 1.0))
                for t in range(NT):
                    ins = dve.tensor_reduce(chosen[:, t, :], onehot[:, t].rearrange("p c e -> p e c"), AX.X,
                                            ALU.add)
                ins.then_inc(chosen_ready, 1)
                dve.wait_ge(gate_exp, 1)
                chain(dve.tensor_reduce(gsum[:], k.gates[:], AX.X, ALU.add))
                chain(dve.reciprocal(gsum[:], gsum[:]))
                chain(dve.tensor_tensor(k.gates[:], k.gates[:],
                                        gsum[:].unsqueeze(2).broadcast_to([P, NT, TOPK]), ALU.mult))
                for t in range(NT):
                    ins = dve.tensor_tensor(work[:, t], onehot[:, t],
                                            k.gates[:, t, :].unsqueeze(2).broadcast_to([P, TOPK, NE]), ALU.mult)
                chain(ins)
                for t in range(NT):
                    ins = dve.tensor_reduce(gate_e[:, t, :], work[:, t].rearrange("p c e -> p e c"), AX.X,
                                            ALU.add)
                ins.then_inc(gateT_ready, 1)
                dve.wait_ge(rank_ps, 1)
                dve.tensor_copy(rank[:], k.bank(1)[:, 0:NT * NE].rearrange("p (t e) -> p t e", e=NE))
                chain(dve.tensor_copy(cnt[:, 0, :], k.bank(1)[:, NT * NE:(NT + 1) * NE]))
                chain(dve.tensor_scalar(cnt[:, 1, :], cnt[:, 0, :], float(SLOTS), None, ALU.is_gt))
                for j in range(2, -(-S // SLOTS)):
                    chain(dve.scalar_tensor_tensor(cnt[:, 1, :], cnt[:, 0, :], float(SLOTS * j), cnt[:, 1, :],
                                                   ALU.is_gt, ALU.add))
                chain(dve.tensor_tensor_scan(cnt[:, 2, :], over[:, 0, :], cnt[:, 1, :], 0.0, ALU.mult, ALU.add))
                chain(dve.tensor_tensor(cnt[:, 3, :], cnt[:, 2, :], cnt[:, 1, :], ALU.subtract))
                chain(dve.tensor_scalar(cnt[:, 4, :], cnt[:, 3, :], float(SLOTS), float((NE - 1) * SLOTS),
                                        ALU.mult, ALU.add))
                chain(dve.tensor_tensor(cnt[:, 4, :], cnt[:, 4, :], route[:, 1, :], ALU.subtract))
                chain(dve.tensor_scalar(over[:], rank[:], float(SLOTS), None, ALU.is_ge))
                chain(dve.tensor_tensor(over[:], over[:], over_t(cnt[:, 4, :]), ALU.mult))
                chain(dve.tensor_tensor(rank[:], rank[:], over_t(route[:, 1, :]), ALU.add))
                chain(dve.tensor_tensor(rank[:], rank[:], over[:], ALU.add))
                for t in range(NT):
                    ins = dve.tensor_tensor(work[:, t], onehot[:, t], over_t(rank[:, t, :], TOPK), ALU.mult)
                chain(ins)
                for t in range(NT):
                    ins = dve.tensor_reduce(destf[:, t, :], work[:, t], AX.X, ALU.add)
                chain(ins)
                dve.tensor_copy(k.dest[:], destf[:]).then_inc(dest_ready, 1)
                chain(dve.tensor_tensor(cmp[:], cnt[:, 2, :].unsqueeze(1).broadcast_to([P, NE, NE]),
                                        route[:, 2, :].unsqueeze(2).broadcast_to([P, NE, NE]), ALU.is_le))
                chain(dve.tensor_reduce(ends[:, NE:2 * NE], cmp[:], AX.X, ALU.add))
                dve.tensor_scalar(ends[:, NE:2 * NE], ends[:, NE:2 * NE], float(NE - 1), None, ALU.min)
                dve.tensor_copy(ends[:, 0:NE], route[:, 0, :])
                chain(dve.tensor_scalar(ends[:, 2 * NE:2 * NE + 1], cnt[:, 2, NE - 1:NE], float(NE), None, ALU.add))
                chain(dve.tensor_copy(k.table[:], ends[0:1, :]))


def stage_experts(k):
    nc, d = k.nc, k.d
    with ExitStack() as ctx:
        sb = lambda n, s, dt=F32: k.sb(n, s, dt, at=ctx)
        sem = k.stage_semaphores(ctx)
        wgu = sb("wgu", [P, NM, KT * 2 * P])
        wd = sb("wd", [P, NM, D])
        bias_new = sb("bias_new", [P, 2 * NM])
        bias = sb("bias", [P, 2 * NM])
        lin_one = sb("lin_one", [P, 2 * NM])
        slot = sb("slot", [P, 1], I32)
        rows = sb("rows", [P, D])
        rowsT = sb("rowsT", [P, KT, P])
        glu = sb("glu", [P, 2, P])
        lin = sb("lin", [P, 2, P])
        prod = sb("prod", [P, 2, P])
        sig = sb("sig", [P, 2, P])
        hidden = sb("hidden", [P, NM, P])
        y = sb("y_rows", [P, D])
        slab_in = [sem(f"slab_in{m}") for m in range(NM)]
        bias_in = sem("bias_in")
        bias_taken = sem("bias_taken")
        lin_one_set = sem("lin_one_set")
        slot_in = sem("slot_in")
        slot_seen = sem("slot_seen")
        rows_in = sem("rows_in")
        rows_ps = sem("rows_ps")
        rowsT_ready = sem("rowsT_ready")
        pair_ps = sem("pair_ps")
        pair_read = sem("pair_read")
        glu_ready = sem("glu_ready")
        sig_ready = sem("sig_ready")
        prod_ready = sem("prod_ready")
        hidden_ready = sem("hidden_ready")
        slab_used = sem("slab_used")
        y_ps = sem("expert_y_ps")
        y_read = sem("expert_y_read")
        y_out = sem("expert_y_out")
        NBANK = 4

        with nc.Block() as block:
            @block.sync
            def _(sp):
                def load(i, e, first):
                    if not first:
                        sp.wait_ge(bias_taken, i)
                    sp.dma_start(bias_new[:], d["b_gate_up"].rearrange("(e p) n -> e p n", p=P)[
                        bass.ds(e, 1), :, :].rearrange("e p n -> p (e n)")).then_inc(bias_in, 16)
                    for m in range(NM):
                        if not first:
                            sp.wait_ge(slab_used, (i - 1) * NM + m + 1)
                        r = (e * NM + m) * P
                        sp.dma_start(wgu[:, m, :], d["w_gate_up"][bass.ds(r, P), :]).then_inc(slab_in[m], 16)
                        sp.dma_start(wd[:, m, :], d["w_down"][bass.ds(r, P), :]).then_inc(slab_in[m], 16)

                blocks = sp.value_load(k.table[0:1, 2 * NE:2 * NE + 1], min_val=NE, max_val=NBLK)
                load(0, 0, True)
                with sp.Fori(1, blocks) as i:
                    e = sp.value_load(k.table[0:1, bass.ds(i, 1)], min_val=0, max_val=NE - 1)
                    load(i, e, False)

            @block.gpsimd
            def _(pool):
                blocks = pool.value_load(k.table[0:1, 2 * NE:2 * NE + 1], min_val=NE, max_val=NBLK)
                pool.memset(lin_one[:], 0.0).then_inc(lin_one_set, 1)
                pool.wait_ge(lin_one_set, 1)
                pool.memset(lin_one[:, 1::2], 1.0).then_inc(lin_one_set, 1)

                def fetch(i, first):
                    pool.dma_start(slot[:], d["slot_token"][bass.ds(i * SLOTS, SLOTS), :]).then_inc(slot_in, 16)
                    if not first:
                        pool.wait_ge(rows_ps, 2 * i)
                    pool.wait_ge(slot_in, 16 * i + 16)
                    pool.sem_inc(slot_seen, 1)
                    pool.indirect_dma_start(
                        out=rows[:], out_offset=None, in_=d["h2"],
                        in_offset=bass.IndirectOffsetOnAxis(ap=slot[:, 0:1], axis=0)).then_inc(rows_in, 16)

                fetch(0, True)
                with pool.Fori(1, blocks + 1) as i:
                    pool.wait_ge(rows_in, 16 * i)
                    fetch(i, False)
                pool.wait_ge(rows_in, 16 * blocks + 16)
                pool.wait_ge(y_out, 16 * blocks + 16)

            @block.tensor
            def _(pe):
                ident = k.sq[:, IDENT, :]
                blocks = pe.value_load(k.table[0:1, 2 * NE:2 * NE + 1], min_val=NE, max_val=NBLK)

                def turn(i):
                    pe.wait_ge(rows_in, 16 * i + 16)
                    for q in range(KT):
                        mm = pe.transpose(k.bank(6 + q // 4)[:, (q % 4) * P:(q % 4 + 1) * P],
                                          rows[:, q * P:(q + 1) * P], ident)
                        if q % 4 == 3:
                            mm.then_inc(rows_ps, 1)

                def up(i, m):
                    pe.wait_ge(slab_in[m], 32 * i + 32)
                    pe.wait_ge(pair_read, NM * i + m + 1)
                    for part in range(2):
                        for q in range(KT):
                            c = (q * 2 + part) * P
                            mm = pe.matmul(k.bank(m % NBANK)[:, part * P:(part + 1) * P],
                                           wgu[:, m, c:c + P], rowsT[:, q, :],
                                           start=(q == 0), stop=(q == KT - 1))
                    mm.then_inc(pair_ps, 1)

                def down(i, m):
                    pe.wait_ge(hidden_ready, NM * i + m + 3)
                    if m == 0:
                        pe.wait_ge(y_read, i + 1)
                    for n in range(2):
                        mm = pe.matmul(k.bank(4 + n), hidden[:, m, :], wd[:, m, n * 512:(n + 1) * 512],
                                       start=(m == 0), stop=(m == NM - 1))
                    mm.then_inc(slab_used, 1)

                turn(0)
                with pe.Fori(0, blocks) as i:
                    pe.wait_ge(rowsT_ready, 2 * i + 2)
                    for m in range(NM):
                        up(i, m)
                        if m:
                            down(i, m - 1)
                    turn(i + 1)
                    down(i, NM - 1)

            @block.scalar
            def _(act):
                blocks = act.value_load(k.table[0:1, 2 * NE:2 * NE + 1], min_val=NE, max_val=NBLK)

                def evac(i):
                    for part in range(2):
                        act.wait_ge(rows_ps, 2 * i + part + 1)
                        act.activation(rowsT[:, 4 * part:4 * part + 4, :],
                                       k.bank(6 + part).rearrange("p (a b) -> p a b", b=P),
                                       ACT.Copy).then_inc(rowsT_ready, 1)

                act.sem_inc(y_read, 1)
                act.sem_inc(y_out, 16)
                evac(0)
                with act.Fori(0, blocks) as i:
                    for m in range(NM):
                        act.wait_ge(glu_ready, NM * i + m + 1)
                        act.wait_ge(hidden_ready, NM * i + m + 1)
                        act.activation(sig[:, m % 2, :], glu[:, m % 2, :], ACT.Sigmoid,
                                       scale=ALPHA).then_inc(sig_ready, 1)
                    act.wait_ge(pair_ps, NM * i + NM)
                    evac(i + 1)
                    act.wait_ge(slab_used, NM * i + NM)
                    act.wait_ge(y_out, 16 * i + 16)
                    act.activation(y[:], k.pp[2][:, :], ACT.Copy).then_inc(y_read, 1)
                    act.wait_ge(y_read, i + 2)
                    act.dma_start(d["expert_rows"][bass.ds(i * SLOTS, SLOTS), :], y[:]).then_inc(y_out, 16)

            @block.vector
            def _(dve):
                blocks = dve.value_load(k.table[0:1, 2 * NE:2 * NE + 1], min_val=NE, max_val=NBLK)
                dve.sem_inc(pair_read, NBANK)
                dve.sem_inc(hidden_ready, 2)
                dve.wait_ge(lin_one_set, 2)
                with dve.Fori(0, blocks) as i:
                    dve.wait_ge(bias_in, 16 * i + 16)
                    dve.tensor_tensor(bias[:], bias_new[:], lin_one[:], ALU.add).then_inc(bias_taken, 1)
                    dve.wait_ge(bias_taken, i + 1)
                    for m in range(NM):
                        dve.wait_ge(pair_ps, NM * i + m + 1)
                        dve.tensor_scalar(glu[:, m % 2, :], k.bank(m % NBANK)[:, 0:P],
                                          bias[:, 2 * m:2 * m + 1], LIMIT, ALU.add, ALU.min).then_inc(glu_ready, 1)
                        dve.tensor_scalar(lin[:, m % 2, :], k.bank(m % NBANK)[:, P:2 * P],
                                          bias[:, 2 * m + 1:2 * m + 2], LIMIT + 1.0,
                                          ALU.add, ALU.min).then_inc(pair_read, 1)
                        dve.wait_ge(glu_ready, NM * i + m + 1)
                        dve.wait_ge(pair_read, NM * i + m + 1 + NBANK)
                        dve.scalar_tensor_tensor(prod[:, m % 2, :], lin[:, m % 2, :], 1.0 - LIMIT,
                                                 glu[:, m % 2, :], ALU.max, ALU.mult).then_inc(prod_ready, 1)
                        dve.wait_ge(prod_ready, NM * i + m + 1)
                        dve.wait_ge(sig_ready, NM * i + m + 1)
                        dve.tensor_tensor(hidden[:, m, :], prod[:, m % 2, :], sig[:, m % 2, :],
                                          ALU.mult).then_inc(hidden_ready, 1)


def stage_combine(k):
    nc, d = k.nc, k.d
    with ExitStack() as ctx:
        sb = lambda n, s, dt=F32: k.sb(n, s, dt, at=ctx)
        sem = k.stage_semaphores(ctx)
        choice = sb("choice", [P, NT, TOPK, D])
        b_down = sb("b_down", [NE, D])
        acc = sb("acc", [P, 2, D])
        junk = sb("combine_junk", [P, D])
        sumsq = sb("combine_sumsq", [P, NT])
        rstd = sb("combine_rstd", [P, NT])
        b_in = sem("b_down_in")
        choice_in = [sem(f"choice_in{t}") for t in range(NT)]
        bias_ps = sem("bias_ps")
        bias_read = sem("bias_read")
        acc_ready = sem("acc_ready")
        acc_sumsq = sem("acc_sumsq")

        with nc.Block() as block:
            @block.sync
            def _(sp):
                sp.dma_start(b_down[:], d["b_down"]).then_inc(b_in, 16)

            @block.gpsimd
            def _(pool):
                for t in range(NT):
                    for c in range(TOPK):
                        pool.indirect_dma_start(
                            out=choice[:, t, c, :], out_offset=None, in_=d["expert_rows"],
                            in_offset=bass.IndirectOffsetOnAxis(ap=k.dest[:, t, c:c + 1], axis=0)
                        ).then_inc(choice_in[t], 16)

            @block.tensor
            def _(pe):
                pe.wait_ge(b_in, 16)
                for t in range(NT):
                    for n in range(2):
                        mm = pe.matmul(k.pp[t][:, n * 512:(n + 1) * 512], k.gateT[:, t * P:(t + 1) * P],
                                       b_down[:, n * 512:(n + 1) * 512], start=True, stop=True)
                    mm.then_inc(bias_ps, 1)

            @block.scalar
            def _(act):
                chain = k.act_chain.on(act)
                for t in range(NT):
                    act.wait_ge(acc_ready, t + 1)
                    chain(act.activation(junk[:], acc[:, t % 2, :], ACT.Square, accum_out=sumsq[:, t:t + 1]))
                    act.activation(rstd[:, t:t + 1], sumsq[:, t:t + 1], ACT.Sqrt, scale=1.0 / D,
                                   bias=k.eps[:, 0:1]).then_inc(acc_sumsq, 1)

            @block.vector
            def _(dve):
                chain = k.dve_chain.on(dve)
                for t in range(NT):
                    a = acc[:, t % 2, :]
                    dve.wait_ge(bias_ps, t + 1)
                    dve.wait_ge(choice_in[t], 16 * TOPK)
                    for c in range(TOPK):
                        ins = dve.scalar_tensor_tensor(a, choice[:, t, c, :], k.gates[:, t, c:c + 1],
                                                       a if c else k.pp[t][:, :], ALU.mult, ALU.add)
                        if c < TOPK - 1:
                            chain(ins)
                    ins.then_inc(acc_ready, 1)
                    dve.wait_ge(acc_sumsq, t + 1)
                    chain(dve.reciprocal(rstd[:, t:t + 1], rstd[:, t:t + 1]))
                    chain(dve.scalar_tensor_tensor(a, a, rstd[:, t:t + 1], k.gate2[:], ALU.mult, ALU.mult))
                    chain(dve.tensor_tensor(k.x[:, t, :], k.x[:, t, :], a, ALU.add))


U_A, G_A, R_F, K_F, V_F, LR_F, G_B = 0, 4, 8, 12, 16, 20, 21
HR = 8
NCH = S // CH
CHUNKS2 = ((20, 3), (23, 2), (12, 3), (15, 3), (18, 2), (8, 3), (11, 1), (0, 3), (3, 3), (6, 2))


def place(h):
    return (h % 2) * (HR // 2) + h // 2


def stage_second(k, scope):
    nc, d = k.nc, k.d
    k.cols = k.sb("cols", [P, NCOL])
    k.silu_b = k.sb("silu_b", [P, 4, S])
    k.y_pool = k.sb("y_pool", [P, 4, S])
    k.alpha = k.sb("alpha", [P, 4, S])
    k.beta = k.sb("beta", [P, 4, S])
    k.kappa = k.sb("kappa", [P, 4, S])
    k.rho = k.sb("rho", [P, 4, S])
    k.bonus = k.sb("bonus", [P, 4, S])
    k.last = k.sb("last_decay", [P, 4, NCH])
    k.v_tok = k.sb("v_tok", [P, NT, 4 * P])
    k.z2 = k.sb("z2", [P, 21, S + 1], at=scope)
    z2 = k.z2
    tiles = [f for a, n in CHUNKS2 for f in range(a, a + n)]
    arrival = {f: n for n, f in enumerate(tiles)}
    with ExitStack() as ctx:
        sb = lambda n, s, dt=F32: k.sb(n, s, dt, at=ctx)
        sem = k.stage_semaphores(ctx)
        hT = sb("h3T", [P, KT, S])
        stage = sb("stage2", [P, 3, KT, 3 * P])
        gain = sb("gain2", [P, D])
        h = sb("h3", [P, D])
        diff = sb("diff", [P, S])
        sumsq = sb("s2_sumsq", [P, NT])
        rstd = sb("s2_rstd", [P, NT])
        inv = sb("pool_inv", [P, 4, 16])
        w_pool = sb("w_pool", [P, 4, P])
        sums = sb("sums", [P, 2, 16 + S])
        pooled = sb("pooled", [P, S])
        small_in = sem("s2_small_in")
        gain_in = sem("s2_gain_in")
        stage_in = [sem(f"s2_stage_in{n}") for n in range(3)]
        stage_used = sem("s2_stage_used")
        sumsq_done = sem("s2_sumsq_done")
        root_ready = sem("s2_root")
        h_ready = sem("s2_h_ready")
        h_ps = sem("s2_h_ps")
        hT_ready = sem("s2_hT_ready")
        z_ps = sem("z_ps")
        z_ready = sem("z_ready")
        sums_set = sem("sums_set")
        pooled_ready = sem("pooled_ready")
        pool_ps = sem("pool_ps")
        pool_read = sem("pool_read")

        with nc.Block() as block:
            @block.sync
            def _(sp):
                sp.dma_start(k.cols[:], d["cols"]).then_inc(small_in, 16)
                sp.dma_start(gain[:], row(d["norm_gain_2"][0:1, :])).then_inc(gain_in, 16)
                sp.dma_start(inv[:], d["pool_inverse"]).then_inc(small_in, 16)
                sp.dma_start(w_pool[:], d["pool_w_2"].rearrange("g c n -> c g n")).then_inc(small_in, 16)
                w = d["w_in_2"].rearrange("(k p) n -> p k n", p=P)
                for n, (a, m) in enumerate(CHUNKS2):
                    if n >= 3:
                        sp.wait_ge(stage_used, n - 2)
                    sp.dma_start(stage[:, n % 3, :, 0:m * P], w[:, :, a * P:(a + m) * P]
                                 ).then_inc(stage_in[n % 3], 16)

            @block.tensor
            def _(pe):
                for t in range(NT):
                    pe.wait_ge(h_ready, t + 1)
                    if t:
                        pe.wait_ge(hT_ready, 2 * t)
                    for q in range(KT):
                        mm = pe.transpose(k.bank(6 + q // 4)[:, (q % 4) * P:(q % 4 + 1) * P],
                                          h[:, q * P:(q + 1) * P], k.sq[:, IDENT, :])
                        if q % 4 == 3:
                            mm.then_inc(h_ps, 1)
                pe.wait_ge(hT_ready, 2 * NT)
                at = 0
                for n, (a, m) in enumerate(CHUNKS2):
                    pe.wait_ge(stage_in[n % 3], 16 * (n // 3 + 1))
                    for c in range(m):
                        if at >= 4:
                            pe.wait_ge(z_ready, at - 3)
                        for q in range(KT):
                            mm = pe.matmul(k.bank(at % 4), stage[:, n % 3, q, c * P:(c + 1) * P],
                                           hT[:, q, :], start=(q == 0), stop=(q == KT - 1))
                        at += 1
                        mm.then_inc(z_ps, 1)
                    pe.wait_ge(z_ps, at)
                    pe.sem_inc(stage_used, 1)
                pe.wait_ge(small_in, 48)
                for g in range(4):
                    pe.wait_ge(pooled_ready, g + 1)
                    pe.matmul(k.bank(4 + g), w_pool[:, g, :], pooled[:], start=True, stop=True
                              ).then_inc(pool_ps, 1)

            @block.scalar
            def _(act):
                chain = k.act_chain.on(act)
                for t in range(NT):
                    act.activation(z2[:, 2 * t:2 * t + 2, 0:512], k.x[:, t, :].rearrange(
                        "p (a n) -> p a n", a=2), ACT.Square, accum_out=sumsq[:, t:t + 1]).then_inc(sumsq_done, 1)
                act.wait_ge(sumsq_done, NT)
                act.activation(rstd[:], sumsq[:], ACT.Sqrt, scale=1.0 / D, bias=k.eps[:, 0:1]
                               ).then_inc(root_ready, 1)
                for t in range(NT):
                    for part in range(2):
                        act.wait_ge(h_ps, 2 * t + part + 1)
                        act.activation(hT[:, 4 * part:4 * part + 4, t * P:(t + 1) * P],
                                       k.bank(6 + part).rearrange("p (a b) -> p a b", b=P),
                                       ACT.Copy).then_inc(hT_ready, 1)
                for n, f in enumerate(tiles):
                    act.wait_ge(z_ps, n + 1)
                    out = k.silu_b[:, f - G_B, :] if f >= G_B else z2[:, f, 1:S + 1]
                    act.activation(out, k.bank(n % 4), ACT.Silu if f >= G_B or G_A <= f < G_A + 4
                                   else ACT.Copy).then_inc(z_ready, 1)

            @block.gpsimd
            def _(pool):
                chain = k.pool_chain.on(pool)
                chain(pool.memset(sums[:], 0.0))
                pool.wait_ge(small_in, 48)
                for g, w in enumerate(WINDOWS):
                    u = z2[:, U_A + g, 1:S + 1]
                    pool.wait_ge(z_ready, arrival[U_A + g] + 1)
                    chain(pool.tensor_copy(sums[:, 0, 16:], u))
                    for n in range(g + 1):
                        s = 1 << n
                        chain(pool.tensor_tensor(sums[:, (n + 1) % 2, 16:], sums[:, n % 2, 16:],
                                                 sums[:, n % 2, 16 - s:16 + S - s], ALU.add))
                    src = sums[:, (g + 1) % 2, 16:]
                    if g:
                        pool.wait_ge(pool_ps, g)
                    pool.tensor_scalar(pooled[:, 16:], src[:, 16:], 1.0 / w, None, ALU.mult)
                    chain(pool.tensor_tensor(pooled[:, 0:16], src[:, 0:16], inv[:, g, :], ALU.mult))
                    pool.tensor_tensor(pooled[:], pooled[:], u, ALU.subtract).then_inc(pooled_ready, 1)
                    pool.wait_ge(pooled_ready, g + 1)

            @block.vector
            def _(dve):
                chain = k.dve_chain.on(dve)
                dve.wait_ge(root_ready, 1)
                dve.memset(z2[:, :, 0:1], 0.0)
                chain(dve.reciprocal(rstd[:], rstd[:]))
                dve.wait_ge(gain_in, 16)
                for t in range(NT):
                    if t:
                        dve.wait_ge(h_ps, 2 * t)
                    dve.scalar_tensor_tensor(h[:], k.x[:, t, :], rstd[:, t:t + 1], gain[:], ALU.mult,
                                             ALU.mult).then_inc(h_ready, 1)
                dve.wait_ge(small_in, 48)
                for f in sorted(range(R_F, LR_F + 1), key=lambda f: arrival[f]):
                    dve.wait_ge(z_ready, arrival[f] + 1)
                    chain(dve.tensor_tensor(diff[:], z2[:, f, 0:S], z2[:, f, 1:S + 1], ALU.subtract))
                    c = MU0 + f - R_F
                    chain(dve.scalar_tensor_tensor(z2[:, f, 1:S + 1], diff[:], k.cols[:, c:c + 1],
                                                   z2[:, f, 1:S + 1], ALU.mult, ALU.add))
                dve.wait_ge(z_ready, arrival[G_A + 3] + 1)
                for g in range(4):
                    dve.wait_ge(pool_ps, g + 1)
                    dve.scalar_tensor_tensor(k.y_pool[:, g, :], k.bank(4 + g), k.cols[:, PS0 + g:PS0 + g + 1],
                                             z2[:, G_A + g, 1:S + 1], ALU.mult, ALU.mult).then_inc(pool_read, 1)


def rwkv_features(k):
    nc, d, z2 = k.nc, k.d, k.z2
    r = z2[:, R_F:R_F + 4, 1:S + 1]
    key = z2[:, K_F:K_F + 4, 1:S + 1]
    v = z2[:, V_F:V_F + 4, 1:S + 1]
    with ExitStack() as ctx:
        sb = lambda n, s, dt=F32: k.sb(n, s, dt, at=ctx)
        sem = k.stage_semaphores(ctx)
        w_lora = sb("w_lora", [P, 4 * P])
        rate = sb("rate", [P, 4, S])
        sigw = sb("sigw", [P, 4, S])
        cum = sb("cum", [P, 4, S])
        grow = sb("decay_grow", [P, 4, S])
        kk = sb("kk", [P, 4, S])
        root = sb("kk_root", [P, 4, S])
        keep = sb("keep", [P, S])
        one_less = sb("one_less", [P, 4])
        lora_in = sem("lora_in")
        tanh_ready = sem("tanh_ready")
        lora_ps = sem("lora_ps")
        sigw_ready = sem("sigw_ready")
        rate_ready = sem("rate_ready")
        cum_ready = sem("cum_ready")
        prev_ready = sem("prev_ready")
        decay_ready = sem("decay_ready")
        kk_ready = sem("kk_ready")
        square_ready = sem("square_ready")
        norm_ps = sem("norm_ps")
        norm_clamped = sem("norm_clamped")
        norm_root = sem("norm_root")
        pair_ready = sem("rk_ready")
        bonus_ps = sem("bonus_ps")

        with nc.Block() as block:
            @block.sync
            def _(sp):
                sp.dma_start(w_lora[0:64, :], d["w_up_2"]).then_inc(lora_in, 16)
                sp.dma_start(w_lora[64:128, :], d["a_up_2"]).then_inc(lora_in, 16)

            @block.tensor
            def _(pe):
                pe.wait_ge(lora_in, 32)
                for j in range(4):
                    mm = pe.matmul(k.bank(4 + j), w_lora[64:128, j * P:(j + 1) * P],
                                   z2[64:128, LR_F, 1:S + 1], start=True, stop=True)
                mm.then_inc(lora_ps, 1)
                pe.wait_ge(tanh_ready, 1)
                for j in range(4):
                    mm = pe.matmul(k.bank(j), w_lora[0:64, j * P:(j + 1) * P],
                                   z2[0:64, LR_F, 1:S + 1], start=True, stop=True)
                mm.then_inc(lora_ps, 1)
                pe.wait_ge(square_ready, 1)
                pe.wait_ge(rate_ready, 4)
                for j in range(4):
                    mm = pe.matmul(k.bank(4 + j), k.sq[:, BLOCK, :], root[:, j, :], start=True, stop=True)
                mm.then_inc(norm_ps, 1)
                pe.wait_ge(pair_ready, 1)
                pe.wait_ge(sigw_ready, 4)
                for j in range(4):
                    mm = pe.matmul(k.bank(j), k.sq[:, BLOCK, :], k.bonus[:, j, :], start=True, stop=True)
                mm.then_inc(bonus_ps, 1)

            @block.scalar
            def _(act):
                act.activation(z2[0:64, LR_F, 1:S + 1], z2[0:64, LR_F, 1:S + 1], ACT.Tanh).then_inc(tanh_ready, 1)
                act.wait_ge(kk_ready, 1)
                act.activation(root[:], kk[:], ACT.Square).then_inc(square_ready, 1)
                act.wait_ge(lora_ps, 1)
                for j in range(4):
                    act.activation(rate[:, j, :], k.bank(4 + j), ACT.Sigmoid,
                                   bias=k.cols[:, A00 + j:A00 + j + 1]).then_inc(rate_ready, 1)
                act.wait_ge(lora_ps, 2)
                for j in range(4):
                    act.activation(sigw[:, j, :], k.bank(j), ACT.Sigmoid,
                                   bias=k.cols[:, W00 + j:W00 + j + 1]).then_inc(sigw_ready, 1)
                act.wait_ge(norm_clamped, 1)
                act.activation(root[:], root[:], ACT.Sqrt).then_inc(norm_root, 1)
                act.wait_ge(cum_ready, 4)
                act.activation(grow[:], cum[:], ACT.Exp, scale=LOG_DECAY).then_inc(decay_ready, 1)
                act.activation(k.rho[:], cum[:], ACT.Exp, scale=-LOG_DECAY).then_inc(decay_ready, 1)
                act.wait_ge(prev_ready, 1)
                act.activation(k.alpha[:], k.alpha[:], ACT.Exp, scale=-LOG_DECAY).then_inc(decay_ready, 1)

            @block.vector
            def _(dve):
                chain = k.dve_chain.on(dve)
                col = lambda c, j: k.cols[:, c + j:c + j + 1]
                for j in range(4):
                    ins = dve.tensor_scalar(kk[:, j, :], key[:, j, :], col(KK0, j), None, ALU.mult)
                ins.then_inc(kk_ready, 1)
                dve.tensor_scalar(one_less[:], k.cols[:, KA0:KA0 + 4], -1.0, 1.0, ALU.mult, ALU.add)
                chain(dve.memset(keep[:], 1.0))
                chain(dve.memset(keep[:, 0:S:CH], 0.0))
                dve.wait_ge(rate_ready, 4)
                for j in range(4):
                    ins = dve.tensor_scalar(k.kappa[:, j, :], rate[:, j, :], col(KA0, j), one_less[:, j:j + 1],
                                            ALU.mult, ALU.add)
                chain(ins)
                chain(dve.tensor_tensor(k.kappa[:], k.kappa[:], key, ALU.mult))
                for j in range(4):
                    ins = dve.scalar_tensor_tensor(k.bonus[:, j, :], r[:, j, :], col(RK0, j), k.kappa[:, j, :],
                                                   ALU.mult, ALU.mult)
                ins.then_inc(pair_ready, 1)
                for j in range(4):
                    dve.wait_ge(sigw_ready, j + 1)
                    dve.tensor_tensor_scan(cum[:, j, :], keep[:], sigw[:, j, :], 0.0, ALU.mult,
                                           ALU.add).then_inc(cum_ready, 1)
                dve.wait_ge(cum_ready, 4)
                dve.tensor_tensor(k.alpha[:], cum[:], sigw[:], ALU.subtract).then_inc(prev_ready, 1)
                dve.wait_ge(norm_ps, 1)
                for j in range(4):
                    ins = dve.tensor_scalar(root[:, j, :], k.bank(4 + j), 1e-24, None, ALU.max)
                ins.then_inc(norm_clamped, 1)
                dve.wait_ge(norm_root, 1)
                chain(dve.reciprocal(root[:], root[:]))
                chain(dve.tensor_tensor(kk[:], kk[:], root[:], ALU.mult))
                chain(dve.tensor_tensor(k.beta[:], kk[:], rate[:], ALU.mult))
                dve.wait_ge(decay_ready, 1)
                chain(dve.tensor_tensor(k.beta[:], k.beta[:], grow[:], ALU.mult))
                chain(dve.tensor_tensor(k.kappa[:], k.kappa[:], grow[:], ALU.mult))
                dve.wait_ge(decay_ready, 2)
                chain(dve.tensor_copy(k.last[:], k.rho[:, :, CH - 1:S:CH]))
                chain(dve.tensor_tensor(k.rho[:], k.rho[:], r, ALU.mult))
                dve.wait_ge(decay_ready, 3)
                chain(dve.scalar_tensor_tensor(k.alpha[:], kk[:], -1.0, k.alpha[:], ALU.mult, ALU.mult))
                dve.wait_ge(bonus_ps, 1)
                for j in range(4):
                    ins = dve.tensor_tensor(k.bonus[:, j, :], k.bank(j), v[:, j, :], ALU.mult)
                chain(ins)


def rwkv_turn(k, name, pairs):
    nc = k.nc
    with ExitStack() as ctx:
        sem = k.stage_semaphores(ctx)
        turn_ps = sem(name + "_tok_ps")
        turn_read = sem(name + "_tok_read")
        jobs = [(dst, src, t) for dst, src in pairs for t in range(NT)]
        with nc.Block() as block:
            @block.tensor
            def _(pe):
                for n, (dst, src, t) in enumerate(jobs):
                    if n >= 8:
                        pe.wait_ge(turn_read, n - 7)
                    for j in range(4):
                        mm = pe.transpose(k.bank(n % 8)[:, j * P:(j + 1) * P], src[:, j, t * P:(t + 1) * P],
                                          k.sq[:, IDENT, :])
                    mm.then_inc(turn_ps, 1)

            @block.scalar
            def _(act):
                for n, (dst, src, t) in enumerate(jobs):
                    act.wait_ge(turn_ps, n + 1)
                    act.activation(dst[:, t, :], k.bank(n % 8), ACT.Copy).then_inc(turn_read, 1)


def rwkv_inverse(k, v_tok, solveT, out_sa, r_v, y_v):
    nc = k.nc
    with ExitStack() as ctx:
        sb = lambda n, s, dt=F32: k.sb(n, s, dt, at=ctx)
        sem = k.stage_semaphores(ctx)
        masks = sb("level_masks", [P, NSQ - LEVEL0, P])
        mT = sb("mT", [P, 2, HR, P])
        level = sb("level", [P, 2, HR, P])
        solve = sb("solve", [P, 2, HR, P])
        product = sb("product", [P, 2, HR, P])
        mask_in = sem("mask_in")
        prod_ps = sem("mat_ps")
        prod_read = sem("mat_read")
        m_ready = sem("m_ready")
        level_ready = sem("level_ready")
        p_ps = sem("p_ps")
        p_ready = sem("p_ready")
        x_ps = sem("x_ps")
        x_ready = sem("solve_ready")
        v_ps = sem("vpart_ps")
        v_read = sem("vpart_read")
        heads = lambda ap: ap.rearrange("p (h n) -> p h n", h=HR)
        over_heads = lambda m: m.unsqueeze(1).broadcast_to([P, HR, P])
        NL = 5
        kinds = (("beta", "alpha"), ("alpha", "beta"), ("kappa", "alpha"), ("kappa", "rho"), ("beta", "rho"))

        with nc.Block() as block:
            @block.sync
            def _(sp):
                sp.dma_start(masks[:], k.d["square"][:, LEVEL0:NSQ, :]).then_inc(mask_in, 16)

            @block.tensor
            def _(pe):
                n = 0
                for pair in range(NT // 2):
                    for e in range(2):
                        t = 2 * pair + e
                        for m, (a, b) in enumerate(kinds):
                            if n >= 4:
                                pe.wait_ge(prod_read, n - 3)
                            for h in range(HR):
                                r = (h % 2) * CH
                                c = place(h) * P
                                left = {"alpha": k.alpha, "beta": k.beta, "kappa": k.kappa}[a]
                                right = {"alpha": k.alpha, "beta": k.beta, "rho": k.rho}[b]
                                mm = pe.matmul(k.pp[n % 4][:, c:c + P],
                                               left[r:r + CH, h // 2, t * P:(t + 1) * P],
                                               right[r:r + CH, h // 2, t * P:(t + 1) * P],
                                               start=True, stop=True)
                            mm.then_inc(prod_ps, 1)
                            n += 1
                            if m in (2, 3):
                                pe.wait_ge(prod_read, n)
                                for h in range(HR):
                                    mm = pe.matmul(k.pp[(n - 1) % 4][:, place(h) * CH:(place(h) + 1) * CH],
                                                   product[:, m - 2, place(h), :],
                                                   v_tok[:, t, h * CH:(h + 1) * CH], start=True, stop=True)
                                mm.then_inc(v_ps, 1)
                                pe.wait_ge(v_read, 2 * t + m - 1)
                    for s in range(NL):
                        for e in range(2):
                            t = 2 * pair + e
                            at = (pair * NL + s) * 2 + e
                            pe.wait_ge(level_ready, at + 1)
                            pe.wait_ge(x_ready, 2 * (NL + 1) * pair + 2 * s + e + 1)
                            pe.wait_ge(prod_read, n)
                            for h in range(HR):
                                mm = pe.matmul(k.pp[2 * e][:, h * P:(h + 1) * P], level[:, e, h, :],
                                               solve[:, e, h, :], start=True, stop=True)
                            mm.then_inc(p_ps, 1)
                        for e in range(2):
                            t = 2 * pair + e
                            at = (pair * NL + s) * 2 + e
                            pe.wait_ge(p_ready, at + 1)
                            for h in range(HR):
                                mm = pe.matmul(k.pp[2 * e + 1][:, h * P:(h + 1) * P], product[:, e, h, :],
                                               solveT[:, t, h, :], start=True, stop=True)
                            if s < NL - 1:
                                for h in range(HR):
                                    mm = pe.matmul(k.pp[2 * e][:, h * P:(h + 1) * P], solveT[:, t, h, :],
                                                   product[:, e, h, :], start=True, stop=True)
                            mm.then_inc(x_ps, 1)
                    pe.wait_ge(x_ready, 2 * (NL + 1) * (pair + 1))

            @block.gpsimd
            def _(pool):
                pool.wait_ge(mask_in, 16)
                for pair in range(NT // 2):
                    for s in range(NL):
                        for e in range(2):
                            at = (pair * NL + s) * 2 + e
                            pool.wait_ge(m_ready, 2 * pair + e + 1)
                            if at >= 2:
                                pool.wait_ge(p_ps, at - 1)
                            pool.tensor_tensor(level[:, e], mT[:, e], over_heads(masks[:, s, :]),
                                               ALU.mult).then_inc(level_ready, 1)

            @block.scalar
            def _(act):
                for pair in range(NT // 2):
                    for e in range(2):
                        t = 2 * pair + e
                        act.wait_ge(prod_ps, 5 * t + 1)
                        if pair:
                            act.wait_ge(level_ready, 2 * NL)
                        act.activation(mT[:, e], heads(k.pp[(5 * t) % 4][:, :]), ACT.Copy).then_inc(m_ready, 1)
                        for m in range(2):
                            act.wait_ge(v_ps, 2 * t + m + 1)
                            act.activation((r_v, y_v)[m][:, t, :], k.pp[(5 * t + 2 + m) % 4][:, 0:HR * CH],
                                           ACT.Copy).then_inc(v_read, 1)
                    for s in range(NL):
                        for e in range(2):
                            at = (pair * NL + s) * 2 + e
                            act.wait_ge(p_ps, at + 1)
                            act.activation(product[:, e], heads(k.pp[2 * e][:, :]), ACT.Copy).then_inc(p_ready, 1)

            @block.vector
            def _(dve):
                chain = k.dve_chain.on(dve)
                dve.wait_ge(mask_in, 16)
                for pair in range(NT // 2):
                    for e in range(2):
                        t = 2 * pair + e
                        for m in range(5):
                            n = 5 * t + m
                            dve.wait_ge(prod_ps, n + 1)
                            src = heads(k.pp[n % 4][:, :])
                            if m < 2:
                                out = (solveT[:, t], solve[:, e])[m]
                                if m == 0:
                                    dve.wait_ge(m_ready, t + 1)
                                    src = mT[:, e]
                                chain(dve.tensor_tensor(out, src, over_heads(masks[:, NL + m, :]), ALU.mult))
                                chain(dve.tensor_tensor(out, out, over_heads(k.sq[:, IDENT, :]), ALU.add))
                                dve.sem_inc(prod_read, 1)
                                if m == 1:
                                    dve.sem_inc(x_ready, 1)
                            elif m < 4:
                                if t:
                                    dve.wait_ge(v_ps, 2 * t - 2 + m - 1)
                                dve.tensor_tensor(product[:, m - 2], src, over_heads(
                                    k.sq[:, (LT, LE)[m - 2], :]), ALU.mult).then_inc(prod_read, 1)
                            else:
                                dve.tensor_tensor(out_sa[:, t], src, over_heads(k.sq[:, LE, :]),
                                                  ALU.mult).then_inc(prod_read, 1)
                    for s in range(NL):
                        for e in range(2):
                            t = 2 * pair + e
                            at = (pair * NL + s) * 2 + e
                            dve.wait_ge(x_ps, at + 1)
                            ins = dve.tensor_tensor(solveT[:, t], solveT[:, t], heads(k.pp[2 * e + 1][:, :]), ALU.add)
                            if s < NL - 1:
                                ins = dve.tensor_tensor(solve[:, e], solve[:, e], heads(k.pp[2 * e][:, :]), ALU.add)
                            ins.then_inc(x_ready, 1)
                            dve.wait_ge(x_ready, 2 * (NL + 1) * pair + 2 + 2 * s + e + 1)


def stage_rwkv(k):
    nc, d, v_tok = k.nc, k.d, k.v_tok
    with ExitStack() as ctx:
        sb = lambda n, s, dt=F32: k.sb(n, s, dt, at=ctx)
        beta_tok = sb("beta_tok", [P, NT, 4 * P])
        kappa_tok = sb("kappa_tok", [P, NT, 4 * P])
        rwkv_turn(k, "bk", ((beta_tok, k.beta), (kappa_tok, k.kappa)))
        solveT = sb("solveT", [P, NT, HR, P])
        out_sa = sb("out_sa", [P, NT, HR, P])
        r_v = sb("r_v", [P, NT, HR * CH])
        y_v = sb("y_v", [P, NT, HR * CH])
        rwkv_inverse(k, v_tok, solveT, out_sa, r_v, y_v)
        rwkv_states(k, v_tok, beta_tok, kappa_tok, solveT, out_sa, r_v, y_v)
        output(k, y_v)


def rwkv_states(k, v_tok, beta_tok, kappa_tok, solveT, out_sa, r_v, y_v):
    nc = k.nc
    with ExitStack() as ctx:
        sb = lambda n, s, dt=F32: k.sb(n, s, dt, at=ctx)
        sem = k.stage_semaphores(ctx)
        state = sb("rwkv_state", [P, 4, CH])
        rhs = sb("rhs", [P, 2, 4 * CH])
        sa = sb("sa", [P, HR * CH])
        state_ready = sem("rwkv_state_ready")
        rhs_ps = sem("rhs_ps")
        rhs_ready = sem("rhs_ready")
        sa_ps = sem("sa_ps")
        sa_ready = sem("sa_ready")
        y_ps = sem("rwkv_y_ps")
        y_read = sem("rwkv_y_read")
        next_ps = sem("next_ps")

        with nc.Block() as block:
            @block.tensor
            def _(pe):
                for c in range(NCH):
                    t, o = c // 2, (c % 2) * CH
                    rows = slice(o, o + CH)
                    pe.wait_ge(state_ready, c + 1)
                    for h in range(HR):
                        r = (h % 2) * CH
                        mm = pe.matmul(k.bank(h % 2)[rows, h // 2 * CH:(h // 2 + 1) * CH],
                                       k.alpha[r:r + CH, h // 2, c * CH:(c + 1) * CH],
                                       state[r:r + CH, h // 2, :], start=True, stop=True)
                    mm.then_inc(rhs_ps, 1)
                    if c:
                        pe.wait_ge(y_read, c)
                    for h in range(HR):
                        r = (h % 2) * CH
                        pe.matmul(k.bank(4 + h % 2)[rows, h // 2 * CH:(h // 2 + 1) * CH],
                                  k.rho[r:r + CH, h // 2, c * CH:(c + 1) * CH],
                                  state[r:r + CH, h // 2, :], start=True, stop=True)
                    for h in range(HR):
                        r = (h % 2) * CH
                        pe.matmul(k.bank(3)[r:r + CH, h // 2 * CH:(h // 2 + 1) * CH],
                                  kappa_tok[rows, t, h * CH:(h + 1) * CH], v_tok[rows, t, h * CH:(h + 1) * CH],
                                  start=(h < 2), stop=False, skip_group_check=True)
                    pe.wait_ge(rhs_ready, c + 1)
                    for h in range(HR):
                        q = place(h)
                        mm = pe.matmul(k.bank(2)[rows, q * CH:(q + 1) * CH], solveT[rows, t, q, rows],
                                       rhs[rows, h % 2, h // 2 * CH:(h // 2 + 1) * CH], start=True, stop=True)
                    mm.then_inc(sa_ps, 1)
                    pe.wait_ge(sa_ready, c + 1)
                    for h in range(HR):
                        r = (h % 2) * CH
                        q = place(h)
                        mm = pe.matmul(k.bank(3)[r:r + CH, h // 2 * CH:(h // 2 + 1) * CH],
                                       beta_tok[rows, t, h * CH:(h + 1) * CH], sa[rows, q * CH:(q + 1) * CH],
                                       start=False, stop=(h >= HR - 2), skip_group_check=True)
                    mm.then_inc(next_ps, 1)
                    for h in range(HR):
                        q = place(h)
                        mm = pe.matmul(k.bank(6)[rows, q * CH:(q + 1) * CH], out_sa[rows, t, q, rows],
                                       sa[rows, q * CH:(q + 1) * CH], start=True, stop=True)
                    mm.then_inc(y_ps, 1)

            @block.scalar
            def _(act):
                for c in range(NCH):
                    rows = slice((c % 2) * CH, (c % 2) * CH + CH)
                    act.wait_ge(sa_ps, c + 1)
                    act.activation(sa[rows, :], k.bank(2)[rows, :], ACT.Copy).then_inc(sa_ready, 1)

            @block.vector
            def _(dve):
                chain = k.dve_chain.on(dve)
                dve.memset(state[:], 0.0).then_inc(state_ready, 1)
                dve.wait_ge(state_ready, 1)
                for c in range(NCH):
                    t = c // 2
                    rows = slice((c % 2) * CH, (c % 2) * CH + CH)
                    two = lambda ap: ap.rearrange("p (b n) -> p b n", b=2)
                    dve.wait_ge(rhs_ps, c + 1)
                    dve.tensor_tensor(rhs[rows], two(k.pp[0][rows, :])[:, :, 0:4 * CH], two(r_v[rows, t, :]),
                                      ALU.add).then_inc(rhs_ready, 1)
                    dve.wait_ge(next_ps, c + 1)
                    chain(dve.tensor_tensor(state[:], state[:], k.bank(3)[:, 0:4 * CH].rearrange(
                        "p (j n) -> p j n", j=4), ALU.add))
                    dve.tensor_tensor(state[:], state[:], k.last[:, :, c:c + 1].broadcast_to([P, 4, CH]),
                                      ALU.mult).then_inc(state_ready, 1)
                    dve.wait_ge(state_ready, c + 2)
                    dve.wait_ge(y_ps, c + 1)
                    y = y_v[rows, t, :]
                    chain(dve.tensor_tensor(two(y), two(y), two(k.pp[2][rows, :])[:, :, 0:4 * CH], ALU.add))
                    dve.tensor_tensor(y, y, k.bank(6)[rows, :], ALU.add).then_inc(y_read, 1)


def output(k, y):
    nc, d = k.nc, k.d
    k.w_out2_in = k.sem("w_out2_in")
    with ExitStack() as ctx:
        sb = lambda n, s, dt=F32: k.sb(n, s, dt, at=ctx)
        sem = k.stage_semaphores(ctx)
        w_out2 = sb("w_out2", [P, KT, D])
        square = sb("gn_square", [P, HR * CH])
        mean = sb("gn_mean", [P, HR])
        var = sb("gn_var", [P, HR])
        normed = sb("normed", [P, 2, HR * CH])
        final = sb("final", [P, 2, D])
        gain = sb("final_gain", [P, D])
        junk = flat(k.alpha[:])[:, 0:D]
        sumsq = sb("final_sumsq", [P, NT])
        rstd = sb("final_rstd", [P, NT])
        w_in = sem("final_w_in")
        centred = sem("centred")
        squared = sem("squared")
        var_ready = sem("var_ready")
        gn_root = sem("gn_root")
        normed_ready = sem("normed_ready")
        turned_ps = sem("gn_turned_ps")
        y_ready = sem("y_rwkv_ready")
        out_ps = sem("out_ps")
        sum_ready = sem("sum_ready")
        final_root = sem("final_root")
        final_ready = sem("final_ready")
        out_done = sem("out_done")
        yb = k.beta
        heads = lambda ap: ap.rearrange("p (h n) -> p h n", h=HR)

        with nc.Block() as block:
            @block.sync
            def _(sp):
                sp.dma_start(w_out2[:], d["w_out_2"].rearrange("(k p) n -> p k n", p=P)).then_inc(w_in, 16)
                sp.dma_start(gain[:], row(d["final_gain_2"][0:1, :])).then_inc(w_in, 16)
                for t in range(NT):
                    sp.wait_ge(final_ready, t + 1)
                    sp.dma_start(d["out"][t * P:(t + 1) * P, :], final[:, t % 2, :]).then_inc(out_done, 16)
                    sp.wait_ge(out_done, 16 * (t + 1))

            @block.tensor
            def _(pe):
                for t in range(NT):
                    pe.wait_ge(normed_ready, t + 1)
                    for j in range(4):
                        mm = pe.transpose(k.bank(j)[:, t * P:(t + 1) * P], normed[:, t % 2, j * P:(j + 1) * P],
                                          k.sq[:, IDENT, :])
                    mm.then_inc(turned_ps, 1)
                pe.wait_ge(w_in, 32)
                for t in range(NT):
                    if t >= 2:
                        pe.wait_ge(sum_ready, t - 1)
                    for n in range(2):
                        for q in range(KT):
                            if q == 4 and t == 0 and n == 0:
                                pe.wait_ge(y_ready, 1)
                            src = k.y_pool[:, q, :] if q < 4 else yb[:, q - 4, :]
                            mm = pe.matmul(k.pp[2 + t % 2][:, n * 512:(n + 1) * 512], src[:, t * P:(t + 1) * P],
                                           w_out2[:, q, n * 512:(n + 1) * 512],
                                           start=(q == 0), stop=(q == KT - 1))
                    mm.then_inc(out_ps, 1)

            @block.scalar
            def _(act):
                chain = k.act_chain.on(act)
                for t in range(NT):
                    act.wait_ge(centred, t + 1)
                    act.activation(square[:], y[:, t, :], ACT.Square).then_inc(squared, 1)
                    act.wait_ge(var_ready, t + 1)
                    act.activation(var[:], var[:], ACT.Sqrt, scale=1.0 / CH, bias=k.eps[:, 1:2]).then_inc(gn_root, 1)
                for t in range(NT):
                    act.wait_ge(sum_ready, t + 1)
                    chain(act.activation(junk, k.x[:, t, :], ACT.Square, accum_out=sumsq[:, t:t + 1]))
                    act.activation(rstd[:, t:t + 1], sumsq[:, t:t + 1], ACT.Sqrt, scale=1.0 / D,
                                   bias=k.eps[:, 0:1]).then_inc(final_root, 1)

            @block.vector
            def _(dve):
                chain = k.dve_chain.on(dve)
                for t in range(NT):
                    yt = heads(y[:, t, :])
                    chain(dve.tensor_reduce(mean[:], yt, AX.X, ALU.add))
                    chain(dve.tensor_scalar(mean[:], mean[:], 1.0 / CH, None, ALU.mult))
                    dve.tensor_tensor(yt, yt, mean[:].unsqueeze(2).broadcast_to([P, HR, CH]),
                                      ALU.subtract).then_inc(centred, 1)
                    dve.wait_ge(squared, t + 1)
                    dve.tensor_reduce(var[:], heads(square[:]), AX.X, ALU.add).then_inc(var_ready, 1)
                    dve.wait_ge(gn_root, t + 1)
                    chain(dve.reciprocal(var[:], var[:]))
                    if t >= 2:
                        dve.wait_ge(turned_ps, t - 1)
                    out = normed[:, t % 2, :].rearrange("p (j two n) -> p two j n", two=2, n=CH)
                    dve.tensor_tensor(out, y[:, t, :].rearrange("p (two j n) -> p two j n", two=2, n=CH),
                                      var[:].rearrange("p (two j) -> p two j", two=2).unsqueeze(3).broadcast_to(
                                          [P, 2, 4, CH]), ALU.mult).then_inc(normed_ready, 1)
                    dve.wait_ge(normed_ready, t + 1)
                dve.wait_ge(turned_ps, NT)
                for j in range(4):
                    ins = dve.tensor_scalar(yb[:, j, :], k.bank(j), k.cols[:, GG0 + j:GG0 + j + 1],
                                            k.cols[:, GB0 + j:GB0 + j + 1], ALU.mult, ALU.add)
                chain(ins)
                chain(dve.tensor_tensor(yb[:], yb[:], k.bonus[:], ALU.add))
                dve.tensor_tensor(yb[:], yb[:], k.silu_b[:], ALU.mult).then_inc(y_ready, 1)
                dve.wait_ge(w_in, 32)
                for t in range(NT):
                    dve.wait_ge(out_ps, t + 1)
                    dve.tensor_tensor(k.x[:, t, :], k.x[:, t, :], k.pp[2 + t % 2][:, :], ALU.add
                                      ).then_inc(sum_ready, 1)
                    dve.wait_ge(final_root, t + 1)
                    chain(dve.reciprocal(rstd[:, t:t + 1], rstd[:, t:t + 1]))
                    if t >= 2:
                        dve.wait_ge(out_done, 16 * (t - 1))
                    dve.scalar_tensor_tensor(final[:, t % 2, :], k.x[:, t, :], rstd[:, t:t + 1], gain[:],
                                             ALU.mult, ALU.mult).then_inc(final_ready, 1)
                    dve.wait_ge(final_ready, t + 1)


def build(nc, dram):
    with ExitStack() as ctx:
        k = Core(nc, ctx, dram)
        with ExitStack() as front:
            stage_front(k, front)
            stage_mixers(k, front)
            stage_router(k, front)
        stage_experts(k)
        stage_combine(k)
        with ExitStack() as scope:
            stage_second(k, scope)
            rwkv_features(k)
            rwkv_turn(k, "v", ((k.v_tok, k.z2[:, V_F:V_F + 4, 1:S + 1]),))
        stage_rwkv(k)


def packed_columns(a):
    names = ["shift_mu_2", "w0_2", "a0_2", "k_k_2", "k_a_2", "r_k_2", "gn_gain_2", "gn_bias_2",
             "pool_scale_2", "c"]
    return np.ascontiguousarray(np.concatenate([np.asarray(a[n]).reshape(-1, P) for n in names]).T)


def kernel(**inputs):
    import concourse.bacc as bacc
    from concourse.bass_utils import run_bass_kernel_spmd

    a = {n: np.asarray(v) for n, v in inputs.items()}
    arrays = {
        "x": a["x"][0],
        "cols": packed_columns(a),
        "w_gate_up": a["w_gate_up"][0].reshape(NE, KT, P, NM, P, 2).transpose(0, 3, 2, 1, 5, 4).reshape(
            NE * NM * P, KT * 2 * P),
        "w_down": a["w_down"][0].reshape(NE * NM * P, D),
        "b_gate_up": a["b_gate_up"][0].reshape(NE, NM, P, 2).transpose(0, 2, 1, 3).reshape(NE * P, 2 * NM),
        "square": square_constants(),
        "log_count": attention_constant(),
        "rope": rope_constant(),
        "route": route_constant(),
        "pool_inverse": pool_constant(),
        "token": np.ascontiguousarray(np.arange(S, dtype=np.int32).reshape(NT, P).T),
        "w_gate_lr": np.concatenate([a["w_gate_lr"][0], a["b_gate"]]),
    }
    for n in ("w_mod", "w_in", "w_out", "router_w", "b_down", "w_in_2", "pool_w_2", "w_up_2", "a_up_2",
              "w_out_2"):
        arrays[n] = a[n][0]
    for n in ("b_mod", "g_pre_mix", "g_gla", "g_post_mix", "g_pre_ffn", "router_b", "g_post_ffn",
              "norm_gain_2", "final_gain_2"):
        arrays[n] = a[n].reshape(1, -1)

    nc = bacc.Bacc("TRN2", target_bir_lowering=False, num_devices=1)
    dram, sent = {}, {}
    for n, v in arrays.items():
        v = np.ascontiguousarray(v)
        sent["in_" + n] = v
        dram[n] = nc.dram_tensor("in_" + n, v.shape, mybir.dt.from_np(v.dtype), kind="ExternalInput").ap()
    dram["out"] = nc.dram_tensor("out", [S, D], F32, kind="ExternalOutput").ap()
    dram["h2"] = nc.dram_tensor("h2_rows", [S, D], F32, kind="Internal").ap()
    dram["slot_token"] = nc.dram_tensor("slot_token", [(NBLK + 1) * SLOTS, 1], I32, kind="Internal").ap()
    dram["expert_rows"] = nc.dram_tensor("expert_rows", [NBLK * SLOTS, D], F32, kind="Internal").ap()
    build(nc, dram)
    result = run_bass_kernel_spmd(nc, [sent], core_ids=[0])
    return result.results[0]["out"].reshape(1, S, D)
```

```python
from contextlib import ExitStack

import numpy as np
import concourse.bass as bass
from concourse import mybir

F32 = mybir.dt.float32
F32R = mybir.dt.float32r
I32 = mybir.dt.int32
U32 = mybir.dt.uint32
ALU = mybir.AluOpType
ACT = mybir.ActivationFunctionType
AX = mybir.AxisListType

P = 128
S = 512
NT = S // P
D = 1024
KT = D // P
HA, DA = 8, 64
HG, DK, DV = 4, 64, 128
RANK = 16
D_IN = 3 * HA * DA + 2 * HG * DK + 2 * HG * DV + RANK
QA, KA, VA = 0, 512, 1024
QG, KG, VG, RG, LR = 1536, 1792, 2048, 2560, 3072
NE, TOPK = 32, 4
SLOTS = 128
EXTRA = (S * TOPK) // (SLOTS + 1)
NBLK = NE + EXTRA
TABLE = 3 * (NBLK + 1) + 2
NM = 8
GN_EPS = 64e-5
EPS = 1e-6
LIMIT, ALPHA = 7.0, 1.702
CH = 64
D_IN2 = 3200
NF2 = D_IN2 // P
LOG_DECAY = float(np.exp(-0.5))
WINDOWS = (2, 4, 8, 16)

MU0, W00, A00, KK0, KA0, RK0, GG0, GB0, PS0, C0 = 0, 13, 17, 21, 25, 29, 33, 37, 41, 45
NCOL = 53

IDENT, ONES, BLOCK, CUM, SUF, BEFORE, LT, LE = range(8)
LEVEL0 = 8
NSQ = LEVEL0 + 7
NSQ_KEPT = 8


def square_constants():
    i = np.arange(P)[:, None]
    j = np.arange(P)[None, :]
    same = i // CH == j // CH
    m = np.zeros((NSQ, P, P), np.float32)
    m[IDENT] = i == j
    m[ONES] = 1.0
    m[BLOCK] = same
    m[CUM] = (same & (i <= j)) / 16.0
    m[SUF] = (same & (i > j)) / 16.0
    m[BEFORE] = i < j
    m[LT] = same & (i < j)
    m[LE] = same & (i <= j)
    for n in range(5):
        s = 2 << n
        m[LEVEL0 + n] = (i // (2 * s) == j // (2 * s)) & (i // s < j // s)
    m[LEVEL0 + 5] = (i // 2 == j // 2) & (i < j)
    m[LEVEL0 + 6] = (i // 2 == j // 2) & (i > j)
    return np.ascontiguousarray(m.transpose(1, 0, 2))


def attention_constant():
    t = np.arange(S)[:, None]
    j = np.arange(S)[None, :]
    d = t - j
    n = sum(((d >= 0) & (d % dil == 0) & (d <= window)).astype(np.float64)
            for window, dil in ((128, 1), (512, 4), (2048, 16)))
    m = np.where(n > 0, np.log(np.maximum(n, 1)), -1e30).astype(np.float32)
    return np.ascontiguousarray(m.reshape(NT, P, S).transpose(1, 0, 2))


def rope_constant():
    half = DA // 2
    freq = (10000.0 ** (-np.arange(half, dtype=np.float32) / half)).astype(np.float32)
    ang = np.arange(S, dtype=np.float32)[:, None] * freq[None, :]
    cs = np.stack([np.cos(ang), np.sin(ang)], 1).astype(np.float32)
    both = np.stack([cs * DA ** -0.5, cs], 1)
    return np.ascontiguousarray(both.reshape(NT, P, 2, 2, half).transpose(1, 0, 2, 3, 4))


def count_constant():
    return np.ascontiguousarray(np.broadcast_to(np.arange(NBLK + 1, dtype=np.float32), (P, NBLK + 1)))


def picked_constant():
    e = np.arange(NE)[:, None]
    p = np.arange(P)[None, :]
    return np.ascontiguousarray(((p % NE == e) & (p < 2 * NE)).astype(np.float32).reshape(-1, 1))


def pool_constant():
    pos = np.arange(16)
    m = np.stack([1.0 / np.minimum(pos + 1, w) for w in WINDOWS]).astype(np.float32)
    return np.ascontiguousarray(np.broadcast_to(m, (P, 4, 16)))


class Chain:

    def __init__(self, sem):
        self.sem, self.n = sem, 0

    def on(self, eng):
        def chained(ins):
            self.n += 1
            ins.then_inc(self.sem, 1)
            eng.wait_ge(self.sem, self.n)
        return chained


class Core:

    def __init__(self, nc, ctx, dram):
        self.nc, self.ctx, self.d = nc, ctx, dram
        self.sb = lambda n, s, dt=F32, at=None: (at or ctx).enter_context(nc.sbuf_tensor(n, s, dt))
        self.sem = lambda n: ctx.enter_context(nc.semaphore(n))
        self.pp = [ctx.enter_context(nc.psum_tensor(f"banks{j}", [P, 1024], F32)) for j in range(4)]
        self.dve_chain = Chain(self.sem("dve_chain"))
        self.act_chain = Chain(self.sem("act_chain"))
        self.pool_chain = Chain(self.sem("pool_chain"))

    def stage_semaphores(self, ctx):
        own = []

        def give_back():
            self.nc.clear_and_free_semaphores(own)
            self.nc.all_engine_barrier()

        def sem(name):
            own.append(self.nc.alloc_semaphore(name))
            return own[-1]

        ctx.callback(give_back)
        return sem

    def bank(self, n):
        return self.pp[n // 2][:, (n % 2) * 512:(n % 2) * 512 + 512]


def flat(ap):
    return ap.rearrange("p a b -> p (a b)")


def stage_front(k, front):
    nc, d = k.nc, k.d
    k.x = k.sb("x", [P, NT, D])
    k.eps = k.sb("eps", [P, 2])
    k.gate2 = k.sb("gate2", [P, D])
    k.sq = k.sb("sq", [P, NSQ_KEPT, P])
    k.dest = k.sb("dest", [P, NT, TOPK], I32)
    k.gates = k.sb("gates", [P, NT, TOPK])
    k.gateT = k.sb("gateT", [NE, S])
    k.table = k.sb("table", [1, TABLE], I32)
    k.mod = k.sb("mod", [P, 6, D], at=front)
    k.proj = k.sb("proj", [P, NT, D_IN], at=front)
    with ExitStack() as ctx:
        sb = lambda n, s, dt=F32: k.sb(n, s, dt, at=ctx)
        sem = k.stage_semaphores(ctx)
        hT = sb("hT", [P, KT, S])
        stage = sb("stage", [P, 3, KT, 512])
        gain = sb("gain", [P, 2, D])
        col = sb("col_c", [P, KT])
        ccol = sb("ccol", [P, 3, KT])
        cb = sb("cb", [P, KT, P])
        h = sb("h", [P, 2, D])
        sumsq = sb("sumsq", [P, NT])
        rstd = sb("rstd", [P, NT])
        small_in = sem("small_in")
        eps_set = sem("eps_set")
        x_in = sem("x_in")
        gain_in = [sem(f"gain_in{i}") for i in range(2)]
        gain_used = sem("gain_used")
        stage_in = [sem(f"stage_in{i}") for i in range(3)]
        stage_used = sem("stage_used")
        c_exp = sem("c_exp")
        c_ready = sem("c_ready")
        mod_ps = sem("mod_ps")
        mod_done = sem("mod_done")
        sumsq_ready = sem("sumsq_ready")
        root_ready = sem("root_ready")
        h_ready = sem("h_ready")
        h_turned = sem("h_turned")
        hT_ready = sem("hT_ready")
        proj_ps = sem("proj_ps")
        proj_done = sem("proj_done")
        w_in = d["w_in"].rearrange("(k p) n -> p k n", p=P)
        w_mod = d["w_mod"].rearrange("(k p) n -> p k n", p=P)
        items = [("mod", j) for j in range(4)] + [("in", j) for j in range(7)] + \
                [("mod", j) for j in range(4, 12)]
        gains = ["g_pre_mix", "g_post_mix", "g_pre_ffn", "g_post_ffn"]

        with nc.Block() as block:
            @block.sync
            def _(sp):
                sp.dma_start(col[:], d["cols"][:, C0:C0 + KT]).then_inc(small_in, 16)
                for n, (kind, j) in enumerate(items):
                    if n >= 3:
                        sp.wait_ge(stage_used, n - 2)
                    w = w_mod[:, :, j * 512:(j + 1) * 512] if kind == "mod" else \
                        w_in[:, :, j * 512:min((j + 1) * 512, D_IN)]
                    sp.dma_start(stage[:, n % 3, :, 0:w.shape[2]], w).then_inc(stage_in[n % 3], 16)

            @block.scalar
            def _(act):
                chain = k.act_chain.on(act)
                act.dma_start(k.sq[:], d["square"][:, 0:NSQ_KEPT, :]).then_inc(small_in, 16)
                act.dma_start(flat(k.mod[:]), d["b_mod"][0:1, :].partition_broadcast(P).rearrange(
                    "p a n -> p (a n)")).then_inc(small_in, 16)
                act.dma_start(k.x[:], d["x"].rearrange("(t p) n -> p t n", p=P)).then_inc(x_in, 16)
                act.wait_ge(small_in, 48)
                act.activation(ccol[:, 0, :], col[:], ACT.Exp, scale=-1.0).then_inc(c_exp, 1)
                act.wait_ge(eps_set, 2)
                act.wait_ge(x_in, 16)
                for t in range(NT):
                    act.activation(k.proj[:, t, 0:D], k.x[:, t, :], ACT.Square,
                                   accum_out=sumsq[:, t:t + 1]).then_inc(sumsq_ready, 1)
                act.wait_ge(sumsq_ready, NT)
                act.activation(rstd[:], sumsq[:], ACT.Sqrt, scale=1.0 / D,
                               bias=k.eps[:, 0:1]).then_inc(root_ready, 1)
                for t in range(NT):
                    for half in range(2):
                        act.wait_ge(h_turned, 2 * t + half + 1)
                        act.activation(hT[:, 4 * half:4 * half + 4, t * P:(t + 1) * P],
                                       k.bank(2 + half).rearrange("p (a b) -> p a b", b=P),
                                       ACT.Copy).then_inc(hT_ready, 1)
                for j in range(7):
                    n = min(512, D_IN - j * 512)
                    for t in range(NT):
                        act.wait_ge(proj_ps, j * NT + t + 1)
                        act.activation(k.proj[:, t, j * 512:j * 512 + n], k.bank(4 + t)[:, 0:n],
                                       ACT.Copy).then_inc(proj_done, 1)

            @block.gpsimd
            def _(pool):
                for n in range(2):
                    pool.dma_start(gain[:, n, :], d[gains[n]][0:1, :].partition_broadcast(P).rearrange(
                        "p a n -> p (a n)")).then_inc(gain_in[n], 16)
                for n in range(2):
                    pool.wait_ge(gain_used, n + 1)
                    pool.dma_start(gain[:, n, :], d[gains[2 + n]][0:1, :].partition_broadcast(P).rearrange(
                        "p a n -> p (a n)")).then_inc(gain_in[n], 16)

            @block.tensor
            def _(pe):
                def mod_chunk(n, j):
                    pe.wait_ge(stage_in[n % 3], 16 * (n // 3 + 1))
                    if j >= 2:
                        pe.wait_ge(mod_done, j - 1)
                    for q in range(KT):
                        mm = pe.matmul(k.bank(j % 2), cb[:, q, :], stage[:, n % 3, q, :],
                                       start=(q == 0), stop=(q == KT - 1))
                    mm.then_inc(mod_ps, 1)
                    pe.wait_ge(mod_ps, j + 1)
                    pe.sem_inc(stage_used, 1)

                pe.wait_ge(c_ready, 1)
                pe.wait_ge(small_in, 48)
                for n in range(4):
                    mod_chunk(n, n)
                for t in range(NT):
                    pe.wait_ge(h_ready, t + 1)
                    if t:
                        pe.wait_ge(hT_ready, 2 * t)
                    for q in range(KT):
                        mm = pe.transpose(k.bank(2 + q // 4)[:, (q % 4) * P:(q % 4 + 1) * P],
                                          h[:, t % 2, q * P:(q + 1) * P], k.sq[:, IDENT, :])
                        if q % 4 == 3:
                            mm.then_inc(h_turned, 1)
                pe.wait_ge(hT_ready, 2 * NT)
                for n in range(4, 11):
                    j = n - 4
                    w = min(512, D_IN - j * 512)
                    pe.wait_ge(stage_in[n % 3], 16 * (n // 3 + 1))
                    for t in range(NT):
                        if j:
                            pe.wait_ge(proj_done, (j - 1) * NT + t + 1)
                        for q in range(KT):
                            mm = pe.matmul(k.bank(4 + t)[:, 0:w], hT[:, q, t * P:(t + 1) * P],
                                           stage[:, n % 3, q, 0:w], start=(q == 0), stop=(q == KT - 1))
                        mm.then_inc(proj_ps, 1)
                    pe.wait_ge(proj_ps, (j + 1) * NT)
                    pe.sem_inc(stage_used, 1)
                for n in range(11, 19):
                    mod_chunk(n, n - 7)

            @block.vector
            def _(dve):
                chain = k.dve_chain.on(dve)
                dve.memset(k.eps[:, 0:1], EPS).then_inc(eps_set, 1)
                dve.memset(k.eps[:, 1:2], GN_EPS).then_inc(eps_set, 1)
                dve.wait_ge(c_exp, 1)
                chain(dve.tensor_scalar(ccol[:, 1, :], ccol[:, 0, :], 1.0, None, ALU.add))
                chain(dve.reciprocal(ccol[:, 2, :], ccol[:, 1, :]))
                chain(dve.tensor_tensor(ccol[:, 1, :], ccol[:, 2, :], col[:], ALU.mult))
                dve.tensor_copy(cb[:], ccol[:, 1, :].unsqueeze(2).broadcast_to([P, KT, P])).then_inc(c_ready, 1)

                def mod_add(j):
                    dve.wait_ge(mod_ps, j + 1)
                    part = flat(k.mod[:])[:, j * 512:(j + 1) * 512]
                    dve.tensor_tensor(part, part, k.bank(j % 2), ALU.add).then_inc(mod_done, 1)

                for j in range(4):
                    mod_add(j)
                dve.wait_ge(mod_done, 4)
                dve.wait_ge(gain_in[0], 16)
                dve.scalar_tensor_tensor(k.mod[:, 1, :], k.mod[:, 1, :], 1.0, gain[:, 0, :],
                                         ALU.add, ALU.mult).then_inc(gain_used, 1)
                dve.wait_ge(root_ready, 1)
                chain(dve.reciprocal(rstd[:], rstd[:]))
                dve.wait_ge(gain_used, 1)
                for t in range(NT):
                    if t >= 2:
                        dve.wait_ge(h_turned, 2 * (t - 1))
                    chain(dve.scalar_tensor_tensor(h[:, t % 2, :], k.x[:, t, :], rstd[:, t:t + 1],
                                                   k.mod[:, 1, :], ALU.mult, ALU.mult))
                    dve.tensor_tensor(h[:, t % 2, :], h[:, t % 2, :], k.mod[:, 0, :],
                                      ALU.add).then_inc(h_ready, 1)
                for j in range(4, 12):
                    mod_add(j)
                    if j == 5:
                        dve.wait_ge(gain_in[1], 16)
                        dve.wait_ge(mod_done, 6)
                        dve.tensor_tensor(k.mod[:, 2, :], k.mod[:, 2, :], gain[:, 1, :],
                                          ALU.mult).then_inc(gain_used, 1)
                dve.wait_ge(mod_done, 12)
                dve.wait_ge(gain_in[0], 32)
                dve.scalar_tensor_tensor(k.mod[:, 4, :], k.mod[:, 4, :], 1.0, gain[:, 0, :],
                                         ALU.add, ALU.mult).then_inc(gain_used, 1)
                dve.wait_ge(gain_in[1], 32)
                dve.tensor_tensor(k.gate2[:], k.mod[:, 5, :], gain[:, 1, :], ALU.mult).then_inc(gain_used, 1)


def stage_mixers(k, front):
    k.cat = k.sb("cat", [P, NT, D], at=front)
    k.w_out = k.sb("w_out", [P, KT, D], at=front)
    k.w_out_in = k.sem("w_out_in")
    attention(k)
    linear_attention(k)


def attention(k):
    nc, d = k.nc, k.d
    half = DA // 2
    units = [(i, h) for i in range(NT) for h in range(HA)]
    NU = len(units)
    with ExitStack() as ctx:
        sb = lambda n, s, dt=F32: k.sb(n, s, dt, at=ctx)
        sem = k.stage_semaphores(ctx)
        log_count = sb("log_count", [P, NT, S])
        zeros = sb("zero_rows", [P, D])
        table = sb("rope_table", [P, NT, 2, 2, half])
        turned = sb("turned", [P, 2, 2 * HA, 2, half])
        cross = sb("cross", [P, 2, 2 * HA, half])
        qkT = sb("qkT", [P, 8, S])
        scores = sb("scores", [P, 2, S])
        probs = sb("probs", [P, 2, S])
        probsT = sb("probsT", [P, 2, S])
        negmax = sb("negmax", [P, NU])
        rowsum = sb("rowsum", [P, NU])
        inv = sb("inv", [P, NU])
        const_in = sem("attn_const_in")
        zeros_set = sem("zeros_set")
        zeros_out = sem("zeros_out")
        rope_done = sem("rope_done")
        turn_ps = sem("turn_ps")
        qkT_ready = sem("qkT_ready")
        scores_ps = sem("scores_ps")
        scores_masked = sem("scores_masked")
        probs_ready = sem("probs_ready")
        probsT_ps = sem("probsT_ps")
        probsT_ready = sem("probsT_ready")
        pv_done = sem("pv_done")
        cat_ready = sem("cat_ready")

        with nc.Block() as block:
            @block.sync
            def _(sp):
                sp.dma_start(table[:], d["rope"]).then_inc(const_in, 16)
                sp.dma_start(log_count[:], d["log_count"]).then_inc(const_in, 16)
                sp.wait_ge(zeros_set, 1)
                sp.dma_start(d["expert_rows"].rearrange("(b p) n -> p b n", p=P)[:, NE:, :],
                             zeros[:].unsqueeze(1).broadcast_to([P, EXTRA, D])).then_inc(zeros_out, 16)
                sp.dma_start(k.w_out[:], d["w_out"].rearrange("(k p) n -> p k n", p=P)).then_inc(k.w_out_in, 16)
                sp.wait_ge(zeros_out, 16)

            @block.vector
            def _(dve):
                chain = k.dve_chain.on(dve)
                dve.memset(zeros[:], 0.0).then_inc(zeros_set, 1)

                def finish_tile(dve, chain, i):
                    a, b = i * HA, (i + 1) * HA
                    dve.wait_ge(pv_done, b)
                    chain(dve.reciprocal(inv[:, a:b], rowsum[:, a:b]))
                    dve.tensor_tensor(k.cat[:, i, 0:HA * DA].rearrange("p (h n) -> p h n", h=HA),
                                      k.bank(6 + i % 2).rearrange("p (h n) -> p h n", h=HA),
                                      inv[:, a:b].unsqueeze(2).broadcast_to([P, HA, DA]),
                                      ALU.mult).then_inc(cat_ready, 1)

                dve.wait_ge(const_in, 32)
                for t in range(NT):
                    if t >= 2:
                        dve.wait_ge(turn_ps, 2 * (t - 1))
                    x = k.proj[:, t, 0:2 * HA * DA].rearrange("p (h two n) -> p h two n", two=2, n=half)
                    cs = [table[:, t, :, c, :].unsqueeze(2).broadcast_to([P, 2, HA, half]) for c in range(2)]
                    grouped = lambda ap: ap.rearrange("p (q h) n -> p q h n", q=2)
                    out = turned[:, t % 2]
                    dve.tensor_tensor(grouped(out[:, :, 0, :]), grouped(x[:, :, 0, :]), cs[0], ALU.mult)
                    dve.tensor_tensor(grouped(cross[:, 0]), grouped(x[:, :, 1, :]), cs[1], ALU.mult)
                    dve.tensor_tensor(grouped(out[:, :, 1, :]), grouped(x[:, :, 1, :]), cs[0], ALU.mult)
                    chain(dve.tensor_tensor(grouped(cross[:, 1]), grouped(x[:, :, 0, :]), cs[1], ALU.mult))
                    dve.tensor_tensor(out[:, :, 0, :], out[:, :, 0, :], cross[:, 0], ALU.subtract)
                    chain(dve.tensor_tensor(out[:, :, 1, :], out[:, :, 1, :], cross[:, 1], ALU.add))
                    dve.sem_inc(rope_done, 1)
                for u, (i, h) in enumerate(units):
                    n = (i + 1) * P
                    dve.wait_ge(scores_ps, u + 1)
                    if u >= 2:
                        dve.wait_ge(probs_ready, u - 1)
                    dve.tensor_tensor_reduce(scores[:, u % 2, 0:n], k.bank(2 + u % 2)[:, 0:n],
                                             log_count[:, i, 0:n], -1.0, 1e30, ALU.add, ALU.min,
                                             negmax[:, u:u + 1]).then_inc(scores_masked, 1)
                    if h == 1 and i:
                        finish_tile(dve, chain, i - 1)
                finish_tile(dve, chain, NT - 1)

            @block.scalar
            def _(act):
                for t in range(NT):
                    for part in range(2):
                        act.wait_ge(turn_ps, 2 * t + part + 1)
                        act.activation(qkT[:, 4 * part:4 * part + 4, t * P:(t + 1) * P],
                                       k.bank(part).rearrange("p (a b) -> p a b", b=P),
                                       ACT.Copy).then_inc(qkT_ready, 1)
                for u in range(NU + 1):
                    if u < NU:
                        n = (units[u][0] + 1) * P
                        act.wait_ge(scores_masked, u + 1)
                        if u >= 2:
                            act.wait_ge(probsT_ps, u - 1)
                        act.activation(probs[:, u % 2, 0:n], scores[:, u % 2, 0:n], ACT.Exp, scale=-1.0,
                                       bias=negmax[:, u:u + 1],
                                       accum_out=rowsum[:, u:u + 1]).then_inc(probs_ready, 1)
                    if u >= 1:
                        v = u - 1
                        n = (units[v][0] + 1) * P
                        act.wait_ge(probsT_ps, v + 1)
                        if v >= 2:
                            act.wait_ge(pv_done, v - 1)
                        act.activation(probsT[:, v % 2, 0:n], k.bank(4 + v % 2)[:, 0:n],
                                       ACT.Copy).then_inc(probsT_ready, 1)

            @block.tensor
            def _(pe):
                for t in range(NT):
                    pe.wait_ge(rope_done, t + 1)
                    for part in range(2):
                        if t:
                            pe.wait_ge(qkT_ready, 2 * (t - 1) + part + 1)
                        for q in range(4):
                            c = 4 * part + q
                            src = turned[:, t % 2].rearrange("p h two n -> p (h two n)")[:, c * P:(c + 1) * P]
                            mm = pe.transpose(k.bank(part)[:, q * P:(q + 1) * P], src, k.sq[:, IDENT, :])
                        mm.then_inc(turn_ps, 1)
                pe.wait_ge(qkT_ready, 2 * NT)
                for u in range(NU + 2):
                    if u < NU:
                        i, h = units[u]
                        r = (h % 2) * DA
                        if u >= 2:
                            pe.wait_ge(scores_masked, u - 1)
                        pe.matmul(k.bank(2 + u % 2)[:, 0:(i + 1) * P],
                                  qkT[r:r + DA, h // 2, i * P:(i + 1) * P],
                                  qkT[r:r + DA, 4 + h // 2, 0:(i + 1) * P],
                                  start=True, stop=True).then_inc(scores_ps, 1)
                    if 1 <= u <= NU:
                        v = u - 1
                        i = units[v][0]
                        pe.wait_ge(probs_ready, v + 1)
                        if v >= 2:
                            pe.wait_ge(probsT_ready, v - 1)
                        for j in range(i + 1):
                            mm = pe.transpose(k.bank(4 + v % 2)[:, j * P:(j + 1) * P],
                                              probs[:, v % 2, j * P:(j + 1) * P], k.sq[:, IDENT, :])
                        mm.then_inc(probsT_ps, 1)
                    if u >= 2:
                        v = u - 2
                        i, h = units[v]
                        pe.wait_ge(probsT_ready, v + 1)
                        if h == 0 and i >= 2:
                            pe.wait_ge(cat_ready, i - 1)
                        for j in range(i + 1):
                            mm = pe.matmul(k.bank(6 + i % 2)[:, h * DA:(h + 1) * DA],
                                           probsT[:, v % 2, j * P:(j + 1) * P],
                                           k.proj[:, j, VA + h * DA:VA + (h + 1) * DA],
                                           start=(j == 0), stop=(j == i))
                        mm.then_inc(pv_done, 1)


def linear_attention(k):
    nc, d = k.nc, k.d
    KW, VW = HG * DK, HG * DV
    NCH = S // CH
    with ExitStack() as ctx:
        sb = lambda n, s, dt=F32: k.sb(n, s, dt, at=ctx)
        sem = k.stage_semaphores(ctx)
        lrT = sb("lrT", [32, S])
        w_lr = sb("w_lr", [32, KW])
        g_gla = sb("g_gla", [P, DV])
        la = sb("la", [P, NT, KW])
        tmp = sb("gla_tmp", [P, NT * KW])
        grow = sb("grow", [P, 3, NT * KW])
        qd = sb("qd", [P, NT, KW])
        kd = sb("kd", [P, NT, KW])
        kl = sb("kl", [P, NT, KW])
        qkdT = sb("qkdT", [P, 4, S])
        decay = sb("decay", [P, 2, NCH])
        att = sb("gla_att", [P, 2, HG, P])
        state = sb("gla_state", [P, NCH, 2, DV])
        junk = sb("gla_junk", [P, DV])
        sumsq = sb("gla_sumsq", [P, NT * HG])
        rstd = sb("gla_rstd", [P, NT * HG])
        const_in = sem("gla_const_in")
        lr_set = sem("lr_set")
        lr_ps = sem("lr_ps")
        lr_ready = sem("lr_ready")
        logit_ps = sem("logit_ps")
        abs_ready = sem("abs_ready")
        log_ready = sem("log_ready")
        la_ready = sem("la_ready")
        cum_ps = sem("cum_ps")
        grow_ready = sem("grow_ready")
        qk_ready = sem("qk_ready")
        qkT_ps = sem("qkdT_ps")
        qkT_ready = sem("qkdT_ready")
        att_ps = sem("att_ps")
        att_ready = sem("att_ready")
        u_ps = sem("u_ps")
        state_ready = sem("state_ready")
        o_ps = sem("o_ps")
        o_read = sem("o_read")
        root_ready = sem("gla_root")
        silu_ready = sem("silu_ready")

        with nc.Block() as block:
            @block.sync
            def _(sp):
                sp.dma_start(w_lr[0:RANK + 1, :], d["w_gate_lr"]).then_inc(const_in, 16)
                sp.dma_start(g_gla[:], d["g_gla"][0:1, :].partition_broadcast(P).rearrange(
                    "p a n -> p (a n)")).then_inc(const_in, 16)

            @block.tensor
            def _(pe):
                for t in range(NT):
                    mm = pe.transpose(k.bank(0)[0:RANK, t * P:(t + 1) * P], k.proj[:, t, LR:LR + RANK],
                                      k.sq[:, IDENT, :])
                mm.then_inc(lr_ps, 1)
                pe.wait_ge(lr_ready, 1)
                pe.wait_ge(const_in, 32)
                for t in range(NT):
                    mm = pe.matmul(k.pp[1][:, t * KW:(t + 1) * KW], lrT[0:RANK + 1, t * P:(t + 1) * P],
                                   w_lr[0:RANK + 1, :], start=True, stop=True)
                mm.then_inc(logit_ps, 1)
                pe.wait_ge(la_ready, 1)
                for t in range(NT):
                    mm = pe.matmul(k.pp[0][:, t * KW:(t + 1) * KW], k.sq[:, CUM, :], la[:, t, :],
                                   start=True, stop=True)
                mm.then_inc(cum_ps, 1)
                for t in range(NT):
                    mm = pe.matmul(k.pp[2][:, t * KW:(t + 1) * KW], k.sq[:, SUF, :], la[:, t, :],
                                   start=True, stop=True)
                mm.then_inc(cum_ps, 1)
                for t in range(NT):
                    for p in range(2):
                        c = p * NCH + 2 * t
                        mm = pe.matmul(k.bank(6)[:, c:c + 2], la[:, t, p * P:(p + 1) * P],
                                       k.sq[:, BLOCK, 0:P:CH], start=True, stop=True)
                mm.then_inc(cum_ps, 1)
                for t in range(NT):
                    pe.wait_ge(qk_ready, 1)
                    if t >= 2:
                        pe.wait_ge(qkT_ready, t - 1)
                    for q in range(4):
                        src = (qd, kd)[q // 2][:, t, (q % 2) * P:(q % 2 + 1) * P]
                        mm = pe.transpose(k.bank(2 + t % 2)[:, q * P:(q + 1) * P], src, k.sq[:, IDENT, :])
                    mm.then_inc(qkT_ps, 1)
                for t in range(NT):
                    pe.wait_ge(qkT_ready, t + 1)
                    pe.wait_ge(grow_ready, 4)
                    if t:
                        pe.wait_ge(att_ready, 2 * t)
                    for h in range(HG):
                        r = (h % 2) * DK
                        mm = pe.matmul(k.bank(6 + h % 2)[:, h // 2 * P:(h // 2 + 1) * P],
                                       qkdT[r:r + DK, 2 + h // 2, t * P:(t + 1) * P],
                                       qkdT[r:r + DK, h // 2, t * P:(t + 1) * P], start=True, stop=True)
                    mm.then_inc(att_ps, 1)
                    if t:
                        pe.wait_ge(state_ready, 2 * t)
                    for c in range(2):
                        for h in range(HG):
                            r = c * CH
                            o = (h % 2) * DK
                            col = h // 2 * DV
                            mm = pe.matmul(k.bank(4 + c)[o:o + DK, col:col + DV],
                                           kl[r:r + CH, t, h * DK:(h + 1) * DK],
                                           k.proj[r:r + CH, t, VG + h * DV:VG + (h + 1) * DV],
                                           start=True, stop=True)
                    mm.then_inc(u_ps, 1)
                    pe.wait_ge(att_ready, 2 * (t + 1))
                    pe.wait_ge(state_ready, 2 * t + 1)
                    if t:
                        pe.wait_ge(o_read, t)
                    for h in range(HG):
                        out = k.bank(h % 2)[:, h // 2 * DV:(h // 2 + 1) * DV]
                        pe.matmul(out, att[:, t % 2, h, :],
                                  k.proj[:, t, VG + h * DV:VG + (h + 1) * DV], start=True, stop=True)
                        for c in range(2):
                            r = (h % 2) * DK
                            mm = pe.matmul(out[c * CH:(c + 1) * CH, :],
                                           qkdT[r:r + DK, h // 2, t * P + c * CH:t * P + (c + 1) * CH],
                                           state[r:r + DK, 2 * t + c, h // 2, :], start=False,
                                           stop=True, skip_group_check=True)
                    mm.then_inc(o_ps, 1)

            @block.scalar
            def _(act):
                chain = k.act_chain.on(act)
                act.wait_ge(lr_ps, 1)
                act.wait_ge(lr_set, 1)
                act.activation(lrT[0:RANK, :], k.bank(0)[0:RANK, :], ACT.Copy).then_inc(lr_ready, 1)
                act.wait_ge(abs_ready, 1)
                chain(act.activation(tmp[:], tmp[:], ACT.Exp))
                act.activation(tmp[:], tmp[:], ACT.Ln, bias=1.0).then_inc(log_ready, 1)
                act.wait_ge(cum_ps, 1)
                act.activation(grow[:, 0, :], k.pp[0][:, :], ACT.Exp).then_inc(grow_ready, 1)
                act.activation(grow[:, 1, :], k.pp[0][:, :], ACT.Exp, scale=-1.0).then_inc(grow_ready, 1)
                act.wait_ge(cum_ps, 2)
                act.activation(grow[:, 2, :], k.pp[2][:, :], ACT.Exp).then_inc(grow_ready, 1)
                act.wait_ge(cum_ps, 3)
                act.activation(decay[:], k.bank(6)[:, 0:2 * NCH].rearrange("p (a c) -> p a c", a=2), ACT.Exp,
                               scale=1.0 / 16).then_inc(grow_ready, 1)
                for t in range(NT):
                    act.wait_ge(qkT_ps, t + 1)
                    act.activation(qkdT[:, :, t * P:(t + 1) * P],
                                   k.bank(2 + t % 2).rearrange("p (a b) -> p a b", b=P),
                                   ACT.Copy).then_inc(qkT_ready, 1)
                for t in range(NT):
                    act.wait_ge(o_ps, t + 1)
                    for h in range(HG):
                        chain(act.activation(junk[:], k.bank(h % 2)[:, h // 2 * DV:(h // 2 + 1) * DV],
                                             ACT.Square, accum_out=sumsq[:, t * HG + h:t * HG + h + 1]))
                    for b in range(2):
                        ins = act.activation(
                            k.cat[:, t, VW:2 * VW].rearrange("p (h n) -> p h n", h=HG)[:, b::2, :],
                            k.bank(b)[:, 0:2 * DV].rearrange("p (h n) -> p h n", n=DV), ACT.Copy)
                    chain(ins)
                    act.sem_inc(o_read, 1)
                act.activation(rstd[:], sumsq[:], ACT.Sqrt, scale=1.0 / DV,
                               bias=k.eps[:, 0:1]).then_inc(root_ready, 1)
                for t in range(NT):
                    act.activation(k.proj[:, t, RG:RG + VW], k.proj[:, t, RG:RG + VW],
                                   ACT.Silu).then_inc(silu_ready, 1)

            @block.vector
            def _(dve):
                chain = k.dve_chain.on(dve)
                dve.memset(lrT[:], 1.0).then_inc(lr_set, 1)
                dve.memset(state[:, 0], 0.0)
                chain(dve.memset(att[:], 0.0))
                dve.wait_ge(logit_ps, 1)
                chain(dve.tensor_scalar(tmp[:], k.pp[1][:, :], -1.0, None, ALU.mult))
                dve.tensor_tensor(tmp[:], tmp[:], k.pp[1][:, :], ALU.min).then_inc(abs_ready, 1)
                dve.wait_ge(log_ready, 1)
                dve.scalar_tensor_tensor(flat(la[:]), k.pp[1][:, :], 0.0, tmp[:], ALU.min,
                                         ALU.subtract).then_inc(la_ready, 1)
                part = lambda n: grow[:, n, :].rearrange("p (t n) -> p t n", t=NT)
                dve.wait_ge(grow_ready, 1)
                dve.scalar_tensor_tensor(qd[:], k.proj[:, :, QG:QG + KW], DK ** -0.5, part(0),
                                         ALU.mult, ALU.mult)
                dve.wait_ge(grow_ready, 2)
                chain(dve.tensor_tensor(kd[:], k.proj[:, :, KG:KG + KW], part(1), ALU.mult))
                dve.wait_ge(grow_ready, 3)
                dve.tensor_tensor(kl[:], k.proj[:, :, KG:KG + KW], part(2), ALU.mult).then_inc(qk_ready, 1)
                mask = k.sq[:, LE, :].bitcast(U32).unsqueeze(1).broadcast_to([P, HG // 2, P])
                dve.wait_ge(grow_ready, 4)
                for t in range(NT):
                    dve.wait_ge(att_ps, t + 1)
                    if t >= 2:
                        dve.wait_ge(o_ps, t - 1)
                    for b in range(2):
                        dve.copy_predicated(att[:, t % 2, b::2, :], mask,
                                            k.bank(6 + b)[:, 0:2 * P].rearrange("p (a b) -> p a b", b=P)
                                            ).then_inc(att_ready, 1)
                    dve.wait_ge(u_ps, t + 1)
                    for c in range(2):
                        n = 2 * t + c
                        if n + 1 < NCH:
                            for p in range(2):
                                ins = dve.scalar_tensor_tensor(
                                    state[:, n + 1, p, :], state[:, n, p, :], decay[:, p, n:n + 1],
                                    k.bank(4 + c)[:, p * DV:(p + 1) * DV],
                                    ALU.mult, ALU.add)
                            chain(ins)
                            dve.sem_inc(state_ready, 1)
                dve.wait_ge(root_ready, 1)
                chain(dve.reciprocal(rstd[:], rstd[:]))
                for t in range(NT):
                    o = k.cat[:, t, VW:2 * VW].rearrange("p (h n) -> p h n", h=HG)
                    scale = rstd[:, t * HG:(t + 1) * HG].unsqueeze(2).broadcast_to([P, HG, DV])
                    gain = g_gla[:].unsqueeze(1).broadcast_to([P, HG, DV])
                    chain(dve.tensor_tensor(o, o, scale, ALU.mult))
                    chain(dve.tensor_tensor(o, o, gain, ALU.mult))
                    dve.wait_ge(silu_ready, t + 1)
                    chain(dve.tensor_tensor(k.cat[:, t, VW:2 * VW], k.cat[:, t, VW:2 * VW],
                                            k.proj[:, t, RG:RG + VW], ALU.mult))


def row(ap):
    return ap.partition_broadcast(P).rearrange("p a n -> p (a n)")


def stage_router(k, front):
    nc, d = k.nc, k.d
    with ExitStack() as ctx:
        sb = lambda n, s, dt=F32: k.sb(n, s, dt, at=ctx)
        sem = k.stage_semaphores(ctx)
        turned = sb("catT", [P, KT, S])
        h2 = sb("h2", [P, NT, D])
        scaled = sb("scaled", [P, D])
        junk = sb("router_junk", [P, D])
        sumsq = sb("router_sumsq", [P, 2, NT])
        rstd = sb("router_rstd", [P, 2, NT])
        w_router = sb("w_router", [P, KT, NE])
        b_router = sb("b_router", [P, NE])
        count = sb("count_const", [P, NBLK + 1])
        token = sb("token", [P, NT], I32)
        none = sb("none", [P, NBLK + 1], I32)
        logits = sb("logits", [P, NT, NE])
        top = sb("top", [P, NT, 8])
        index = sb("index", [P, NT, 8], U32)
        indexf = sb("indexf", [P, NT, 8])
        onehot = sb("onehot", [P, NT, TOPK, NE])
        work = sb("route_work", [P, NT, TOPK, NE])
        chosen = sb("chosen", [P, NT, NE])
        gate_e = sb("gate_e", [P, NT, NE])
        gsum = sb("gsum", [P, NT])
        rank = sb("rank", [P, NT, NE])
        ones = sb("ones_row", [P, NE])
        cnt = sb("cnt", [P, 3, NE])
        cmp = sb("cmp", [P, NBLK + 1, NE])
        destf = sb("destf", [P, 3, NT, TOPK])
        listed = sb("listed", [P, NT, TOPK], I32)
        plan = sb("plan", [P, TABLE])
        const_in = sem("router_const_in")
        cat_ps = sem("cat_ps")
        catT_ready = sem("catT_ready")
        y_ps = sem("y_ps")
        y_sumsq = sem("y_sumsq")
        x_ready = sem("resid_ready")
        x_sumsq = sem("x_sumsq")
        y_read = sem("y_read")
        h2_ready = sem("h2_ready")
        h2_out = sem("h2_out")
        h2_ps = sem("h2_ps")
        h2T_ready = sem("h2T_ready")
        logits_ps = sem("logits_ps")
        gate_diff = sem("gate_diff")
        gate_exp = sem("gate_exp")
        chosen_ready = sem("chosen_ready")
        rank_ps = sem("rank_ps")
        gateT_ps = sem("gateT_ps")
        none_set = sem("none_set")
        none_out = sem("none_out")
        dest_ready = sem("dest_ready")
        table_ready = sem("table_ready")
        lists_out = sem("lists_out")
        gateT_ready = sem("gateT_ready")

        with nc.Block() as block:
            @block.sync
            def _(sp):
                sp.dma_start(w_router[:], d["router_w"].rearrange("(k p) n -> p k n", p=P)).then_inc(const_in, 16)
                sp.dma_start(b_router[:], row(d["router_b"][0:1, :])).then_inc(const_in, 16)
                sp.dma_start(count[:], d["count"]).then_inc(const_in, 16)
                sp.dma_start(token[:], d["token"]).then_inc(const_in, 16)
                sp.wait_ge(none_set, 1)
                sp.dma_start(d["slot_token"].rearrange("(p n) one -> p (n one)", p=SLOTS),
                             none[:]).then_inc(none_out, 16)
                for t in range(NT):
                    sp.wait_ge(h2_ready, t + 1)
                    sp.dma_start(d["h2"][t * P:(t + 1) * P, :], h2[:, t, :]).then_inc(h2_out, 16)
                sp.wait_ge(h2_out, 16 * NT)

            @block.gpsimd
            def _(pool):
                pool.memset(none[:], 0).then_inc(none_set, 1)
                pool.wait_ge(none_out, 16)
                pool.wait_ge(const_in, 64)
                pool.wait_ge(dest_ready, 1)
                for t in range(NT):
                    for c in range(TOPK):
                        pool.indirect_dma_start(
                            out=d["slot_token"],
                            out_offset=bass.IndirectOffsetOnAxis(ap=listed[:, t, c:c + 1], axis=0),
                            in_=token[:, t:t + 1], in_offset=None).then_inc(lists_out, 16)
                pool.wait_ge(lists_out, 16 * NT * TOPK)

            @block.tensor
            def _(pe):
                ident = k.sq[:, IDENT, :]

                def turn_and_project(t):
                    if t:
                        pe.wait_ge(catT_ready, 2 * t)
                    for q in range(KT):
                        mm = pe.transpose(k.bank(q // 4)[:, (q % 4) * P:(q % 4 + 1) * P],
                                          k.cat[:, t, q * P:(q + 1) * P], ident)
                        if q % 4 == 3:
                            mm.then_inc(cat_ps, 1)
                    pe.wait_ge(catT_ready, 2 * (t + 1))
                    if t >= 2:
                        pe.wait_ge(y_read, t - 1)
                    for n in range(2):
                        for q in range(KT):
                            mm = pe.matmul(k.pp[1 + t % 2][:, n * 512:(n + 1) * 512],
                                           turned[:, q, t * P:(t + 1) * P],
                                           k.w_out[:, q, n * 512:(n + 1) * 512],
                                           start=(q == 0), stop=(q == KT - 1))
                    mm.then_inc(y_ps, 1)

                def turn_h2(t):
                    pe.wait_ge(h2_ready, t + 1)
                    if t:
                        pe.wait_ge(h2T_ready, 2 * t)
                    for q in range(KT):
                        mm = pe.transpose(k.bank(6 + q // 4)[:, (q % 4) * P:(q % 4 + 1) * P],
                                          h2[:, t, q * P:(q + 1) * P], ident)
                        if q % 4 == 3:
                            mm.then_inc(h2_ps, 1)

                pe.wait_ge(k.w_out_in, 16)
                turn_and_project(0)
                for t in range(1, NT):
                    turn_and_project(t)
                    turn_h2(t - 1)
                turn_h2(NT - 1)
                pe.wait_ge(h2T_ready, 2 * NT)
                pe.wait_ge(const_in, 64)
                for t in range(NT):
                    for q in range(KT):
                        mm = pe.matmul(k.bank(0)[:, t * NE:(t + 1) * NE], turned[:, q, t * P:(t + 1) * P],
                                       w_router[:, q, :], start=(q == 0), stop=(q == KT - 1))
                mm.then_inc(logits_ps, 1)
                pe.wait_ge(chosen_ready, 1)
                for t in range(NT):
                    for s in range(t + 1):
                        pe.matmul(k.bank(1)[:, t * NE:(t + 1) * NE],
                                  k.sq[:, BEFORE if s == t else ONES, :], chosen[:, s, :],
                                  start=(s == 0), stop=(s == t))
                for s in range(NT):
                    mm = pe.matmul(k.bank(1)[:, NT * NE:(NT + 1) * NE], k.sq[:, ONES, :], chosen[:, s, :],
                                   start=(s == 0), stop=(s == NT - 1))
                mm.then_inc(rank_ps, 1)
                pe.wait_ge(gateT_ready, 1)
                for t in range(NT):
                    mm = pe.transpose(k.bank(2)[0:NE, t * P:(t + 1) * P], gate_e[:, t, :], ident)
                mm.then_inc(gateT_ps, 1)

            @block.scalar
            def _(act):
                def root(part, t):
                    chain(act.activation(rstd[:, part, t:t + 1], sumsq[:, part, t:t + 1], ACT.Sqrt,
                                         scale=1.0 / D, bias=k.eps[:, 0:1]))

                def evac(bank0, ps, ready, t):
                    for part in range(2):
                        act.wait_ge(ps, 2 * t + part + 1)
                        act.activation(turned[:, 4 * part:4 * part + 4, t * P:(t + 1) * P],
                                       k.bank(bank0 + part).rearrange("p (a b) -> p a b", b=P),
                                       ACT.Copy).then_inc(ready, 1)

                chain = k.act_chain.on(act)
                for t in range(NT + 1):
                    if t < NT:
                        evac(0, cat_ps, catT_ready, t)
                    if t < NT:
                        act.wait_ge(y_ps, t + 1)
                        chain(act.activation(junk[:], k.pp[1 + t % 2][:, :], ACT.Square,
                                             accum_out=sumsq[:, 0, t:t + 1]))
                        root(0, t)
                        act.sem_inc(y_sumsq, 1)
                        act.wait_ge(x_ready, t + 1)
                        chain(act.activation(junk[:], k.x[:, t, :], ACT.Square,
                                             accum_out=sumsq[:, 1, t:t + 1]))
                        root(1, t)
                        act.sem_inc(x_sumsq, 1)
                    if t:
                        evac(6, h2_ps, h2T_ready, t - 1)
                act.wait_ge(gate_diff, 1)
                act.activation(k.gates[:], k.gates[:], ACT.Exp).then_inc(gate_exp, 1)
                act.wait_ge(gateT_ps, 1)
                act.activation(k.gateT[:], k.bank(2)[0:NE, :], ACT.Copy)

            @block.vector
            def _(dve):
                chain = k.dve_chain.on(dve)
                for t in range(NT):
                    dve.wait_ge(y_sumsq, t + 1)
                    chain(dve.reciprocal(rstd[:, 0, t:t + 1], rstd[:, 0, t:t + 1]))
                    chain(dve.scalar_tensor_tensor(scaled[:], k.pp[1 + t % 2][:, :], rstd[:, 0, t:t + 1],
                                                   k.mod[:, 2, :], ALU.mult, ALU.mult))
                    dve.sem_inc(y_read, 1)
                    dve.tensor_tensor(k.x[:, t, :], k.x[:, t, :], scaled[:], ALU.add).then_inc(x_ready, 1)
                    dve.wait_ge(x_sumsq, t + 1)
                    chain(dve.reciprocal(rstd[:, 1, t:t + 1], rstd[:, 1, t:t + 1]))
                    chain(dve.scalar_tensor_tensor(h2[:, t, :], k.x[:, t, :], rstd[:, 1, t:t + 1],
                                                   k.mod[:, 4, :], ALU.mult, ALU.mult))
                    dve.tensor_tensor(h2[:, t, :], h2[:, t, :], k.mod[:, 3, :], ALU.add).then_inc(h2_ready, 1)
                dve.wait_ge(const_in, 64)
                dve.wait_ge(logits_ps, 1)
                over_t = lambda ap, n=NT: ap.unsqueeze(1).broadcast_to([P, n, NE])
                chain(dve.tensor_tensor(logits[:], k.bank(0)[:, 0:NT * NE].rearrange("p (t e) -> p t e", e=NE),
                                        over_t(b_router[:]), ALU.add))
                for t in range(NT):
                    ins = dve.max(top[:, t, :], logits[:, t, :])
                chain(ins)
                for t in range(NT):
                    ins = dve.max_index(index[:, t, :], top[:, t, :], logits[:, t, :])
                chain(ins)
                chain(dve.tensor_copy(indexf[:], index[:]))
                for t in range(NT):
                    ins = dve.tensor_tensor(onehot[:, t], over_t(count[:, 0:NE], TOPK),
                                            indexf[:, t, 0:TOPK].unsqueeze(2).broadcast_to([P, TOPK, NE]),
                                            ALU.is_equal)
                dve.tensor_tensor(k.gates[:], top[:, :, 0:TOPK], top[:, :, 0:1].broadcast_to([P, NT, TOPK]),
                                  ALU.subtract).then_inc(gate_diff, 1)
                chain(dve.memset(ones[:], 1.0))
                for t in range(NT):
                    ins = dve.tensor_reduce(chosen[:, t, :], onehot[:, t].rearrange("p c e -> p e c"), AX.X,
                                            ALU.add)
                ins.then_inc(chosen_ready, 1)
                dve.wait_ge(gate_exp, 1)
                chain(dve.tensor_reduce(gsum[:], k.gates[:], AX.X, ALU.add))
                chain(dve.reciprocal(gsum[:], gsum[:]))
                chain(dve.tensor_tensor(k.gates[:], k.gates[:],
                                        gsum[:].unsqueeze(2).broadcast_to([P, NT, TOPK]), ALU.mult))
                for t in range(NT):
                    ins = dve.tensor_tensor(work[:, t], onehot[:, t],
                                            k.gates[:, t, :].unsqueeze(2).broadcast_to([P, TOPK, NE]), ALU.mult)
                chain(ins)
                for t in range(NT):
                    ins = dve.tensor_reduce(gate_e[:, t, :], work[:, t].rearrange("p c e -> p e c"), AX.X,
                                            ALU.add)
                ins.then_inc(gateT_ready, 1)
                dve.wait_ge(rank_ps, 1)
                dve.tensor_copy(rank[:], k.bank(1)[:, 0:NT * NE].rearrange("p (t e) -> p t e", e=NE))
                total = k.bank(1)[:, NT * NE:(NT + 1) * NE]
                chain(dve.tensor_scalar(cnt[:, 0, :], total, 0.0, None, ALU.is_gt))
                for j in range(1, -(-S // SLOTS)):
                    chain(dve.scalar_tensor_tensor(cnt[:, 0, :], total, float(SLOTS * j), cnt[:, 0, :],
                                                   ALU.is_gt, ALU.add))
                chain(dve.tensor_tensor_scan(cnt[:, 1, :], ones[:], cnt[:, 0, :], 0.0, ALU.mult, ALU.add))
                chain(dve.tensor_tensor(cnt[:, 2, :], cnt[:, 1, :], cnt[:, 0, :], ALU.subtract))
                for part, of_expert in enumerate((lambda t: rank[:, t, :], lambda t: cnt[:, 2, :])):
                    for t in range(NT):
                        ins = dve.tensor_tensor(work[:, t], onehot[:, t], over_t(of_expert(t), TOPK), ALU.mult)
                    chain(ins)
                    for t in range(NT):
                        ins = dve.tensor_reduce(destf[:, part, t, :], work[:, t], AX.X, ALU.add)
                    chain(ins)
                chain(dve.tensor_scalar(destf[:, 2], destf[:, 0], float(SLOTS), None, ALU.is_ge))
                for j in range(2, -(-S // SLOTS)):
                    chain(dve.scalar_tensor_tensor(destf[:, 2], destf[:, 0], float(SLOTS * j), destf[:, 2],
                                                   ALU.is_ge, ALU.add))
                chain(dve.scalar_tensor_tensor(destf[:, 0], destf[:, 2], -float(SLOTS), destf[:, 0],
                                               ALU.mult, ALU.add))
                chain(dve.tensor_tensor(destf[:, 1], destf[:, 1], destf[:, 2], ALU.add))
                chain(dve.scalar_tensor_tensor(listed[:], destf[:, 0], float(NBLK + 1), destf[:, 1],
                                               ALU.mult, ALU.add))
                dve.sem_inc(dest_ready, 1)
                dve.scalar_tensor_tensor(k.dest[:], destf[:, 1], float(SLOTS), destf[:, 0], ALU.mult, ALU.add)
                many = NBLK + 1
                chain(dve.tensor_tensor(cmp[:], cnt[:, 1, :].unsqueeze(1).broadcast_to([P, many, NE]),
                                        count[:].unsqueeze(2).broadcast_to([P, many, NE]), ALU.is_le))
                chain(dve.tensor_reduce(plan[:, 0:many], cmp[:], AX.X, ALU.add))
                chain(dve.tensor_scalar(plan[:, 0:many], plan[:, 0:many], float(NE - 1), None, ALU.min))
                dve.memset(plan[:, many:many + 1], 1.0)
                chain(dve.tensor_tensor(plan[:, many + 1:2 * many], plan[:, 1:many], plan[:, 0:many - 1],
                                        ALU.not_equal))
                chain(dve.tensor_scalar(plan[:, 2 * many:3 * many], plan[:, many:2 * many], 0.0, None,
                                        ALU.is_equal))
                chain(dve.tensor_scalar(plan[:, TABLE - 1:TABLE], cnt[:, 1, NE - 1:NE], float(NE), None,
                                        ALU.max))
                chain(dve.tensor_scalar(plan[:, TABLE - 2:TABLE - 1], plan[:, TABLE - 1:TABLE], -1.0, None,
                                        ALU.add))
                chain(dve.tensor_copy(k.table[:], plan[0:1, :]))


def stage_experts(k):
    nc, d = k.nc, k.d
    UP = 2 * P
    HALF = KT // 2 * UP
    with ExitStack() as ctx:
        sb = lambda n, s, dt=F32: k.sb(n, s, dt, at=ctx)
        sem = k.stage_semaphores(ctx)
        wgu = sb("wgu", [P, NM, KT * UP])
        wd = sb("wd", [P, NM, D])
        wgu_hi = sb("wgu_hi", [P, 2, KT * UP], F32R)
        wgu_lo = sb("wgu_lo", [P, 2, KT * UP], F32R)
        wd_hi = sb("wd_hi", [P, 2, D], F32R)
        wd_lo = sb("wd_lo", [P, 2, D], F32R)
        bias = sb("bias", [P, NM * UP], F32R)
        picked = sb("picked", [P, 1])
        pick = sb("pick", [P, P], F32R)
        slots = sb("slots", [SLOTS, NBLK + 1], I32)
        slot = sb("slot", [P, 1], I32)
        rows = sb("rows", [P, D])
        rowsT = sb("rowsT", [P, 2, KT, P], F32R)
        glu = sb("glu", [P, 2, P])
        lin = sb("lin", [P, 2, P])
        prod = sb("prod", [P, 2, P])
        sig = sb("sig", [P, 2, P])
        hidden = sb("hidden", [P, 2, P])
        hT = sb("hiddenT", [P, 2, 2, P], F32R)
        y = sb("y_rows", [P, D])
        gu_in = [sem(f"gu_in{m}") for m in range(NM)]
        wd_in = [sem(f"wd_in{m}") for m in range(NM)]
        bias_in = sem("bias_in")
        bias_high = sem("bias_high")
        bias_ready = sem("bias_ready")
        slab_free = sem("slab_free")
        picked_in = sem("picked_in")
        pick_ready = sem("pick_ready")
        slots_in = sem("slots_in")
        slot_ready = sem("slot_ready")
        slot_seen = sem("slot_seen")
        rows_in = sem("rows_in")
        rows_ps = sem("rows_ps")
        rowsT_high = sem("rowsT_high")
        rowsT_ready = sem("rowsT_ready")
        gu_high = sem("gu_high")
        gu_ready = sem("gu_ready")
        wd_high = sem("wd_high")
        wd_ready = sem("wd_ready")
        half_up_ps = sem("half_up_ps")
        up_ps = sem("up_ps")
        up_read = sem("up_read")
        glu_ready = sem("glu_ready")
        sig_ready = sem("sig_ready")
        prod_ready = sem("prod_ready")
        hidden_ready = sem("hidden_ready")
        hiddenT_ps = sem("hiddenT_ps")
        hiddenT_high = sem("hiddenT_high")
        hiddenT_ready = sem("hiddenT_ready")
        down_ps = sem("down_ps")
        y_read = sem("expert_y_read")
        y_out = sem("expert_y_out")
        f = lambda ap: ap.bitcast(F32)
        raw_bias = wgu[:, NM - 1, :]

        def blocks_on(eng):
            return eng.value_load(k.table[0:1, TABLE - 1:TABLE], min_val=NE, max_val=NBLK)

        def last_on(eng):
            return eng.value_load(k.table[0:1, TABLE - 2:TABLE - 1], min_val=NE - 1, max_val=NBLK - 1)

        def after(eng, sem, n):
            if not isinstance(n, int) or n > 0:
                eng.wait_ge(sem, n)

        def begun(g):
            return not isinstance(g, int) or g >= 0

        with nc.Block() as block:
            @block.sync
            def _(sp):
                def load_picked(i, e):
                    after(sp, pick_ready, i)
                    sp.dma_start(picked[:], d["picked"][bass.ds(e * P, P), :]).then_inc(picked_in, 16)

                def slabs(i, load_gu, load_wd, store=False):
                    for m in range(NM + 1):
                        if m == NM - 1 and isinstance(i, int) and i == 0:
                            sp.wait_ge(bias_ready, 2)
                        if m < NM:
                            after(sp, gu_ready, 2 * (NM * (i - 1) + m + 1))
                            sp.sem_inc(slab_free, 1)
                            after(sp, gu_in[(m - 3) % NM], 16 * (i + (m >= 3)))
                            load_gu(m)
                        if m == 4 and store:
                            store_rows(i - 1)
                        if m:
                            after(sp, wd_ready, NM * (i - 1) + m)
                            load_wd(m - 1)

                def store_rows(n):
                    sp.wait_ge(y_read, n)
                    sp.dma_start(d["expert_rows"][bass.ds(n * SLOTS - SLOTS, SLOTS), :], y[:]).then_inc(y_out, 16)

                def load(i, e, store=True):
                    rows_of = lambda m: bass.ds((e * NM + m) * P, P)
                    slabs(i, lambda m: sp.dma_start(wgu[:, m, :], d["w_gate_up"][rows_of(m), :]
                                                    ).then_inc(gu_in[m], 16),
                          lambda m: sp.dma_start(wd[:, m, :], d["w_down"][rows_of(m), :]
                                                 ).then_inc(wd_in[m], 16), store)

                def expert(i):
                    return sp.value_load(k.table[0:1, bass.ds(i, 1)], min_val=0, max_val=NE - 1)

                sp.dma_start(slots[:], d["slot_token"].rearrange("(p n) one -> p (n one)", p=SLOTS)
                             ).then_inc(slots_in, 16)
                for part in range(2):
                    sp.dma_start(raw_bias[part * NE:(part + 1) * NE, :], d["b_gate_up"]).then_inc(bias_in, 16)
                blocks = blocks_on(sp)
                for i in range(2):
                    e = expert(i)
                    load_picked(i, e)
                    load(i, e, False)
                with sp.Fori(2, blocks) as i:
                    e = expert(i)
                    other = sp.value_load(k.table[0:1, bass.ds(i + (NBLK + 1), 1)], min_val=0, max_val=1)
                    same = sp.value_load(k.table[0:1, bass.ds(i + 2 * (NBLK + 1), 1)], min_val=0, max_val=1)
                    load_picked(i, e)
                    with sp.If(other > 0):
                        load(i, e)
                    with sp.If(same > 0):
                        slabs(i, lambda m: sp.sem_inc(gu_in[m], 16), lambda m: sp.sem_inc(wd_in[m], 16), True)
                load_picked(blocks, NE - 1)
                last = last_on(sp)
                sp.wait_ge(gu_ready, 2 * NM * last + 2)
                sp.sem_inc(gu_in[0], 16)
                store_rows(last)
                store_rows(last + 1)

            @block.gpsimd
            def _(pool):
                blocks = blocks_on(pool)

                def gather(i):
                    after(pool, rows_in, 16 * i)
                    pool.tensor_copy(slot[:], slots[:, bass.ds(i, 1)]).then_inc(slot_ready, 1)
                    after(pool, rows_ps, 2 * i)
                    pool.wait_ge(slot_ready, i + 1)
                    pool.sem_inc(slot_seen, 1)
                    pool.indirect_dma_start(
                        out=rows[:], out_offset=None, in_=d["h2"],
                        in_offset=bass.IndirectOffsetOnAxis(ap=slot[:, 0:1], axis=0)).then_inc(rows_in, 16)

                def split_wd(g, m):
                    if begun(g):
                        pool.wait_ge(wd_high, g + 1)
                        pool.tensor_tensor(wd_lo[:, m % 2, :], wd[:, m, :], f(wd_hi[:, m % 2, :]),
                                           ALU.subtract).then_inc(wd_ready, 1)

                def steps(i):
                    for m in range(NM):
                        split_wd(NM * i + m - 1, (m - 1) % NM)
                        if m == 0:
                            gather(i + 1)

                pool.wait_ge(slots_in, 16)
                gather(0)
                steps(0)
                with pool.Fori(1, blocks) as i:
                    steps(i)
                split_wd(NM * last_on(pool) + (NM - 1), NM - 1)
                pool.wait_ge(rows_in, 16 * blocks + 16)
                pool.wait_ge(picked_in, 16 * blocks + 16)
                pool.wait_ge(y_out, 16 * blocks + 16)

            @block.tensor
            def _(pe):
                blocks = blocks_on(pe)

                def turn_rows(i):
                    pe.wait_ge(rows_in, 16 * i + 16)
                    for q in range(KT):
                        mm = pe.transpose(k.bank(6 + q // 4)[:, (q % 4) * P:(q % 4 + 1) * P],
                                          rows[:, q * P:(q + 1) * P], k.sq[:, IDENT, :])
                        if q % 4 == 3:
                            mm.then_inc(rows_ps, 1)

                def up(g, m, i):
                    after(pe, up_read, g - 1)
                    out = k.bank(m % 2)[:, 0:UP]
                    pe.matmul(out, pick[:], bias[:, m * UP:(m + 1) * UP], start=True, stop=False)
                    for q in range(KT):
                        if q % (KT // 2) == 0:
                            pe.wait_ge(gu_ready, 2 * g + 1 + q // (KT // 2))
                            if m == 0:
                                pe.wait_ge(rowsT_ready, 2 * i + 1 + q // (KT // 2))
                        hi, lo = (w[:, m % 2, q * UP:(q + 1) * UP] for w in (wgu_hi, wgu_lo))
                        pe.matmul(out, rowsT[:, 0, q, :], hi, start=False, stop=False)
                        pe.matmul(out, rowsT[:, 0, q, :], lo, start=False, stop=False)
                        mm = pe.matmul(out, rowsT[:, 1, q, :], hi, start=False, stop=(q == KT - 1))
                        if q == KT // 2 - 1:
                            mm.then_inc(half_up_ps, 1)
                    mm.then_inc(up_ps, 1)

                def turn_hidden(g, m):
                    if begun(g):
                        pe.wait_ge(hidden_ready, g + 1)
                        after(pe, hiddenT_ready, g - 1)
                        pe.transpose(k.bank(2 + m % 2)[:, 0:P], hidden[:, m % 2, :],
                                     k.sq[:, IDENT, :]).then_inc(hiddenT_ps, 1)

                def down(g, m, i):
                    if begun(g):
                        pe.wait_ge(hiddenT_ready, g + 1)
                        pe.wait_ge(wd_ready, g + 1)
                        if m == 0:
                            after(pe, y_read, i)
                        for a, w in ((0, wd_hi), (0, wd_lo), (1, wd_hi)):
                            for n in range(2):
                                mm = pe.matmul(k.bank(4 + n), hT[:, m % 2, a, :],
                                               w[:, m % 2, n * 512:(n + 1) * 512],
                                               start=(m == 0 and a == 0 and w is wd_hi),
                                               stop=(m == NM - 1 and a == 1))
                        mm.then_inc(down_ps, 1)

                def steps(i):
                    pe.wait_ge(pick_ready, i + 1)
                    for m in range(NM):
                        g = NM * i + m
                        if m == NM - 1:
                            turn_rows(i + 1)
                        up(g, m, i)
                        turn_hidden(g - 1, (m - 1) % NM)
                        down(g - 2, (m - 2) % NM, i)

                turn_rows(0)
                pe.wait_ge(bias_ready, 2)
                steps(0)
                with pe.Fori(1, blocks) as i:
                    steps(i)
                last = NM * last_on(pe)
                turn_hidden(last + (NM - 1), NM - 1)
                down(last + (NM - 2), NM - 2, blocks)
                down(last + (NM - 1), NM - 1, blocks)

            @block.scalar
            def _(act):
                blocks = blocks_on(act)

                def sigmoid(g, m):
                    if begun(g):
                        act.wait_ge(glu_ready, g + 1)
                        after(act, hidden_ready, g - 1)
                        act.activation(sig[:, m % 2, :], glu[:, m % 2, :], ACT.Sigmoid,
                                       scale=ALPHA).then_inc(sig_ready, 1)

                def gu_highs(g, m, i):
                    act.wait_ge(gu_in[m], 16 * i + 16)
                    after(act, up_ps, g - 1)
                    for h in range(2):
                        act.activation(wgu_hi[:, m % 2, h * HALF:(h + 1) * HALF],
                                       wgu[:, m, h * HALF:(h + 1) * HALF], ACT.Copy).then_inc(gu_high, 1)

                def wd_highs(g, m, i):
                    if begun(g):
                        act.wait_ge(wd_in[m], 16 * i + 16)
                        after(act, down_ps, g - 1)
                        act.activation(wd_hi[:, m % 2, :], wd[:, m, :], ACT.Copy).then_inc(wd_high, 1)

                def row_highs(i, g=None):
                    for part in range(2):
                        if g is not None:
                            act.wait_ge(up_ps if part else half_up_ps, g + 1)
                        act.wait_ge(rows_ps, 2 * i + part + 1)
                        act.activation(rowsT[:, 0, 4 * part:4 * part + 4, :],
                                       k.bank(6 + part).rearrange("p (a b) -> p a b", b=P),
                                       ACT.Copy).then_inc(rowsT_high, 1)

                def hidden_high(g, m):
                    if begun(g):
                        act.wait_ge(hiddenT_ps, g + 1)
                        after(act, down_ps, g - 1)
                        act.activation(hT[:, m % 2, 0, :], k.bank(2 + m % 2)[:, 0:P],
                                       ACT.Copy).then_inc(hiddenT_high, 1)

                def read_y(i):
                    act.wait_ge(down_ps, NM * i + NM)
                    act.wait_ge(y_out, 16 * i + 16)
                    act.activation(y[:], k.pp[2][:, :], ACT.Copy).then_inc(y_read, 1)

                def steps(i):
                    for m in range(NM):
                        g = NM * i + m
                        before = (m - 1) % NM
                        sigmoid(g - 1, before)
                        if m == 2 and begun(i - 1):
                            read_y(i - 1)
                        gu_highs(g + 1, (m + 1) % NM, i + (m == NM - 1))
                        wd_highs(g - 1, before, i - (m == 0))
                        if m == NM - 1:
                            row_highs(i + 1, g)
                        hidden_high(g - 1, before)

                act.sem_inc(y_out, 16)
                act.wait_ge(bias_in, 32)
                act.wait_ge(bias_ready, 1)
                act.activation(bias[:], raw_bias, ACT.Copy).then_inc(bias_high, 1)
                gu_highs(0, 0, 0)
                row_highs(0)
                steps(0)
                with act.Fori(1, blocks) as i:
                    steps(i)
                last = last_on(act)
                end = NM * last + (NM - 1)
                sigmoid(end, NM - 1)
                wd_highs(end, NM - 1, last)
                hidden_high(end, NM - 1)
                read_y(last)

            @block.vector
            def _(dve):
                blocks = blocks_on(dve)

                def activate(g, m):
                    if begun(g):
                        dve.wait_ge(up_ps, g + 1)
                        dve.tensor_scalar(glu[:, m % 2, :], k.bank(m % 2)[:, 0:P], LIMIT, None,
                                          ALU.min).then_inc(glu_ready, 1)
                        dve.tensor_scalar(lin[:, m % 2, :], k.bank(m % 2)[:, P:UP], LIMIT, -LIMIT,
                                          ALU.min, ALU.max).then_inc(up_read, 1)
                        dve.wait_ge(glu_ready, g + 1)
                        dve.wait_ge(up_read, g + 1)
                        dve.scalar_tensor_tensor(prod[:, m % 2, :], lin[:, m % 2, :], 1.0,
                                                 glu[:, m % 2, :], ALU.add, ALU.mult).then_inc(prod_ready, 1)

                def finish_hidden(g, m):
                    if begun(g):
                        dve.wait_ge(prod_ready, g + 1)
                        dve.wait_ge(sig_ready, g + 1)
                        dve.tensor_tensor(hidden[:, m % 2, :], prod[:, m % 2, :], sig[:, m % 2, :],
                                          ALU.mult).then_inc(hidden_ready, 1)

                def gu_lows(g, m, h):
                    dve.wait_ge(gu_high, 2 * g + h + 1)
                    part = slice(h * HALF, (h + 1) * HALF)
                    dve.tensor_tensor(wgu_lo[:, m % 2, part], wgu[:, m, part], f(wgu_hi[:, m % 2, part]),
                                      ALU.subtract).then_inc(gu_ready, 1)

                def row_lows(i):
                    for part in range(2):
                        dve.wait_ge(rowsT_high, 2 * i + part + 1)
                        four = slice(4 * part, 4 * part + 4)
                        dve.tensor_tensor(rowsT[:, 1, four, :], k.bank(6 + part).rearrange(
                            "p (a b) -> p a b", b=P), f(rowsT[:, 0, four, :]),
                            ALU.subtract).then_inc(rowsT_ready, 1)

                def hidden_low(g, m):
                    if begun(g):
                        dve.wait_ge(hiddenT_high, g + 1)
                        dve.tensor_tensor(hT[:, m % 2, 1, :], k.bank(2 + m % 2)[:, 0:P],
                                          f(hT[:, m % 2, 0, :]), ALU.subtract).then_inc(hiddenT_ready, 1)

                def pick_expert(i):
                    dve.wait_ge(picked_in, 16 * i + 16)
                    dve.tensor_copy(pick[:], picked[:].broadcast_to([P, P])).then_inc(pick_ready, 1)

                def steps(i):
                    for m in range(NM):
                        g = NM * i + m
                        before = (m - 1) % NM
                        activate(g - 1, before)
                        finish_hidden(g - 1, before)
                        gu_lows(g + 1, (m + 1) % NM, 0)
                        gu_lows(g + 1, (m + 1) % NM, 1)
                        if m == NM - 1:
                            row_lows(i + 1)
                            dve.wait_ge(up_ps, g + 1)
                            pick_expert(i + 1)
                        hidden_low(g - 1, before)

                dve.memset(raw_bias[2 * NE:P, :], 0.0).then_inc(bias_ready, 1)
                dve.wait_ge(bias_high, 1)
                low = slice(NE, 2 * NE)
                dve.tensor_tensor(bias[low, :], raw_bias[low, :], f(bias[low, :]), ALU.subtract
                                  ).then_inc(bias_ready, 1)
                gu_lows(0, 0, 0)
                gu_lows(0, 0, 1)
                pick_expert(0)
                row_lows(0)
                steps(0)
                with dve.Fori(1, blocks) as i:
                    steps(i)
                last = NM * last_on(dve) + (NM - 1)
                activate(last, NM - 1)
                finish_hidden(last, NM - 1)
                hidden_low(last, NM - 1)


def stage_combine(k):
    nc, d = k.nc, k.d
    with ExitStack() as ctx:
        sb = lambda n, s, dt=F32: k.sb(n, s, dt, at=ctx)
        sem = k.stage_semaphores(ctx)
        choice = sb("choice", [P, NT, TOPK, D])
        b_down = sb("b_down", [NE, D])
        acc = sb("acc", [P, 2, D])
        junk = sb("combine_junk", [P, D])
        sumsq = sb("combine_sumsq", [P, NT])
        rstd = sb("combine_rstd", [P, NT])
        b_in = sem("b_down_in")
        choice_in = [sem(f"choice_in{t}") for t in range(NT)]
        bias_ps = sem("bias_ps")
        bias_read = sem("bias_read")
        acc_ready = sem("acc_ready")
        acc_sumsq = sem("acc_sumsq")

        with nc.Block() as block:
            @block.sync
            def _(sp):
                sp.dma_start(b_down[:], d["b_down"]).then_inc(b_in, 16)

            @block.gpsimd
            def _(pool):
                for t in range(NT):
                    for c in range(TOPK):
                        pool.indirect_dma_start(
                            out=choice[:, t, c, :], out_offset=None, in_=d["expert_rows"],
                            in_offset=bass.IndirectOffsetOnAxis(ap=k.dest[:, t, c:c + 1], axis=0)
                        ).then_inc(choice_in[t], 16)

            @block.tensor
            def _(pe):
                pe.wait_ge(b_in, 16)
                for t in range(NT):
                    for n in range(2):
                        mm = pe.matmul(k.pp[t][:, n * 512:(n + 1) * 512], k.gateT[:, t * P:(t + 1) * P],
                                       b_down[:, n * 512:(n + 1) * 512], start=True, stop=True)
                    mm.then_inc(bias_ps, 1)

            @block.scalar
            def _(act):
                chain = k.act_chain.on(act)
                for t in range(NT):
                    act.wait_ge(acc_ready, t + 1)
                    chain(act.activation(junk[:], acc[:, t % 2, :], ACT.Square, accum_out=sumsq[:, t:t + 1]))
                    act.activation(rstd[:, t:t + 1], sumsq[:, t:t + 1], ACT.Sqrt, scale=1.0 / D,
                                   bias=k.eps[:, 0:1]).then_inc(acc_sumsq, 1)

            @block.vector
            def _(dve):
                chain = k.dve_chain.on(dve)
                for t in range(NT):
                    a = acc[:, t % 2, :]
                    dve.wait_ge(bias_ps, t + 1)
                    dve.wait_ge(choice_in[t], 16 * TOPK)
                    for c in range(TOPK):
                        ins = dve.scalar_tensor_tensor(a, choice[:, t, c, :], k.gates[:, t, c:c + 1],
                                                       a if c else k.pp[t][:, :], ALU.mult, ALU.add)
                        if c < TOPK - 1:
                            chain(ins)
                    ins.then_inc(acc_ready, 1)
                    dve.wait_ge(acc_sumsq, t + 1)
                    chain(dve.reciprocal(rstd[:, t:t + 1], rstd[:, t:t + 1]))
                    chain(dve.scalar_tensor_tensor(a, a, rstd[:, t:t + 1], k.gate2[:], ALU.mult, ALU.mult))
                    chain(dve.tensor_tensor(k.x[:, t, :], k.x[:, t, :], a, ALU.add))


U_A, G_A, R_F, K_F, V_F, LR_F, G_B = 0, 4, 8, 12, 16, 20, 21
HR = 8
NCH = S // CH
CHUNKS2 = ((20, 3), (23, 2), (12, 3), (15, 3), (18, 2), (8, 3), (11, 1), (0, 3), (3, 3), (6, 2))


def place(h):
    return (h % 2) * (HR // 2) + h // 2


def stage_second(k, scope):
    nc, d = k.nc, k.d
    k.cols = k.sb("cols", [P, NCOL])
    k.silu_b = k.sb("silu_b", [P, 4, S])
    k.y_pool = k.sb("y_pool", [P, 4, S])
    k.alpha = k.sb("alpha", [P, 4, S])
    k.beta = k.sb("beta", [P, 4, S])
    k.kappa = k.sb("kappa", [P, 4, S])
    k.rho = k.sb("rho", [P, 4, S])
    k.bonus = k.sb("bonus", [P, 4, S])
    k.last = k.sb("last_decay", [P, 4, NCH])
    k.v_tok = k.sb("v_tok", [P, NT, 4 * P])
    k.z2 = k.sb("z2", [P, 21, S + 1], at=scope)
    z2 = k.z2
    tiles = [f for a, n in CHUNKS2 for f in range(a, a + n)]
    arrival = {f: n for n, f in enumerate(tiles)}
    with ExitStack() as ctx:
        sb = lambda n, s, dt=F32: k.sb(n, s, dt, at=ctx)
        sem = k.stage_semaphores(ctx)
        hT = sb("h3T", [P, KT, S])
        stage = sb("stage2", [P, 3, KT, 3 * P])
        gain = sb("gain2", [P, D])
        h = sb("h3", [P, D])
        diff = sb("diff", [P, S])
        sumsq = sb("s2_sumsq", [P, NT])
        rstd = sb("s2_rstd", [P, NT])
        inv = sb("pool_inv", [P, 4, 16])
        w_pool = sb("w_pool", [P, 4, P])
        sums = sb("sums", [P, 2, 16 + S])
        pooled = sb("pooled", [P, S])
        small_in = sem("s2_small_in")
        gain_in = sem("s2_gain_in")
        stage_in = [sem(f"s2_stage_in{n}") for n in range(3)]
        stage_used = sem("s2_stage_used")
        sumsq_done = sem("s2_sumsq_done")
        root_ready = sem("s2_root")
        h_ready = sem("s2_h_ready")
        h_ps = sem("s2_h_ps")
        hT_ready = sem("s2_hT_ready")
        z_ps = sem("z_ps")
        z_ready = sem("z_ready")
        sums_set = sem("sums_set")
        pooled_ready = sem("pooled_ready")
        pool_ps = sem("pool_ps")
        pool_read = sem("pool_read")

        with nc.Block() as block:
            @block.sync
            def _(sp):
                sp.dma_start(k.cols[:], d["cols"]).then_inc(small_in, 16)
                sp.dma_start(gain[:], row(d["norm_gain_2"][0:1, :])).then_inc(gain_in, 16)
                sp.dma_start(inv[:], d["pool_inverse"]).then_inc(small_in, 16)
                sp.dma_start(w_pool[:], d["pool_w_2"].rearrange("g c n -> c g n")).then_inc(small_in, 16)
                w = d["w_in_2"].rearrange("(k p) n -> p k n", p=P)
                for n, (a, m) in enumerate(CHUNKS2):
                    if n >= 3:
                        sp.wait_ge(stage_used, n - 2)
                    sp.dma_start(stage[:, n % 3, :, 0:m * P], w[:, :, a * P:(a + m) * P]
                                 ).then_inc(stage_in[n % 3], 16)

            @block.tensor
            def _(pe):
                for t in range(NT):
                    pe.wait_ge(h_ready, t + 1)
                    if t:
                        pe.wait_ge(hT_ready, 2 * t)
                    for q in range(KT):
                        mm = pe.transpose(k.bank(6 + q // 4)[:, (q % 4) * P:(q % 4 + 1) * P],
                                          h[:, q * P:(q + 1) * P], k.sq[:, IDENT, :])
                        if q % 4 == 3:
                            mm.then_inc(h_ps, 1)
                pe.wait_ge(hT_ready, 2 * NT)
                at = 0
                for n, (a, m) in enumerate(CHUNKS2):
                    pe.wait_ge(stage_in[n % 3], 16 * (n // 3 + 1))
                    for c in range(m):
                        if at >= 4:
                            pe.wait_ge(z_ready, at - 3)
                        for q in range(KT):
                            mm = pe.matmul(k.bank(at % 4), stage[:, n % 3, q, c * P:(c + 1) * P],
                                           hT[:, q, :], start=(q == 0), stop=(q == KT - 1))
                        at += 1
                        mm.then_inc(z_ps, 1)
                    pe.wait_ge(z_ps, at)
                    pe.sem_inc(stage_used, 1)
                pe.wait_ge(small_in, 48)
                for g in range(4):
                    pe.wait_ge(pooled_ready, g + 1)
                    pe.matmul(k.bank(4 + g), w_pool[:, g, :], pooled[:], start=True, stop=True
                              ).then_inc(pool_ps, 1)

            @block.scalar
            def _(act):
                chain = k.act_chain.on(act)
                for t in range(NT):
                    act.activation(z2[:, 2 * t:2 * t + 2, 0:512], k.x[:, t, :].rearrange(
                        "p (a n) -> p a n", a=2), ACT.Square, accum_out=sumsq[:, t:t + 1]).then_inc(sumsq_done, 1)
                act.wait_ge(sumsq_done, NT)
                act.activation(rstd[:], sumsq[:], ACT.Sqrt, scale=1.0 / D, bias=k.eps[:, 0:1]
                               ).then_inc(root_ready, 1)
                for t in range(NT):
                    for part in range(2):
                        act.wait_ge(h_ps, 2 * t + part + 1)
                        act.activation(hT[:, 4 * part:4 * part + 4, t * P:(t + 1) * P],
                                       k.bank(6 + part).rearrange("p (a b) -> p a b", b=P),
                                       ACT.Copy).then_inc(hT_ready, 1)
                for n, f in enumerate(tiles):
                    act.wait_ge(z_ps, n + 1)
                    out = k.silu_b[:, f - G_B, :] if f >= G_B else z2[:, f, 1:S + 1]
                    act.activation(out, k.bank(n % 4), ACT.Silu if f >= G_B or G_A <= f < G_A + 4
                                   else ACT.Copy).then_inc(z_ready, 1)

            @block.gpsimd
            def _(pool):
                chain = k.pool_chain.on(pool)
                chain(pool.memset(sums[:], 0.0))
                pool.wait_ge(small_in, 48)
                for g, w in enumerate(WINDOWS):
                    u = z2[:, U_A + g, 1:S + 1]
                    pool.wait_ge(z_ready, arrival[U_A + g] + 1)
                    chain(pool.tensor_copy(sums[:, 0, 16:], u))
                    for n in range(g + 1):
                        s = 1 << n
                        chain(pool.tensor_tensor(sums[:, (n + 1) % 2, 16:], sums[:, n % 2, 16:],
                                                 sums[:, n % 2, 16 - s:16 + S - s], ALU.add))
                    src = sums[:, (g + 1) % 2, 16:]
                    if g:
                        pool.wait_ge(pool_ps, g)
                    pool.tensor_scalar(pooled[:, 16:], src[:, 16:], 1.0 / w, None, ALU.mult)
                    chain(pool.tensor_tensor(pooled[:, 0:16], src[:, 0:16], inv[:, g, :], ALU.mult))
                    pool.tensor_tensor(pooled[:], pooled[:], u, ALU.subtract).then_inc(pooled_ready, 1)
                    pool.wait_ge(pooled_ready, g + 1)

            @block.vector
            def _(dve):
                chain = k.dve_chain.on(dve)
                dve.wait_ge(root_ready, 1)
                dve.memset(z2[:, :, 0:1], 0.0)
                chain(dve.reciprocal(rstd[:], rstd[:]))
                dve.wait_ge(gain_in, 16)
                for t in range(NT):
                    if t:
                        dve.wait_ge(h_ps, 2 * t)
                    dve.scalar_tensor_tensor(h[:], k.x[:, t, :], rstd[:, t:t + 1], gain[:], ALU.mult,
                                             ALU.mult).then_inc(h_ready, 1)
                dve.wait_ge(small_in, 48)
                for f in sorted(range(R_F, LR_F + 1), key=lambda f: arrival[f]):
                    dve.wait_ge(z_ready, arrival[f] + 1)
                    chain(dve.tensor_tensor(diff[:], z2[:, f, 0:S], z2[:, f, 1:S + 1], ALU.subtract))
                    c = MU0 + f - R_F
                    chain(dve.scalar_tensor_tensor(z2[:, f, 1:S + 1], diff[:], k.cols[:, c:c + 1],
                                                   z2[:, f, 1:S + 1], ALU.mult, ALU.add))
                dve.wait_ge(z_ready, arrival[G_A + 3] + 1)
                for g in range(4):
                    dve.wait_ge(pool_ps, g + 1)
                    dve.scalar_tensor_tensor(k.y_pool[:, g, :], k.bank(4 + g), k.cols[:, PS0 + g:PS0 + g + 1],
                                             z2[:, G_A + g, 1:S + 1], ALU.mult, ALU.mult).then_inc(pool_read, 1)


def rwkv_features(k):
    nc, d, z2 = k.nc, k.d, k.z2
    r = z2[:, R_F:R_F + 4, 1:S + 1]
    key = z2[:, K_F:K_F + 4, 1:S + 1]
    v = z2[:, V_F:V_F + 4, 1:S + 1]
    with ExitStack() as ctx:
        sb = lambda n, s, dt=F32: k.sb(n, s, dt, at=ctx)
        sem = k.stage_semaphores(ctx)
        w_lora = sb("w_lora", [P, 4 * P])
        rate = sb("rate", [P, 4, S])
        sigw = sb("sigw", [P, 4, S])
        cum = sb("cum", [P, 4, S])
        grow = sb("decay_grow", [P, 4, S])
        kk = sb("kk", [P, 4, S])
        root = sb("kk_root", [P, 4, S])
        keep = sb("keep", [P, S])
        one_less = sb("one_less", [P, 4])
        lora_in = sem("lora_in")
        tanh_ready = sem("tanh_ready")
        lora_ps = sem("lora_ps")
        sigw_ready = sem("sigw_ready")
        rate_ready = sem("rate_ready")
        cum_ready = sem("cum_ready")
        prev_ready = sem("prev_ready")
        decay_ready = sem("decay_ready")
        kk_ready = sem("kk_ready")
        square_ready = sem("square_ready")
        norm_ps = sem("norm_ps")
        norm_clamped = sem("norm_clamped")
        norm_root = sem("norm_root")
        pair_ready = sem("rk_ready")
        bonus_ps = sem("bonus_ps")

        with nc.Block() as block:
            @block.sync
            def _(sp):
                sp.dma_start(w_lora[0:64, :], d["w_up_2"]).then_inc(lora_in, 16)
                sp.dma_start(w_lora[64:128, :], d["a_up_2"]).then_inc(lora_in, 16)

            @block.tensor
            def _(pe):
                pe.wait_ge(lora_in, 32)
                for j in range(4):
                    mm = pe.matmul(k.bank(4 + j), w_lora[64:128, j * P:(j + 1) * P],
                                   z2[64:128, LR_F, 1:S + 1], start=True, stop=True)
                mm.then_inc(lora_ps, 1)
                pe.wait_ge(tanh_ready, 1)
                for j in range(4):
                    mm = pe.matmul(k.bank(j), w_lora[0:64, j * P:(j + 1) * P],
                                   z2[0:64, LR_F, 1:S + 1], start=True, stop=True)
                mm.then_inc(lora_ps, 1)
                pe.wait_ge(square_ready, 1)
                pe.wait_ge(rate_ready, 4)
                for j in range(4):
                    mm = pe.matmul(k.bank(4 + j), k.sq[:, BLOCK, :], root[:, j, :], start=True, stop=True)
                mm.then_inc(norm_ps, 1)
                pe.wait_ge(pair_ready, 1)
                pe.wait_ge(sigw_ready, 4)
                for j in range(4):
                    mm = pe.matmul(k.bank(j), k.sq[:, BLOCK, :], k.bonus[:, j, :], start=True, stop=True)
                mm.then_inc(bonus_ps, 1)

            @block.scalar
            def _(act):
                act.activation(z2[0:64, LR_F, 1:S + 1], z2[0:64, LR_F, 1:S + 1], ACT.Tanh).then_inc(tanh_ready, 1)
                act.wait_ge(kk_ready, 1)
                act.activation(root[:], kk[:], ACT.Square).then_inc(square_ready, 1)
                act.wait_ge(lora_ps, 1)
                for j in range(4):
                    act.activation(rate[:, j, :], k.bank(4 + j), ACT.Sigmoid,
                                   bias=k.cols[:, A00 + j:A00 + j + 1]).then_inc(rate_ready, 1)
                act.wait_ge(lora_ps, 2)
                for j in range(4):
                    act.activation(sigw[:, j, :], k.bank(j), ACT.Sigmoid,
                                   bias=k.cols[:, W00 + j:W00 + j + 1]).then_inc(sigw_ready, 1)
                act.wait_ge(norm_clamped, 1)
                act.activation(root[:], root[:], ACT.Sqrt).then_inc(norm_root, 1)
                act.wait_ge(cum_ready, 4)
                act.activation(grow[:], cum[:], ACT.Exp, scale=LOG_DECAY).then_inc(decay_ready, 1)
                act.activation(k.rho[:], cum[:], ACT.Exp, scale=-LOG_DECAY).then_inc(decay_ready, 1)
                act.wait_ge(prev_ready, 1)
                act.activation(k.alpha[:], k.alpha[:], ACT.Exp, scale=-LOG_DECAY).then_inc(decay_ready, 1)

            @block.vector
            def _(dve):
                chain = k.dve_chain.on(dve)
                col = lambda c, j: k.cols[:, c + j:c + j + 1]
                for j in range(4):
                    ins = dve.tensor_scalar(kk[:, j, :], key[:, j, :], col(KK0, j), None, ALU.mult)
                ins.then_inc(kk_ready, 1)
                dve.tensor_scalar(one_less[:], k.cols[:, KA0:KA0 + 4], -1.0, 1.0, ALU.mult, ALU.add)
                chain(dve.memset(keep[:], 1.0))
                chain(dve.memset(keep[:, 0:S:CH], 0.0))
                dve.wait_ge(rate_ready, 4)
                for j in range(4):
                    ins = dve.tensor_scalar(k.kappa[:, j, :], rate[:, j, :], col(KA0, j), one_less[:, j:j + 1],
                                            ALU.mult, ALU.add)
                chain(ins)
                chain(dve.tensor_tensor(k.kappa[:], k.kappa[:], key, ALU.mult))
                for j in range(4):
                    ins = dve.scalar_tensor_tensor(k.bonus[:, j, :], r[:, j, :], col(RK0, j), k.kappa[:, j, :],
                                                   ALU.mult, ALU.mult)
                ins.then_inc(pair_ready, 1)
                for j in range(4):
                    dve.wait_ge(sigw_ready, j + 1)
                    dve.tensor_tensor_scan(cum[:, j, :], keep[:], sigw[:, j, :], 0.0, ALU.mult,
                                           ALU.add).then_inc(cum_ready, 1)
                dve.wait_ge(cum_ready, 4)
                dve.tensor_tensor(k.alpha[:], cum[:], sigw[:], ALU.subtract).then_inc(prev_ready, 1)
                dve.wait_ge(norm_ps, 1)
                for j in range(4):
                    ins = dve.tensor_scalar(root[:, j, :], k.bank(4 + j), 1e-24, None, ALU.max)
                ins.then_inc(norm_clamped, 1)
                dve.wait_ge(norm_root, 1)
                chain(dve.reciprocal(root[:], root[:]))
                chain(dve.tensor_tensor(kk[:], kk[:], root[:], ALU.mult))
                chain(dve.tensor_tensor(k.beta[:], kk[:], rate[:], ALU.mult))
                dve.wait_ge(decay_ready, 1)
                chain(dve.tensor_tensor(k.beta[:], k.beta[:], grow[:], ALU.mult))
                chain(dve.tensor_tensor(k.kappa[:], k.kappa[:], grow[:], ALU.mult))
                dve.wait_ge(decay_ready, 2)
                chain(dve.tensor_copy(k.last[:], k.rho[:, :, CH - 1:S:CH]))
                chain(dve.tensor_tensor(k.rho[:], k.rho[:], r, ALU.mult))
                dve.wait_ge(decay_ready, 3)
                chain(dve.scalar_tensor_tensor(k.alpha[:], kk[:], -1.0, k.alpha[:], ALU.mult, ALU.mult))
                dve.wait_ge(bonus_ps, 1)
                for j in range(4):
                    ins = dve.tensor_tensor(k.bonus[:, j, :], k.bank(j), v[:, j, :], ALU.mult)
                chain(ins)


def rwkv_turn(k, name, pairs):
    nc = k.nc
    with ExitStack() as ctx:
        sem = k.stage_semaphores(ctx)
        turn_ps = sem(name + "_tok_ps")
        turn_read = sem(name + "_tok_read")
        jobs = [(dst, src, t) for dst, src in pairs for t in range(NT)]
        with nc.Block() as block:
            @block.tensor
            def _(pe):
                for n, (dst, src, t) in enumerate(jobs):
                    if n >= 8:
                        pe.wait_ge(turn_read, n - 7)
                    for j in range(4):
                        mm = pe.transpose(k.bank(n % 8)[:, j * P:(j + 1) * P], src[:, j, t * P:(t + 1) * P],
                                          k.sq[:, IDENT, :])
                    mm.then_inc(turn_ps, 1)

            @block.scalar
            def _(act):
                for n, (dst, src, t) in enumerate(jobs):
                    act.wait_ge(turn_ps, n + 1)
                    act.activation(dst[:, t, :], k.bank(n % 8), ACT.Copy).then_inc(turn_read, 1)


def rwkv_inverse(k, v_tok, solveT, out_sa, r_v, y_v):
    nc = k.nc
    with ExitStack() as ctx:
        sb = lambda n, s, dt=F32: k.sb(n, s, dt, at=ctx)
        sem = k.stage_semaphores(ctx)
        masks = sb("level_masks", [P, NSQ - LEVEL0, P])
        mT = sb("mT", [P, 2, HR, P])
        level = sb("level", [P, 2, HR, P])
        solve = sb("solve", [P, 2, HR, P])
        product = sb("product", [P, 2, HR, P])
        mask_in = sem("mask_in")
        prod_ps = sem("mat_ps")
        prod_read = sem("mat_read")
        m_ready = sem("m_ready")
        level_ready = sem("level_ready")
        p_ps = sem("p_ps")
        p_ready = sem("p_ready")
        x_ps = sem("x_ps")
        x_ready = sem("solve_ready")
        v_ps = sem("vpart_ps")
        v_read = sem("vpart_read")
        heads = lambda ap: ap.rearrange("p (h n) -> p h n", h=HR)
        over_heads = lambda m: m.unsqueeze(1).broadcast_to([P, HR, P])
        NL = 5
        kinds = (("beta", "alpha"), ("alpha", "beta"), ("kappa", "alpha"), ("kappa", "rho"), ("beta", "rho"))

        with nc.Block() as block:
            @block.sync
            def _(sp):
                sp.dma_start(masks[:], k.d["square"][:, LEVEL0:NSQ, :]).then_inc(mask_in, 16)

            @block.tensor
            def _(pe):
                n = 0
                for pair in range(NT // 2):
                    for e in range(2):
                        t = 2 * pair + e
                        for m, (a, b) in enumerate(kinds):
                            if n >= 4:
                                pe.wait_ge(prod_read, n - 3)
                            for h in range(HR):
                                r = (h % 2) * CH
                                c = place(h) * P
                                left = {"alpha": k.alpha, "beta": k.beta, "kappa": k.kappa}[a]
                                right = {"alpha": k.alpha, "beta": k.beta, "rho": k.rho}[b]
                                mm = pe.matmul(k.pp[n % 4][:, c:c + P],
                                               left[r:r + CH, h // 2, t * P:(t + 1) * P],
                                               right[r:r + CH, h // 2, t * P:(t + 1) * P],
                                               start=True, stop=True)
                            mm.then_inc(prod_ps, 1)
                            n += 1
                            if m in (2, 3):
                                pe.wait_ge(prod_read, n)
                                for h in range(HR):
                                    mm = pe.matmul(k.pp[(n - 1) % 4][:, place(h) * CH:(place(h) + 1) * CH],
                                                   product[:, m - 2, place(h), :],
                                                   v_tok[:, t, h * CH:(h + 1) * CH], start=True, stop=True)
                                mm.then_inc(v_ps, 1)
                                pe.wait_ge(v_read, 2 * t + m - 1)
                    for s in range(NL):
                        for e in range(2):
                            t = 2 * pair + e
                            at = (pair * NL + s) * 2 + e
                            pe.wait_ge(level_ready, at + 1)
                            pe.wait_ge(x_ready, 2 * (NL + 1) * pair + 2 * s + e + 1)
                            pe.wait_ge(prod_read, n)
                            for h in range(HR):
                                mm = pe.matmul(k.pp[2 * e][:, h * P:(h + 1) * P], level[:, e, h, :],
                                               solve[:, e, h, :], start=True, stop=True)
                            mm.then_inc(p_ps, 1)
                        for e in range(2):
                            t = 2 * pair + e
                            at = (pair * NL + s) * 2 + e
                            pe.wait_ge(p_ready, at + 1)
                            for h in range(HR):
                                mm = pe.matmul(k.pp[2 * e + 1][:, h * P:(h + 1) * P], product[:, e, h, :],
                                               solveT[:, t, h, :], start=True, stop=True)
                            if s < NL - 1:
                                for h in range(HR):
                                    mm = pe.matmul(k.pp[2 * e][:, h * P:(h + 1) * P], solveT[:, t, h, :],
                                                   product[:, e, h, :], start=True, stop=True)
                            mm.then_inc(x_ps, 1)
                    pe.wait_ge(x_ready, 2 * (NL + 1) * (pair + 1))

            @block.gpsimd
            def _(pool):
                pool.wait_ge(mask_in, 16)
                for pair in range(NT // 2):
                    for s in range(NL):
                        for e in range(2):
                            at = (pair * NL + s) * 2 + e
                            pool.wait_ge(m_ready, 2 * pair + e + 1)
                            if at >= 2:
                                pool.wait_ge(p_ps, at - 1)
                            pool.tensor_tensor(level[:, e], mT[:, e], over_heads(masks[:, s, :]),
                                               ALU.mult).then_inc(level_ready, 1)

            @block.scalar
            def _(act):
                for pair in range(NT // 2):
                    for e in range(2):
                        t = 2 * pair + e
                        act.wait_ge(prod_ps, 5 * t + 1)
                        if pair:
                            act.wait_ge(level_ready, 2 * NL)
                        act.activation(mT[:, e], heads(k.pp[(5 * t) % 4][:, :]), ACT.Copy).then_inc(m_ready, 1)
                        for m in range(2):
                            act.wait_ge(v_ps, 2 * t + m + 1)
                            act.activation((r_v, y_v)[m][:, t, :], k.pp[(5 * t + 2 + m) % 4][:, 0:HR * CH],
                                           ACT.Copy).then_inc(v_read, 1)
                    for s in range(NL):
                        for e in range(2):
                            at = (pair * NL + s) * 2 + e
                            act.wait_ge(p_ps, at + 1)
                            act.activation(product[:, e], heads(k.pp[2 * e][:, :]), ACT.Copy).then_inc(p_ready, 1)

            @block.vector
            def _(dve):
                chain = k.dve_chain.on(dve)
                dve.wait_ge(mask_in, 16)
                for pair in range(NT // 2):
                    for e in range(2):
                        t = 2 * pair + e
                        for m in range(5):
                            n = 5 * t + m
                            dve.wait_ge(prod_ps, n + 1)
                            src = heads(k.pp[n % 4][:, :])
                            if m < 2:
                                out = (solveT[:, t], solve[:, e])[m]
                                if m == 0:
                                    dve.wait_ge(m_ready, t + 1)
                                    src = mT[:, e]
                                chain(dve.tensor_tensor(out, src, over_heads(masks[:, NL + m, :]), ALU.mult))
                                chain(dve.tensor_tensor(out, out, over_heads(k.sq[:, IDENT, :]), ALU.add))
                                dve.sem_inc(prod_read, 1)
                                if m == 1:
                                    dve.sem_inc(x_ready, 1)
                            elif m < 4:
                                if t:
                                    dve.wait_ge(v_ps, 2 * t - 2 + m - 1)
                                dve.tensor_tensor(product[:, m - 2], src, over_heads(
                                    k.sq[:, (LT, LE)[m - 2], :]), ALU.mult).then_inc(prod_read, 1)
                            else:
                                dve.tensor_tensor(out_sa[:, t], src, over_heads(k.sq[:, LE, :]),
                                                  ALU.mult).then_inc(prod_read, 1)
                    for s in range(NL):
                        for e in range(2):
                            t = 2 * pair + e
                            at = (pair * NL + s) * 2 + e
                            dve.wait_ge(x_ps, at + 1)
                            ins = dve.tensor_tensor(solveT[:, t], solveT[:, t], heads(k.pp[2 * e + 1][:, :]), ALU.add)
                            if s < NL - 1:
                                ins = dve.tensor_tensor(solve[:, e], solve[:, e], heads(k.pp[2 * e][:, :]), ALU.add)
                            ins.then_inc(x_ready, 1)
                            dve.wait_ge(x_ready, 2 * (NL + 1) * pair + 2 + 2 * s + e + 1)


def stage_rwkv(k):
    nc, d, v_tok = k.nc, k.d, k.v_tok
    with ExitStack() as ctx:
        sb = lambda n, s, dt=F32: k.sb(n, s, dt, at=ctx)
        beta_tok = sb("beta_tok", [P, NT, 4 * P])
        kappa_tok = sb("kappa_tok", [P, NT, 4 * P])
        rwkv_turn(k, "bk", ((beta_tok, k.beta), (kappa_tok, k.kappa)))
        solveT = sb("solveT", [P, NT, HR, P])
        out_sa = sb("out_sa", [P, NT, HR, P])
        r_v = sb("r_v", [P, NT, HR * CH])
        y_v = sb("y_v", [P, NT, HR * CH])
        rwkv_inverse(k, v_tok, solveT, out_sa, r_v, y_v)
        rwkv_states(k, v_tok, beta_tok, kappa_tok, solveT, out_sa, r_v, y_v)
        output(k, y_v)


def rwkv_states(k, v_tok, beta_tok, kappa_tok, solveT, out_sa, r_v, y_v):
    nc = k.nc
    with ExitStack() as ctx:
        sb = lambda n, s, dt=F32: k.sb(n, s, dt, at=ctx)
        sem = k.stage_semaphores(ctx)
        state = sb("rwkv_state", [P, 4, CH])
        rhs = sb("rhs", [P, 2, 4 * CH])
        sa = sb("sa", [P, HR * CH])
        state_ready = sem("rwkv_state_ready")
        rhs_ps = sem("rhs_ps")
        rhs_ready = sem("rhs_ready")
        sa_ps = sem("sa_ps")
        sa_ready = sem("sa_ready")
        y_ps = sem("rwkv_y_ps")
        y_read = sem("rwkv_y_read")
        next_ps = sem("next_ps")

        with nc.Block() as block:
            @block.tensor
            def _(pe):
                for c in range(NCH):
                    t, o = c // 2, (c % 2) * CH
                    rows = slice(o, o + CH)
                    pe.wait_ge(state_ready, c + 1)
                    for h in range(HR):
                        r = (h % 2) * CH
                        mm = pe.matmul(k.bank(h % 2)[rows, h // 2 * CH:(h // 2 + 1) * CH],
                                       k.alpha[r:r + CH, h // 2, c * CH:(c + 1) * CH],
                                       state[r:r + CH, h // 2, :], start=True, stop=True)
                    mm.then_inc(rhs_ps, 1)
                    if c:
                        pe.wait_ge(y_read, c)
                    for h in range(HR):
                        r = (h % 2) * CH
                        pe.matmul(k.bank(4 + h % 2)[rows, h // 2 * CH:(h // 2 + 1) * CH],
                                  k.rho[r:r + CH, h // 2, c * CH:(c + 1) * CH],
                                  state[r:r + CH, h // 2, :], start=True, stop=True)
                    for h in range(HR):
                        r = (h % 2) * CH
                        pe.matmul(k.bank(3)[r:r + CH, h // 2 * CH:(h // 2 + 1) * CH],
                                  kappa_tok[rows, t, h * CH:(h + 1) * CH], v_tok[rows, t, h * CH:(h + 1) * CH],
                                  start=(h < 2), stop=False, skip_group_check=True)
                    pe.wait_ge(rhs_ready, c + 1)
                    for h in range(HR):
                        q = place(h)
                        mm = pe.matmul(k.bank(2)[rows, q * CH:(q + 1) * CH], solveT[rows, t, q, rows],
                                       rhs[rows, h % 2, h // 2 * CH:(h // 2 + 1) * CH], start=True, stop=True)
                    mm.then_inc(sa_ps, 1)
                    pe.wait_ge(sa_ready, c + 1)
                    for h in range(HR):
                        r = (h % 2) * CH
                        q = place(h)
                        mm = pe.matmul(k.bank(3)[r:r + CH, h // 2 * CH:(h // 2 + 1) * CH],
                                       beta_tok[rows, t, h * CH:(h + 1) * CH], sa[rows, q * CH:(q + 1) * CH],
                                       start=False, stop=(h >= HR - 2), skip_group_check=True)
                    mm.then_inc(next_ps, 1)
                    for h in range(HR):
                        q = place(h)
                        mm = pe.matmul(k.bank(6)[rows, q * CH:(q + 1) * CH], out_sa[rows, t, q, rows],
                                       sa[rows, q * CH:(q + 1) * CH], start=True, stop=True)
                    mm.then_inc(y_ps, 1)

            @block.scalar
            def _(act):
                for c in range(NCH):
                    rows = slice((c % 2) * CH, (c % 2) * CH + CH)
                    act.wait_ge(sa_ps, c + 1)
                    act.activation(sa[rows, :], k.bank(2)[rows, :], ACT.Copy).then_inc(sa_ready, 1)

            @block.vector
            def _(dve):
                chain = k.dve_chain.on(dve)
                dve.memset(state[:], 0.0).then_inc(state_ready, 1)
                dve.wait_ge(state_ready, 1)
                for c in range(NCH):
                    t = c // 2
                    rows = slice((c % 2) * CH, (c % 2) * CH + CH)
                    two = lambda ap: ap.rearrange("p (b n) -> p b n", b=2)
                    dve.wait_ge(rhs_ps, c + 1)
                    dve.tensor_tensor(rhs[rows], two(k.pp[0][rows, :])[:, :, 0:4 * CH], two(r_v[rows, t, :]),
                                      ALU.add).then_inc(rhs_ready, 1)
                    dve.wait_ge(next_ps, c + 1)
                    chain(dve.tensor_tensor(state[:], state[:], k.bank(3)[:, 0:4 * CH].rearrange(
                        "p (j n) -> p j n", j=4), ALU.add))
                    dve.tensor_tensor(state[:], state[:], k.last[:, :, c:c + 1].broadcast_to([P, 4, CH]),
                                      ALU.mult).then_inc(state_ready, 1)
                    dve.wait_ge(state_ready, c + 2)
                    dve.wait_ge(y_ps, c + 1)
                    y = y_v[rows, t, :]
                    chain(dve.tensor_tensor(two(y), two(y), two(k.pp[2][rows, :])[:, :, 0:4 * CH], ALU.add))
                    dve.tensor_tensor(y, y, k.bank(6)[rows, :], ALU.add).then_inc(y_read, 1)


def output(k, y):
    nc, d = k.nc, k.d
    k.w_out2_in = k.sem("w_out2_in")
    with ExitStack() as ctx:
        sb = lambda n, s, dt=F32: k.sb(n, s, dt, at=ctx)
        sem = k.stage_semaphores(ctx)
        w_out2 = sb("w_out2", [P, KT, D])
        square = sb("gn_square", [P, HR * CH])
        mean = sb("gn_mean", [P, HR])
        var = sb("gn_var", [P, HR])
        normed = sb("normed", [P, 2, HR * CH])
        final = sb("final", [P, 2, D])
        gain = sb("final_gain", [P, D])
        junk = flat(k.alpha[:])[:, 0:D]
        sumsq = sb("final_sumsq", [P, NT])
        rstd = sb("final_rstd", [P, NT])
        w_in = sem("final_w_in")
        centred = sem("centred")
        squared = sem("squared")
        var_ready = sem("var_ready")
        gn_root = sem("gn_root")
        normed_ready = sem("normed_ready")
        turned_ps = sem("gn_turned_ps")
        y_ready = sem("y_rwkv_ready")
        out_ps = sem("out_ps")
        sum_ready = sem("sum_ready")
        final_root = sem("final_root")
        final_ready = sem("final_ready")
        out_done = sem("out_done")
        yb = k.beta
        heads = lambda ap: ap.rearrange("p (h n) -> p h n", h=HR)

        with nc.Block() as block:
            @block.sync
            def _(sp):
                sp.dma_start(w_out2[:], d["w_out_2"].rearrange("(k p) n -> p k n", p=P)).then_inc(w_in, 16)
                sp.dma_start(gain[:], row(d["final_gain_2"][0:1, :])).then_inc(w_in, 16)
                for t in range(NT):
                    sp.wait_ge(final_ready, t + 1)
                    sp.dma_start(d["out"][t * P:(t + 1) * P, :], final[:, t % 2, :]).then_inc(out_done, 16)
                    sp.wait_ge(out_done, 16 * (t + 1))

            @block.tensor
            def _(pe):
                for t in range(NT):
                    pe.wait_ge(normed_ready, t + 1)
                    for j in range(4):
                        mm = pe.transpose(k.bank(j)[:, t * P:(t + 1) * P], normed[:, t % 2, j * P:(j + 1) * P],
                                          k.sq[:, IDENT, :])
                    mm.then_inc(turned_ps, 1)
                pe.wait_ge(w_in, 32)
                for t in range(NT):
                    if t >= 2:
                        pe.wait_ge(sum_ready, t - 1)
                    for n in range(2):
                        for q in range(KT):
                            if q == 4 and t == 0 and n == 0:
                                pe.wait_ge(y_ready, 1)
                            src = k.y_pool[:, q, :] if q < 4 else yb[:, q - 4, :]
                            mm = pe.matmul(k.pp[2 + t % 2][:, n * 512:(n + 1) * 512], src[:, t * P:(t + 1) * P],
                                           w_out2[:, q, n * 512:(n + 1) * 512],
                                           start=(q == 0), stop=(q == KT - 1))
                    mm.then_inc(out_ps, 1)

            @block.scalar
            def _(act):
                chain = k.act_chain.on(act)
                for t in range(NT):
                    act.wait_ge(centred, t + 1)
                    act.activation(square[:], y[:, t, :], ACT.Square).then_inc(squared, 1)
                    act.wait_ge(var_ready, t + 1)
                    act.activation(var[:], var[:], ACT.Sqrt, scale=1.0 / CH, bias=k.eps[:, 1:2]).then_inc(gn_root, 1)
                for t in range(NT):
                    act.wait_ge(sum_ready, t + 1)
                    chain(act.activation(junk, k.x[:, t, :], ACT.Square, accum_out=sumsq[:, t:t + 1]))
                    act.activation(rstd[:, t:t + 1], sumsq[:, t:t + 1], ACT.Sqrt, scale=1.0 / D,
                                   bias=k.eps[:, 0:1]).then_inc(final_root, 1)

            @block.vector
            def _(dve):
                chain = k.dve_chain.on(dve)
                for t in range(NT):
                    yt = heads(y[:, t, :])
                    chain(dve.tensor_reduce(mean[:], yt, AX.X, ALU.add))
                    chain(dve.tensor_scalar(mean[:], mean[:], 1.0 / CH, None, ALU.mult))
                    dve.tensor_tensor(yt, yt, mean[:].unsqueeze(2).broadcast_to([P, HR, CH]),
                                      ALU.subtract).then_inc(centred, 1)
                    dve.wait_ge(squared, t + 1)
                    dve.tensor_reduce(var[:], heads(square[:]), AX.X, ALU.add).then_inc(var_ready, 1)
                    dve.wait_ge(gn_root, t + 1)
                    chain(dve.reciprocal(var[:], var[:]))
                    if t >= 2:
                        dve.wait_ge(turned_ps, t - 1)
                    out = normed[:, t % 2, :].rearrange("p (j two n) -> p two j n", two=2, n=CH)
                    dve.tensor_tensor(out, y[:, t, :].rearrange("p (two j n) -> p two j n", two=2, n=CH),
                                      var[:].rearrange("p (two j) -> p two j", two=2).unsqueeze(3).broadcast_to(
                                          [P, 2, 4, CH]), ALU.mult).then_inc(normed_ready, 1)
                    dve.wait_ge(normed_ready, t + 1)
                dve.wait_ge(turned_ps, NT)
                for j in range(4):
                    ins = dve.tensor_scalar(yb[:, j, :], k.bank(j), k.cols[:, GG0 + j:GG0 + j + 1],
                                            k.cols[:, GB0 + j:GB0 + j + 1], ALU.mult, ALU.add)
                chain(ins)
                chain(dve.tensor_tensor(yb[:], yb[:], k.bonus[:], ALU.add))
                dve.tensor_tensor(yb[:], yb[:], k.silu_b[:], ALU.mult).then_inc(y_ready, 1)
                dve.wait_ge(w_in, 32)
                for t in range(NT):
                    dve.wait_ge(out_ps, t + 1)
                    dve.tensor_tensor(k.x[:, t, :], k.x[:, t, :], k.pp[2 + t % 2][:, :], ALU.add
                                      ).then_inc(sum_ready, 1)
                    dve.wait_ge(final_root, t + 1)
                    chain(dve.reciprocal(rstd[:, t:t + 1], rstd[:, t:t + 1]))
                    if t >= 2:
                        dve.wait_ge(out_done, 16 * (t - 1))
                    dve.scalar_tensor_tensor(final[:, t % 2, :], k.x[:, t, :], rstd[:, t:t + 1], gain[:],
                                             ALU.mult, ALU.mult).then_inc(final_ready, 1)
                    dve.wait_ge(final_ready, t + 1)


def build(nc, dram):
    with ExitStack() as ctx:
        k = Core(nc, ctx, dram)
        with ExitStack() as front:
            stage_front(k, front)
            stage_mixers(k, front)
            stage_router(k, front)
        stage_experts(k)
        stage_combine(k)
        with ExitStack() as scope:
            stage_second(k, scope)
            rwkv_features(k)
            rwkv_turn(k, "v", ((k.v_tok, k.z2[:, V_F:V_F + 4, 1:S + 1]),))
        stage_rwkv(k)


def packed_columns(a):
    names = ["shift_mu_2", "w0_2", "a0_2", "k_k_2", "k_a_2", "r_k_2", "gn_gain_2", "gn_bias_2",
             "pool_scale_2", "c"]
    return np.ascontiguousarray(np.concatenate([np.asarray(a[n]).reshape(-1, P) for n in names]).T)


def kernel(**inputs):
    import concourse.bacc as bacc
    from concourse.bass_utils import run_bass_kernel_spmd

    a = {n: np.asarray(v) for n, v in inputs.items()}
    arrays = {
        "x": a["x"][0],
        "cols": packed_columns(a),
        "w_gate_up": a["w_gate_up"][0].reshape(NE, KT, P, NM, P, 2).transpose(0, 3, 2, 1, 5, 4).reshape(
            NE * NM * P, KT * 2 * P),
        "w_down": a["w_down"][0].reshape(NE * NM * P, D),
        "b_gate_up": a["b_gate_up"][0].reshape(NE, NM, P, 2).transpose(0, 1, 3, 2).reshape(NE, NM * 2 * P),
        "picked": picked_constant(),
        "square": square_constants(),
        "log_count": attention_constant(),
        "rope": rope_constant(),
        "count": count_constant(),
        "pool_inverse": pool_constant(),
        "token": np.ascontiguousarray(np.arange(S, dtype=np.int32).reshape(NT, P).T),
        "w_gate_lr": np.concatenate([a["w_gate_lr"][0], a["b_gate"]]),
    }
    for n in ("w_mod", "w_in", "w_out", "router_w", "b_down", "w_in_2", "pool_w_2", "w_up_2", "a_up_2",
              "w_out_2"):
        arrays[n] = a[n][0]
    for n in ("b_mod", "g_pre_mix", "g_gla", "g_post_mix", "g_pre_ffn", "router_b", "g_post_ffn",
              "norm_gain_2", "final_gain_2"):
        arrays[n] = a[n].reshape(1, -1)

    nc = bacc.Bacc("TRN2", target_bir_lowering=False, num_devices=1)
    dram, sent = {}, {}
    for n, v in arrays.items():
        v = np.ascontiguousarray(v)
        sent["in_" + n] = v
        dram[n] = nc.dram_tensor("in_" + n, v.shape, mybir.dt.from_np(v.dtype), kind="ExternalInput").ap()
    dram["out"] = nc.dram_tensor("out", [S, D], F32, kind="ExternalOutput").ap()
    dram["h2"] = nc.dram_tensor("h2_rows", [S, D], F32, kind="Internal").ap()
    dram["slot_token"] = nc.dram_tensor("slot_token", [(NBLK + 1) * SLOTS, 1], I32, kind="Internal").ap()
    dram["expert_rows"] = nc.dram_tensor("expert_rows", [NBLK * SLOTS, D], F32, kind="Internal").ap()
    build(nc, dram)
    result = run_bass_kernel_spmd(nc, [sent], core_ids=[0])
    return result.results[0]["out"].reshape(1, S, D)
```

```python
from contextlib import ExitStack

import numpy as np
import concourse.bass as bass
from concourse import mybir

F32 = mybir.dt.float32
F32R = mybir.dt.float32r
I32 = mybir.dt.int32
U32 = mybir.dt.uint32
ALU = mybir.AluOpType
ACT = mybir.ActivationFunctionType
AX = mybir.AxisListType

P = 128
S = 512
NT = S // P
D = 1024
KT = D // P
HA, DA = 8, 64
HG, DK, DV = 4, 64, 128
RANK = 16
D_IN = 3 * HA * DA + 2 * HG * DK + 2 * HG * DV + RANK
QA, KA, VA = 0, 512, 1024
QG, KG, VG, RG, LR = 1536, 1792, 2048, 2560, 3072
NE, TOPK = 32, 4
SLOTS = 128
EXTRA = (S * TOPK) // (SLOTS + 1)
NBLK = NE + EXTRA
TABLE = 3 * (NBLK + 1) + 2
UP = 2 * P
NM = 8
GN_EPS = 64e-5
EPS = 1e-6
LIMIT, ALPHA = 7.0, 1.702
CH = 64
D_IN2 = 3200
NF2 = D_IN2 // P
LOG_DECAY = float(np.exp(-0.5))
WINDOWS = (2, 4, 8, 16)

MU0, W00, A00, KK0, KA0, RK0, GG0, GB0, PS0, C0 = 0, 13, 17, 21, 25, 29, 33, 37, 41, 45
NCOL = 53

IDENT, ONES, BLOCK, CUM, SUF, BEFORE, LT, LE = range(8)
LEVEL0 = 8
NSQ = LEVEL0 + 7
NSQ_KEPT = 8


def square_constants():
    i = np.arange(P)[:, None]
    j = np.arange(P)[None, :]
    same = i // CH == j // CH
    m = np.zeros((NSQ, P, P), np.float32)
    m[IDENT] = i == j
    m[ONES] = 1.0
    m[BLOCK] = same
    m[CUM] = (same & (i <= j)) / 16.0
    m[SUF] = (same & (i > j)) / 16.0
    m[BEFORE] = i < j
    m[LT] = same & (i < j)
    m[LE] = same & (i <= j)
    for n in range(5):
        s = 2 << n
        m[LEVEL0 + n] = (i // (2 * s) == j // (2 * s)) & (i // s < j // s)
    m[LEVEL0 + 5] = (i // 2 == j // 2) & (i < j)
    m[LEVEL0 + 6] = (i // 2 == j // 2) & (i > j)
    return np.ascontiguousarray(m.transpose(1, 0, 2))


def attention_constant():
    t = np.arange(S)[:, None]
    j = np.arange(S)[None, :]
    d = t - j
    n = sum(((d >= 0) & (d % dil == 0) & (d <= window)).astype(np.float64)
            for window, dil in ((128, 1), (512, 4), (2048, 16)))
    m = np.where(n > 0, np.log(np.maximum(n, 1)), -1e30).astype(np.float32)
    return np.ascontiguousarray(m.reshape(NT, P, S).transpose(1, 0, 2))


def rope_constant():
    half = DA // 2
    freq = (10000.0 ** (-np.arange(half, dtype=np.float32) / half)).astype(np.float32)
    ang = np.arange(S, dtype=np.float32)[:, None] * freq[None, :]
    cs = np.stack([np.cos(ang), np.sin(ang)], 1).astype(np.float32)
    both = np.stack([cs * DA ** -0.5, cs], 1)
    return np.ascontiguousarray(both.reshape(NT, P, 2, 2, half).transpose(1, 0, 2, 3, 4))


def count_constant():
    return np.ascontiguousarray(np.broadcast_to(np.arange(NBLK + 1, dtype=np.float32), (P, NBLK + 1)))


def picked_constant():
    e = np.arange(NE)[:, None]
    p = np.arange(P)[None, :]
    return np.ascontiguousarray(((p % NE == e) & (p < 2 * NE)).astype(np.float32).reshape(-1, 1))


def pool_constant():
    pos = np.arange(16)
    m = np.stack([1.0 / np.minimum(pos + 1, w) for w in WINDOWS]).astype(np.float32)
    return np.ascontiguousarray(np.broadcast_to(m, (P, 4, 16)))


class Chain:

    def __init__(self, sem):
        self.sem, self.n = sem, 0

    def on(self, eng):
        def chained(ins):
            self.n += 1
            ins.then_inc(self.sem, 1)
            eng.wait_ge(self.sem, self.n)
        return chained


class Core:

    def __init__(self, nc, ctx, dram):
        self.nc, self.ctx, self.d = nc, ctx, dram
        self.sb = lambda n, s, dt=F32, at=None: (at or ctx).enter_context(nc.sbuf_tensor(n, s, dt))
        self.sem = lambda n: ctx.enter_context(nc.semaphore(n))
        self.pp = [ctx.enter_context(nc.psum_tensor(f"banks{j}", [P, 1024], F32)) for j in range(4)]
        self.dve_chain = Chain(self.sem("dve_chain"))
        self.act_chain = Chain(self.sem("act_chain"))
        self.pool_chain = Chain(self.sem("pool_chain"))

    def stage_semaphores(self, ctx):
        own = []

        def give_back():
            self.nc.clear_and_free_semaphores(own)
            self.nc.all_engine_barrier()

        def sem(name):
            own.append(self.nc.alloc_semaphore(name))
            return own[-1]

        ctx.callback(give_back)
        return sem

    def bank(self, n):
        return self.pp[n // 2][:, (n % 2) * 512:(n % 2) * 512 + 512]


def flat(ap):
    return ap.rearrange("p a b -> p (a b)")


def persistent(k):
    k.x = k.sb("x", [P, NT, D])
    k.eps = k.sb("eps", [P, 2])
    k.gate2 = k.sb("gate2", [P, D])
    k.sq = k.sb("sq", [P, NSQ_KEPT, P])
    k.dest = k.sb("dest", [P, NT, TOPK], I32)
    k.gates = k.sb("gates", [P, NT, TOPK])
    k.gateT = k.sb("gateT", [NE, S])
    k.table = k.sb("table", [1, TABLE], I32)


def early_weights(k, weights):
    k.early = k.sb("early", [P, NT * D_IN], at=weights)
    k.n_early = NT * D_IN // (KT * UP)
    k.gu_in = [k.sem(f"gu_in{m}") for m in range(NM)]
    k.early_slab = lambda m: k.early[:, m * KT * UP:(m + 1) * KT * UP]


def stage_front(k, front):
    nc, d = k.nc, k.d
    k.mod = k.sb("mod", [P, 6, D], at=front)
    k.proj = k.early[:].rearrange("p (t n) -> p t n", t=NT)
    WM = 256
    NMOD, NIN = 6 * D // WM, D_IN // WM
    WIDE = D_IN - (NIN - 1) * WM
    HEAD = 2 * D // WM
    with ExitStack() as ctx:
        sb = lambda n, s, dt=F32: k.sb(n, s, dt, at=ctx)
        sem = k.stage_semaphores(ctx)
        hT = sb("hT", [P, 2, KT, S], F32R)
        stage = sb("stage", [P, 3, KT, WIDE])
        w_hi = sb("w_in_hi", [P, 2, KT, WIDE], F32R)
        w_lo = sb("w_in_lo", [P, 2, KT, WIDE], F32R)
        gain = sb("gain", [P, 2, D])
        col = sb("col_c", [P, KT])
        ccol = sb("ccol", [P, 3, KT])
        acc = sb("mod_acc", [P, 2, WM])
        sumsq = sb("sumsq", [P, NT])
        rstd = sb("rstd", [P, NT])
        squares = lambda t: k.proj[:, t, D:2 * D]
        h = lambda t: k.proj[:, t, 2 * D:3 * D]
        col_in = sem("col_in")
        sq_in = sem("sq_in")
        mod_zero = sem("mod_zero")
        bias_in = sem("b_mod_in")
        eps_set = sem("eps_set")
        x_in = sem("x_in")
        gain_in = [sem(f"gain_in{i}") for i in range(2)]
        gain_used = sem("gain_used")
        stage_in = [sem(f"stage_in{i}") for i in range(3)]
        stage_used = sem("stage_used")
        c_exp = sem("c_exp")
        acc_ready = sem("acc_ready_mod")
        mod_ps = sem("mod_ps")
        mod_done = sem("mod_done")
        sumsq_ready = sem("sumsq_ready")
        root_ready = sem("root_ready")
        h_ready = sem("h_ready")
        h_turned = sem("h_turned")
        hT_high = sem("hT_high")
        hT_ready = sem("hT_ready")
        w_high = sem("w_high")
        w_ready = sem("w_ready")
        proj_ps = sem("proj_ps")
        proj_done = sem("proj_done")
        w_in = d["w_in"].rearrange("(k p) n -> p k n", p=P)
        w_mod = d["w_mod"].rearrange("(k p) n -> p k n", p=P)
        width = lambda j: WIDE if j == NIN - 1 else WM
        items = [("mod", j) for j in range(HEAD)] + [("in", 0), ("in", 1)]
        rest = list(range(HEAD, NMOD))
        sums_before = [[], []]
        for j in range(2, NIN):
            sums_before.append([rest.pop(0) for _ in range(2 if len(rest) > NIN - j else 1)])
            items += [("mod", m) for m in sums_before[j]] + [("in", j)]
        items += [("mod", j) for j in rest]
        gains = ["g_pre_mix", "g_post_mix", "g_pre_ffn", "g_post_ffn"]
        four = lambda ap: ap.rearrange("p (a b) -> p a b", b=P)

        with nc.Block() as block:
            @block.sync
            def _(sp):
                sp.dma_start(col[:], d["cols"][:, C0:C0 + KT]).then_inc(col_in, 16)
                for n, (kind, j) in enumerate(items):
                    if n >= 3:
                        sp.wait_ge(stage_used, n - 2)
                    w = w_mod[:, :, j * WM:(j + 1) * WM] if kind == "mod" else \
                        w_in[:, :, j * WM:j * WM + width(j)]
                    sp.dma_start(stage[:, n % 3, :, 0:w.shape[2]], w).then_inc(stage_in[n % 3], 16)

            @block.scalar
            def _(act):
                act.wait_ge(mod_zero, 1)
                act.dma_start(flat(k.mod[0:1]), d["b_mod"]).then_inc(bias_in, 16)
                act.dma_start(k.sq[:], d["square"][:, 0:NSQ_KEPT, :]).then_inc(sq_in, 16)
                act.dma_start(k.x[:], d["x"].rearrange("(t p) n -> p t n", p=P)).then_inc(x_in, 16)
                act.wait_ge(col_in, 16)
                act.activation(ccol[:, 0, :], col[:], ACT.Exp, scale=-1.0).then_inc(c_exp, 1)
                act.wait_ge(eps_set, 2)
                act.wait_ge(x_in, 16)
                for t in range(NT):
                    act.activation(squares(t), k.x[:, t, :], ACT.Square,
                                   accum_out=sumsq[:, t:t + 1]).then_inc(sumsq_ready, 1)
                act.wait_ge(sumsq_ready, NT)
                act.activation(rstd[:], sumsq[:], ACT.Sqrt, scale=1.0 / D,
                               bias=k.eps[:, 0:1]).then_inc(root_ready, 1)

                def mod_copy(j):
                    act.wait_ge(mod_ps, j + 1)
                    act.activation(flat(k.mod[:])[:, j * WM:(j + 1) * WM], k.bank(j % 2)[:, 0:WM], ACT.Copy
                                   ).then_inc(mod_done, 1)

                def high(j):
                    n = items.index(("in", j))
                    act.wait_ge(stage_in[n % 3], 16 * (n // 3 + 1))
                    if j >= 2:
                        act.wait_ge(proj_ps, (j - 1) * NT)
                    act.activation(w_hi[:, j % 2, :, 0:width(j)], stage[:, n % 3, :, 0:width(j)],
                                   ACT.Copy).then_inc(w_high, 1)

                def turned(t):
                    for half in range(2):
                        act.wait_ge(h_turned, 2 * t + half + 1)
                        act.activation(hT[:, 0, 4 * half:4 * half + 4, t * P:(t + 1) * P],
                                       four(k.bank(2 + half)), ACT.Copy).then_inc(hT_high, 1)

                for j in range(HEAD):
                    mod_copy(j)
                high(0)
                for t in range(NT):
                    turned(t)
                    if t == 1:
                        high(1)
                for j in range(NIN):
                    for m in sums_before[j]:
                        mod_copy(m)
                    for t in range(NT):
                        act.wait_ge(proj_ps, j * NT + t + 1)
                        act.activation(k.proj[:, t, j * WM:j * WM + width(j)],
                                       k.bank(4 + t)[:, 0:width(j)], ACT.Copy).then_inc(proj_done, 1)
                    if j + 2 < NIN:
                        high(j + 2)
                for m in rest:
                    mod_copy(m)

            @block.gpsimd
            def _(pool):
                pool.memset(k.mod[:], 0.0).then_inc(mod_zero, 1)
                for n in range(2):
                    pool.dma_start(gain[:, n, :], row(d[gains[n]][0:1, :])).then_inc(gain_in[n], 16)
                for n in range(2):
                    pool.wait_ge(gain_used, n + 1)
                    pool.dma_start(gain[:, n, :], row(d[gains[2 + n]][0:1, :])).then_inc(gain_in[n], 16)

            @block.tensor
            def _(pe):
                def mod_sum(j):
                    pe.wait_ge(acc_ready, j + 1)
                    if j >= 2:
                        pe.wait_ge(mod_done, j - 1)
                    pe.matmul(k.bank(j % 2)[:, 0:WM], k.sq[:, ONES, :], acc[:, j % 2, :], start=True,
                              stop=True).then_inc(mod_ps, 1)

                def project(j):
                    w = width(j)
                    pe.wait_ge(w_ready, j + 1)
                    for t in range(NT):
                        if j:
                            pe.wait_ge(proj_done, (j - 1) * NT + t + 1)
                        tt = slice(t * P, (t + 1) * P)
                        for q in range(KT):
                            for a, b in ((0, w_hi), (0, w_lo), (1, w_hi)):
                                mm = pe.matmul(k.bank(4 + t)[:, 0:w], hT[:, a, q, tt], b[:, j % 2, q, 0:w],
                                               start=(q == 0 and a == 0 and b is w_hi),
                                               stop=(q == KT - 1 and a == 1))
                        mm.then_inc(proj_ps, 1)

                pe.wait_ge(sq_in, 16)
                for j in range(HEAD):
                    mod_sum(j)
                for t in range(NT):
                    pe.wait_ge(h_ready, t + 1)
                    for q in range(KT):
                        if t and q % 4 == 0:
                            pe.wait_ge(hT_ready, 2 * t - 1 + q // 4)
                        mm = pe.transpose(k.bank(2 + q // 4)[:, (q % 4) * P:(q % 4 + 1) * P],
                                          h(t)[:, q * P:(q + 1) * P], k.sq[:, IDENT, :])
                        if q % 4 == 3:
                            mm.then_inc(h_turned, 1)
                pe.wait_ge(hT_ready, 2 * NT)
                project(0)
                project(1)
                for kind, j in items[HEAD + 2:]:
                    if kind == "mod":
                        mod_sum(j)
                    else:
                        project(j)

            @block.vector
            def _(dve):
                chain = k.dve_chain.on(dve)
                dve.memset(k.eps[:, 0:1], EPS).then_inc(eps_set, 1)
                dve.memset(k.eps[:, 1:2], GN_EPS).then_inc(eps_set, 1)
                dve.wait_ge(c_exp, 1)
                chain(dve.tensor_scalar(ccol[:, 1, :], ccol[:, 0, :], 1.0, None, ALU.add))
                chain(dve.reciprocal(ccol[:, 2, :], ccol[:, 1, :]))
                chain(dve.tensor_tensor(ccol[:, 1, :], ccol[:, 2, :], col[:], ALU.mult))

                def mod_products(n, j):
                    dve.wait_ge(stage_in[n % 3], 16 * (n // 3 + 1))
                    if j >= 2:
                        dve.wait_ge(mod_ps, j - 1)
                    a = acc[:, j % 2, :]
                    bias = flat(k.mod[:])[:, j * WM:(j + 1) * WM]
                    for q in range(KT):
                        chain(dve.scalar_tensor_tensor(a, stage[:, n % 3, q, 0:WM], ccol[:, 1, q:q + 1],
                                                       a if q else bias, ALU.mult, ALU.add))
                    dve.sem_inc(acc_ready, 1)
                    dve.sem_inc(stage_used, 1)

                def low(n, j):
                    dve.wait_ge(w_high, j + 1)
                    dve.tensor_tensor(w_lo[:, j % 2, :, 0:width(j)], stage[:, n % 3, :, 0:width(j)],
                                      w_hi[:, j % 2, :, 0:width(j)].bitcast(F32), ALU.subtract
                                      ).then_inc(w_ready, 1)
                    dve.wait_ge(w_ready, j + 1)
                    dve.sem_inc(stage_used, 1)

                def turned_low(t):
                    for half in range(2):
                        dve.wait_ge(hT_high, 2 * t + half + 1)
                        at = (slice(4 * half, 4 * half + 4), slice(t * P, (t + 1) * P))
                        dve.tensor_tensor(hT[:, 1, at[0], at[1]], four(k.bank(2 + half)),
                                          hT[:, 0, at[0], at[1]].bitcast(F32), ALU.subtract
                                          ).then_inc(hT_ready, 1)

                dve.wait_ge(bias_in, 16)
                for j in range(HEAD):
                    mod_products(j, j)
                dve.wait_ge(mod_done, HEAD)
                dve.wait_ge(gain_in[0], 16)
                dve.scalar_tensor_tensor(k.mod[:, 1, :], k.mod[:, 1, :], 1.0, gain[:, 0, :],
                                         ALU.add, ALU.mult).then_inc(gain_used, 1)
                dve.wait_ge(root_ready, 1)
                chain(dve.reciprocal(rstd[:], rstd[:]))
                dve.wait_ge(gain_used, 1)
                for t in range(NT):
                    chain(dve.scalar_tensor_tensor(h(t), k.x[:, t, :], rstd[:, t:t + 1],
                                                   k.mod[:, 1, :], ALU.mult, ALU.mult))
                    dve.tensor_tensor(h(t), h(t), k.mod[:, 0, :], ALU.add).then_inc(h_ready, 1)
                    if t:
                        turned_low(t - 1)
                    if t in (0, 2):
                        low(HEAD + t // 2, t // 2)
                turned_low(NT - 1)
                for n, (kind, j) in list(enumerate(items))[HEAD + 2:]:
                    if kind == "in":
                        low(n, j)
                        continue
                    mod_products(n, j)
                    if j == NMOD // 2 + 2:
                        dve.wait_ge(gain_in[1], 16)
                        dve.wait_ge(mod_done, NMOD // 2)
                        dve.tensor_tensor(k.mod[:, 2, :], k.mod[:, 2, :], gain[:, 1, :],
                                          ALU.mult).then_inc(gain_used, 1)
                dve.wait_ge(mod_done, NMOD)
                dve.wait_ge(gain_in[0], 32)
                dve.scalar_tensor_tensor(k.mod[:, 4, :], k.mod[:, 4, :], 1.0, gain[:, 0, :],
                                         ALU.add, ALU.mult).then_inc(gain_used, 1)
                dve.wait_ge(gain_in[1], 32)
                dve.tensor_tensor(k.gate2[:], k.mod[:, 5, :], gain[:, 1, :], ALU.mult).then_inc(gain_used, 1)


def stage_mixers(k, front):
    k.cat = k.sb("cat", [P, NT, D], at=front)
    k.w_out = k.sb("w_out", [P, KT, D], at=front)
    k.w_out_in = k.sem("w_out_in")
    attention(k)
    linear_attention(k)


def attention(k):
    nc, d = k.nc, k.d
    half = DA // 2
    units = [(i, h) for i in range(NT) for h in range(HA)]
    NU = len(units)
    with ExitStack() as ctx:
        sb = lambda n, s, dt=F32: k.sb(n, s, dt, at=ctx)
        sem = k.stage_semaphores(ctx)
        log_count = sb("log_count", [P, NT, S])
        zeros = k.cat[:, NT - 1, :]
        table = sb("rope_table", [P, NT, 2, 2, half])
        turned = sb("turned", [P, 2, 2 * HA, 2, half])
        cross = sb("cross", [P, 2, 2 * HA, half])
        kT = sb("kT", [P, 4, S])
        qT = sb("qT", [P, 4, 2, S])
        scores = sb("scores", [P, 2, S])
        probs = sb("probs", [P, 2, S])
        probsT = sb("probsT", [P, 2, S])
        negmax = sb("negmax", [P, NU])
        rowsum = sb("rowsum", [P, NU])
        inv = sb("inv", [P, NU])
        const_in = sem("attn_const_in")
        zeros_set = sem("zeros_set")
        zeros_out = sem("zeros_out")
        qT_zero = sem("qT_zero")
        rope_done = sem("rope_done")
        turn_ps = sem("turn_ps")
        qkT_ready = sem("qkT_ready")
        scores_ps = sem("scores_ps")
        scores_masked = sem("scores_masked")
        probs_ready = sem("probs_ready")
        probsT_ps = sem("probsT_ps")
        probsT_ready = sem("probsT_ready")
        pv_done = sem("pv_done")
        cat_ready = sem("cat_ready")

        with nc.Block() as block:
            @block.sync
            def _(sp):
                sp.dma_start(table[:], d["rope"]).then_inc(const_in, 16)
                sp.dma_start(log_count[:], d["log_count"]).then_inc(const_in, 16)
                sp.wait_ge(zeros_set, 1)
                sp.dma_start(d["expert_rows"].rearrange("(b p) n -> p b n", p=P)[:, NE:, :],
                             zeros.unsqueeze(1).broadcast_to([P, EXTRA, D])).then_inc(zeros_out, 16)
                sp.dma_start(k.w_out[:], d["w_out"].rearrange("(k p) n -> p k n", p=P)).then_inc(k.w_out_in, 16)
                sp.wait_ge(zeros_out, 16)

            @block.vector
            def _(dve):
                chain = k.dve_chain.on(dve)
                dve.memset(zeros, 0.0).then_inc(zeros_set, 1)
                for head in range(2):
                    other = slice((1 - head) * DA, (2 - head) * DA)
                    dve.memset(qT[other, :, head, :], 0.0).then_inc(qT_zero, 1)

                def finish_tile(dve, chain, i):
                    a, b = i * HA, (i + 1) * HA
                    dve.wait_ge(pv_done, b)
                    chain(dve.reciprocal(inv[:, a:b], rowsum[:, a:b]))
                    dve.tensor_tensor(k.cat[:, i, 0:HA * DA].rearrange("p (h n) -> p h n", h=HA),
                                      k.bank(6 + i % 2).rearrange("p (h n) -> p h n", h=HA),
                                      inv[:, a:b].unsqueeze(2).broadcast_to([P, HA, DA]),
                                      ALU.mult).then_inc(cat_ready, 1)

                dve.wait_ge(const_in, 32)
                for t in range(NT):
                    if t >= 2:
                        dve.wait_ge(turn_ps, 2 * (t - 1))
                    x = k.proj[:, t, 0:2 * HA * DA].rearrange("p (h two n) -> p h two n", two=2, n=half)
                    cs = [table[:, t, :, c, :].unsqueeze(2).broadcast_to([P, 2, HA, half]) for c in range(2)]
                    grouped = lambda ap: ap.rearrange("p (q h) n -> p q h n", q=2)
                    out = turned[:, t % 2]
                    dve.tensor_tensor(grouped(out[:, :, 0, :]), grouped(x[:, :, 0, :]), cs[0], ALU.mult)
                    dve.tensor_tensor(grouped(cross[:, 0]), grouped(x[:, :, 1, :]), cs[1], ALU.mult)
                    dve.tensor_tensor(grouped(out[:, :, 1, :]), grouped(x[:, :, 1, :]), cs[0], ALU.mult)
                    chain(dve.tensor_tensor(grouped(cross[:, 1]), grouped(x[:, :, 0, :]), cs[1], ALU.mult))
                    dve.tensor_tensor(out[:, :, 0, :], out[:, :, 0, :], cross[:, 0], ALU.subtract)
                    chain(dve.tensor_tensor(out[:, :, 1, :], out[:, :, 1, :], cross[:, 1], ALU.add))
                    dve.sem_inc(rope_done, 1)
                for u, (i, h) in enumerate(units):
                    n = (i + 1) * P
                    dve.wait_ge(scores_ps, u + 1)
                    if u >= 2:
                        dve.wait_ge(probs_ready, u - 1)
                    dve.tensor_tensor_reduce(scores[:, u % 2, 0:n], k.bank(2 + u % 2)[:, 0:n],
                                             log_count[:, i, 0:n], -1.0, 1e30, ALU.add, ALU.min,
                                             negmax[:, u:u + 1]).then_inc(scores_masked, 1)
                    if h == 1 and i:
                        finish_tile(dve, chain, i - 1)
                dve.wait_ge(zeros_out, 16)
                finish_tile(dve, chain, NT - 1)

            @block.scalar
            def _(act):
                for t in range(NT):
                    for part in range(2):
                        act.wait_ge(turn_ps, 2 * t + part + 1)
                        src = k.bank(part).rearrange("p (a b) -> p a b", b=P)
                        if part:
                            act.activation(kT[:, :, t * P:(t + 1) * P], src, ACT.Copy).then_inc(qkT_ready, 1)
                        else:
                            for head in range(2):
                                r = slice(head * DA, (head + 1) * DA)
                                act.activation(qT[r, :, head, t * P:(t + 1) * P], src[r],
                                               ACT.Copy).then_inc(qkT_ready, 1)
                for u in range(NU + 1):
                    if u < NU:
                        n = (units[u][0] + 1) * P
                        act.wait_ge(scores_masked, u + 1)
                        if u >= 2:
                            act.wait_ge(probsT_ps, u - 1)
                        act.activation(probs[:, u % 2, 0:n], scores[:, u % 2, 0:n], ACT.Exp, scale=-1.0,
                                       bias=negmax[:, u:u + 1],
                                       accum_out=rowsum[:, u:u + 1]).then_inc(probs_ready, 1)
                    if u >= 1:
                        v = u - 1
                        n = (units[v][0] + 1) * P
                        act.wait_ge(probsT_ps, v + 1)
                        if v >= 2:
                            act.wait_ge(pv_done, v - 1)
                        act.activation(probsT[:, v % 2, 0:n], k.bank(4 + v % 2)[:, 0:n],
                                       ACT.Copy).then_inc(probsT_ready, 1)

            @block.tensor
            def _(pe):
                for t in range(NT):
                    pe.wait_ge(rope_done, t + 1)
                    for part in range(2):
                        if t:
                            pe.wait_ge(qkT_ready, 3 * (t - 1) + part + 2)
                        for q in range(4):
                            c = 4 * part + q
                            src = turned[:, t % 2].rearrange("p h two n -> p (h two n)")[:, c * P:(c + 1) * P]
                            mm = pe.transpose(k.bank(part)[:, q * P:(q + 1) * P], src, k.sq[:, IDENT, :])
                        mm.then_inc(turn_ps, 1)
                pe.wait_ge(qkT_ready, 3 * NT)
                pe.wait_ge(qT_zero, 2)
                for u in range(NU + 2):
                    if u < NU:
                        i, h = units[u]
                        if u >= 2:
                            pe.wait_ge(scores_masked, u - 1)
                        pe.matmul(k.bank(2 + u % 2)[:, 0:(i + 1) * P],
                                  qT[:, h // 2, h % 2, i * P:(i + 1) * P], kT[:, h // 2, 0:(i + 1) * P],
                                  start=True, stop=True).then_inc(scores_ps, 1)
                    if 1 <= u <= NU:
                        v = u - 1
                        i = units[v][0]
                        pe.wait_ge(probs_ready, v + 1)
                        if v >= 2:
                            pe.wait_ge(probsT_ready, v - 1)
                        for j in range(i + 1):
                            mm = pe.transpose(k.bank(4 + v % 2)[:, j * P:(j + 1) * P],
                                              probs[:, v % 2, j * P:(j + 1) * P], k.sq[:, IDENT, :])
                        mm.then_inc(probsT_ps, 1)
                    if u >= 2:
                        v = u - 2
                        i, h = units[v]
                        pe.wait_ge(probsT_ready, v + 1)
                        if h == 0 and i >= 2:
                            pe.wait_ge(cat_ready, i - 1)
                        wide = min(2 * DA, (HA - h) * DA)
                        for j in range(i + 1):
                            mm = pe.matmul(k.bank(6 + i % 2)[:, h * DA:h * DA + wide],
                                           probsT[:, v % 2, j * P:(j + 1) * P],
                                           k.proj[:, j, VA + h * DA:VA + h * DA + wide],
                                           start=(j == 0), stop=(j == i))
                        mm.then_inc(pv_done, 1)


def linear_attention(k):
    nc, d = k.nc, k.d
    KW, VW = HG * DK, HG * DV
    NCH = S // CH
    with ExitStack() as ctx:
        sb = lambda n, s, dt=F32: k.sb(n, s, dt, at=ctx)
        sem = k.stage_semaphores(ctx)
        lrT = sb("lrT", [32, S])
        w_lr = sb("w_lr", [32, KW])
        g_gla = sb("g_gla", [P, DV])
        la = sb("la", [P, NT, KW])
        tmp = sb("gla_tmp", [P, NT * KW])
        grow = sb("grow", [P, 3, NT * KW])
        qd = sb("qd", [P, NT, KW])
        kd = sb("kd", [P, NT, KW])
        kl = sb("kl", [P, NT, KW])
        qkdT = sb("qkdT", [P, 4, S])
        decay = sb("decay", [P, 2, NCH])
        att = sb("gla_att", [P, 2, HG, P])
        state = sb("gla_state", [P, NCH, 2, DV])
        junk = sb("gla_junk", [P, DV])
        sumsq = sb("gla_sumsq", [P, NT * HG])
        rstd = sb("gla_rstd", [P, NT * HG])
        const_in = sem("gla_const_in")
        lr_set = sem("lr_set")
        lr_ps = sem("lr_ps")
        lr_ready = sem("lr_ready")
        logit_ps = sem("logit_ps")
        abs_ready = sem("abs_ready")
        log_ready = sem("log_ready")
        la_ready = sem("la_ready")
        cum_ps = sem("cum_ps")
        grow_ready = sem("grow_ready")
        qk_ready = sem("qk_ready")
        qkT_ps = sem("qkdT_ps")
        qkT_ready = sem("qkdT_ready")
        att_ps = sem("att_ps")
        att_ready = sem("att_ready")
        u_ps = sem("u_ps")
        state_ready = sem("state_ready")
        o_ps = sem("o_ps")
        o_read = sem("o_read")
        root_ready = sem("gla_root")
        silu_ready = sem("silu_ready")

        with nc.Block() as block:
            @block.sync
            def _(sp):
                sp.dma_start(w_lr[0:RANK + 1, :], d["w_gate_lr"]).then_inc(const_in, 16)
                sp.dma_start(g_gla[:], d["g_gla"][0:1, :].partition_broadcast(P).rearrange(
                    "p a n -> p (a n)")).then_inc(const_in, 16)

            @block.tensor
            def _(pe):
                for t in range(NT):
                    mm = pe.transpose(k.bank(0)[0:RANK, t * P:(t + 1) * P], k.proj[:, t, LR:LR + RANK],
                                      k.sq[:, IDENT, :])
                mm.then_inc(lr_ps, 1)
                pe.wait_ge(lr_ready, 1)
                pe.wait_ge(const_in, 32)
                for t in range(NT):
                    mm = pe.matmul(k.pp[1][:, t * KW:(t + 1) * KW], lrT[0:RANK + 1, t * P:(t + 1) * P],
                                   w_lr[0:RANK + 1, :], start=True, stop=True)
                mm.then_inc(logit_ps, 1)
                pe.wait_ge(la_ready, 1)
                for t in range(NT):
                    mm = pe.matmul(k.pp[0][:, t * KW:(t + 1) * KW], k.sq[:, CUM, :], la[:, t, :],
                                   start=True, stop=True)
                mm.then_inc(cum_ps, 1)
                for t in range(NT):
                    mm = pe.matmul(k.pp[2][:, t * KW:(t + 1) * KW], k.sq[:, SUF, :], la[:, t, :],
                                   start=True, stop=True)
                mm.then_inc(cum_ps, 1)
                for t in range(NT):
                    for p in range(2):
                        c = p * NCH + 2 * t
                        mm = pe.matmul(k.bank(6)[:, c:c + 2], la[:, t, p * P:(p + 1) * P],
                                       k.sq[:, BLOCK, 0:P:CH], start=True, stop=True)
                mm.then_inc(cum_ps, 1)
                for t in range(NT):
                    pe.wait_ge(qk_ready, 1)
                    if t >= 2:
                        pe.wait_ge(qkT_ready, t - 1)
                    for q in range(4):
                        src = (qd, kd)[q // 2][:, t, (q % 2) * P:(q % 2 + 1) * P]
                        mm = pe.transpose(k.bank(2 + t % 2)[:, q * P:(q + 1) * P], src, k.sq[:, IDENT, :])
                    mm.then_inc(qkT_ps, 1)
                for t in range(NT):
                    pe.wait_ge(qkT_ready, t + 1)
                    pe.wait_ge(grow_ready, 4)
                    if t:
                        pe.wait_ge(att_ready, 2 * t)
                    for h in range(HG):
                        r = (h % 2) * DK
                        mm = pe.matmul(k.bank(6 + h % 2)[:, h // 2 * P:(h // 2 + 1) * P],
                                       qkdT[r:r + DK, 2 + h // 2, t * P:(t + 1) * P],
                                       qkdT[r:r + DK, h // 2, t * P:(t + 1) * P], start=True, stop=True)
                    mm.then_inc(att_ps, 1)
                    if t:
                        pe.wait_ge(state_ready, 2 * t)
                    for c in range(2):
                        for h in range(HG):
                            r = c * CH
                            o = (h % 2) * DK
                            col = h // 2 * DV
                            mm = pe.matmul(k.bank(4 + c)[o:o + DK, col:col + DV],
                                           kl[r:r + CH, t, h * DK:(h + 1) * DK],
                                           k.proj[r:r + CH, t, VG + h * DV:VG + (h + 1) * DV],
                                           start=True, stop=True)
                    mm.then_inc(u_ps, 1)
                    pe.wait_ge(att_ready, 2 * (t + 1))
                    pe.wait_ge(state_ready, 2 * t + 1)
                    if t:
                        pe.wait_ge(o_read, t)
                    for h in range(HG):
                        out = k.bank(h % 2)[:, h // 2 * DV:(h // 2 + 1) * DV]
                        pe.matmul(out, att[:, t % 2, h, :],
                                  k.proj[:, t, VG + h * DV:VG + (h + 1) * DV], start=True, stop=True)
                        for c in range(2):
                            r = (h % 2) * DK
                            mm = pe.matmul(out[c * CH:(c + 1) * CH, :],
                                           qkdT[r:r + DK, h // 2, t * P + c * CH:t * P + (c + 1) * CH],
                                           state[r:r + DK, 2 * t + c, h // 2, :], start=False,
                                           stop=True, skip_group_check=True)
                    mm.then_inc(o_ps, 1)

            @block.scalar
            def _(act):
                chain = k.act_chain.on(act)
                act.wait_ge(lr_ps, 1)
                act.wait_ge(lr_set, 1)
                act.activation(lrT[0:RANK, :], k.bank(0)[0:RANK, :], ACT.Copy).then_inc(lr_ready, 1)
                act.wait_ge(abs_ready, 1)
                chain(act.activation(tmp[:], tmp[:], ACT.Exp))
                act.activation(tmp[:], tmp[:], ACT.Ln, bias=1.0).then_inc(log_ready, 1)
                act.wait_ge(cum_ps, 1)
                act.activation(grow[:, 0, :], k.pp[0][:, :], ACT.Exp).then_inc(grow_ready, 1)
                act.activation(grow[:, 1, :], k.pp[0][:, :], ACT.Exp, scale=-1.0).then_inc(grow_ready, 1)
                act.wait_ge(cum_ps, 2)
                act.activation(grow[:, 2, :], k.pp[2][:, :], ACT.Exp).then_inc(grow_ready, 1)
                act.wait_ge(cum_ps, 3)
                act.activation(decay[:], k.bank(6)[:, 0:2 * NCH].rearrange("p (a c) -> p a c", a=2), ACT.Exp,
                               scale=1.0 / 16).then_inc(grow_ready, 1)
                for t in range(NT):
                    act.wait_ge(qkT_ps, t + 1)
                    act.activation(qkdT[:, :, t * P:(t + 1) * P],
                                   k.bank(2 + t % 2).rearrange("p (a b) -> p a b", b=P),
                                   ACT.Copy).then_inc(qkT_ready, 1)
                for t in range(NT):
                    act.wait_ge(o_ps, t + 1)
                    for h in range(HG):
                        chain(act.activation(junk[:], k.bank(h % 2)[:, h // 2 * DV:(h // 2 + 1) * DV],
                                             ACT.Square, accum_out=sumsq[:, t * HG + h:t * HG + h + 1]))
                    for b in range(2):
                        ins = act.activation(
                            k.cat[:, t, VW:2 * VW].rearrange("p (h n) -> p h n", h=HG)[:, b::2, :],
                            k.bank(b)[:, 0:2 * DV].rearrange("p (h n) -> p h n", n=DV), ACT.Copy)
                    chain(ins)
                    act.sem_inc(o_read, 1)
                act.activation(rstd[:], sumsq[:], ACT.Sqrt, scale=1.0 / DV,
                               bias=k.eps[:, 0:1]).then_inc(root_ready, 1)
                for t in range(NT):
                    act.activation(k.proj[:, t, RG:RG + VW], k.proj[:, t, RG:RG + VW],
                                   ACT.Silu).then_inc(silu_ready, 1)

            @block.vector
            def _(dve):
                chain = k.dve_chain.on(dve)
                dve.memset(lrT[:], 1.0).then_inc(lr_set, 1)
                dve.memset(state[:, 0], 0.0)
                chain(dve.memset(att[:], 0.0))
                dve.wait_ge(logit_ps, 1)
                chain(dve.tensor_scalar(tmp[:], k.pp[1][:, :], -1.0, None, ALU.mult))
                dve.tensor_tensor(tmp[:], tmp[:], k.pp[1][:, :], ALU.min).then_inc(abs_ready, 1)
                dve.wait_ge(log_ready, 1)
                dve.scalar_tensor_tensor(flat(la[:]), k.pp[1][:, :], 0.0, tmp[:], ALU.min,
                                         ALU.subtract).then_inc(la_ready, 1)
                part = lambda n: grow[:, n, :].rearrange("p (t n) -> p t n", t=NT)
                dve.wait_ge(grow_ready, 1)
                dve.scalar_tensor_tensor(qd[:], k.proj[:, :, QG:QG + KW], DK ** -0.5, part(0),
                                         ALU.mult, ALU.mult)
                dve.wait_ge(grow_ready, 2)
                chain(dve.tensor_tensor(kd[:], k.proj[:, :, KG:KG + KW], part(1), ALU.mult))
                dve.wait_ge(grow_ready, 3)
                dve.tensor_tensor(kl[:], k.proj[:, :, KG:KG + KW], part(2), ALU.mult).then_inc(qk_ready, 1)
                mask = k.sq[:, LE, :].bitcast(U32).unsqueeze(1).broadcast_to([P, HG // 2, P])
                dve.wait_ge(grow_ready, 4)
                for t in range(NT):
                    dve.wait_ge(att_ps, t + 1)
                    if t >= 2:
                        dve.wait_ge(o_ps, t - 1)
                    for b in range(2):
                        dve.copy_predicated(att[:, t % 2, b::2, :], mask,
                                            k.bank(6 + b)[:, 0:2 * P].rearrange("p (a b) -> p a b", b=P)
                                            ).then_inc(att_ready, 1)
                    dve.wait_ge(u_ps, t + 1)
                    for c in range(2):
                        n = 2 * t + c
                        if n + 1 < NCH:
                            for p in range(2):
                                ins = dve.scalar_tensor_tensor(
                                    state[:, n + 1, p, :], state[:, n, p, :], decay[:, p, n:n + 1],
                                    k.bank(4 + c)[:, p * DV:(p + 1) * DV],
                                    ALU.mult, ALU.add)
                            chain(ins)
                            dve.sem_inc(state_ready, 1)
                dve.wait_ge(root_ready, 1)
                chain(dve.reciprocal(rstd[:], rstd[:]))
                for t in range(NT):
                    o = k.cat[:, t, VW:2 * VW].rearrange("p (h n) -> p h n", h=HG)
                    scale = rstd[:, t * HG:(t + 1) * HG].unsqueeze(2).broadcast_to([P, HG, DV])
                    gain = g_gla[:].unsqueeze(1).broadcast_to([P, HG, DV])
                    chain(dve.tensor_tensor(o, o, scale, ALU.mult))
                    chain(dve.tensor_tensor(o, o, gain, ALU.mult))
                    dve.wait_ge(silu_ready, t + 1)
                    chain(dve.tensor_tensor(k.cat[:, t, VW:2 * VW], k.cat[:, t, VW:2 * VW],
                                            k.proj[:, t, RG:RG + VW], ALU.mult))


def row(ap):
    return ap.partition_broadcast(P).rearrange("p a n -> p (a n)")


def stage_router(k, front):
    nc, d = k.nc, k.d
    with ExitStack() as ctx:
        sb = lambda n, s, dt=F32: k.sb(n, s, dt, at=ctx)
        sem = k.stage_semaphores(ctx)
        turned = sb("catT", [P, KT, S])
        h2 = sb("h2", [P, NT, D])
        scaled = sb("scaled", [P, D])
        junk = sb("router_junk", [P, D])
        sumsq = sb("router_sumsq", [P, 2, NT])
        rstd = sb("router_rstd", [P, 2, NT])
        w_router = sb("w_router", [P, KT, NE])
        b_router = sb("b_router", [P, NE])
        count = sb("count_const", [P, NBLK + 1])
        token = sb("token", [P, NT], I32)
        none = sb("none", [P, NBLK + 1], I32)
        logits = sb("logits", [P, NT, NE])
        top = sb("top", [P, NT, 8])
        index = sb("index", [P, NT, 8], U32)
        indexf = sb("indexf", [P, NT, 8])
        onehot = sb("onehot", [P, NT, TOPK, NE])
        work = sb("route_work", [P, NT, TOPK, NE])
        chosen = sb("chosen", [P, NT, NE])
        gate_e = sb("gate_e", [P, NT, NE])
        gsum = sb("gsum", [P, NT])
        rank = sb("rank", [P, NT, NE])
        ones = sb("ones_row", [P, NE])
        cnt = sb("cnt", [P, 3, NE])
        cmp = sb("cmp", [P, NBLK + 1, NE])
        destf = sb("destf", [P, 3, NT, TOPK])
        listed = sb("listed", [P, NT, TOPK], I32)
        plan = sb("plan", [P, TABLE])
        const_in = sem("router_const_in")
        cat_ps = sem("cat_ps")
        catT_ready = sem("catT_ready")
        y_ps = sem("y_ps")
        y_sumsq = sem("y_sumsq")
        x_ready = sem("resid_ready")
        x_sumsq = sem("x_sumsq")
        y_read = sem("y_read")
        h2_ready = sem("h2_ready")
        h2_out = sem("h2_out")
        h2_ps = sem("h2_ps")
        h2T_ready = sem("h2T_ready")
        logits_ps = sem("logits_ps")
        gate_diff = sem("gate_diff")
        gate_exp = sem("gate_exp")
        chosen_ready = sem("chosen_ready")
        rank_ps = sem("rank_ps")
        gateT_ps = sem("gateT_ps")
        none_set = sem("none_set")
        none_out = sem("none_out")
        dest_ready = sem("dest_ready")
        table_ready = sem("table_ready")
        lists_out = sem("lists_out")
        gateT_ready = sem("gateT_ready")

        with nc.Block() as block:
            @block.sync
            def _(sp):
                sp.dma_start(w_router[:], d["router_w"].rearrange("(k p) n -> p k n", p=P)).then_inc(const_in, 16)
                sp.dma_start(b_router[:], row(d["router_b"][0:1, :])).then_inc(const_in, 16)
                sp.dma_start(count[:], d["count"]).then_inc(const_in, 16)
                sp.dma_start(token[:], d["token"]).then_inc(const_in, 16)
                for m in range(k.n_early):
                    sp.dma_start(k.early_slab(m), d["w_gate_up"][m * P:(m + 1) * P, :]).then_inc(k.gu_in[m], 16)
                sp.wait_ge(none_set, 1)
                sp.dma_start(d["slot_token"].rearrange("(p n) one -> p (n one)", p=SLOTS),
                             none[:]).then_inc(none_out, 16)
                for t in range(NT):
                    sp.wait_ge(h2_ready, t + 1)
                    sp.dma_start(d["h2"][t * P:(t + 1) * P, :], h2[:, t, :]).then_inc(h2_out, 16)
                sp.wait_ge(h2_out, 16 * NT)

            @block.gpsimd
            def _(pool):
                pool.memset(none[:], 0).then_inc(none_set, 1)
                pool.wait_ge(none_out, 16)
                pool.wait_ge(const_in, 64)
                pool.wait_ge(dest_ready, 1)
                for t in range(NT):
                    for c in range(TOPK):
                        pool.indirect_dma_start(
                            out=d["slot_token"],
                            out_offset=bass.IndirectOffsetOnAxis(ap=listed[:, t, c:c + 1], axis=0),
                            in_=token[:, t:t + 1], in_offset=None).then_inc(lists_out, 16)
                pool.wait_ge(lists_out, 16 * NT * TOPK)

            @block.tensor
            def _(pe):
                ident = k.sq[:, IDENT, :]

                def turn_and_project(t):
                    if t:
                        pe.wait_ge(catT_ready, 2 * t)
                    for q in range(KT):
                        mm = pe.transpose(k.bank(q // 4)[:, (q % 4) * P:(q % 4 + 1) * P],
                                          k.cat[:, t, q * P:(q + 1) * P], ident)
                        if q % 4 == 3:
                            mm.then_inc(cat_ps, 1)
                    pe.wait_ge(catT_ready, 2 * (t + 1))
                    if t >= 2:
                        pe.wait_ge(y_read, t - 1)
                    for n in range(2):
                        for q in range(KT):
                            mm = pe.matmul(k.pp[1 + t % 2][:, n * 512:(n + 1) * 512],
                                           turned[:, q, t * P:(t + 1) * P],
                                           k.w_out[:, q, n * 512:(n + 1) * 512],
                                           start=(q == 0), stop=(q == KT - 1))
                    mm.then_inc(y_ps, 1)

                def turn_h2(t):
                    pe.wait_ge(h2_ready, t + 1)
                    if t:
                        pe.wait_ge(h2T_ready, 2 * t)
                    for q in range(KT):
                        mm = pe.transpose(k.bank(6 + q // 4)[:, (q % 4) * P:(q % 4 + 1) * P],
                                          h2[:, t, q * P:(q + 1) * P], ident)
                        if q % 4 == 3:
                            mm.then_inc(h2_ps, 1)

                pe.wait_ge(k.w_out_in, 16)
                turn_and_project(0)
                for t in range(1, NT):
                    turn_and_project(t)
                    turn_h2(t - 1)
                turn_h2(NT - 1)
                pe.wait_ge(h2T_ready, 2 * NT)
                pe.wait_ge(const_in, 64)
                for t in range(NT):
                    for q in range(KT):
                        mm = pe.matmul(k.bank(0)[:, t * NE:(t + 1) * NE], turned[:, q, t * P:(t + 1) * P],
                                       w_router[:, q, :], start=(q == 0), stop=(q == KT - 1))
                mm.then_inc(logits_ps, 1)
                pe.wait_ge(chosen_ready, 1)
                for t in range(NT):
                    for s in range(t + 1):
                        pe.matmul(k.bank(1)[:, t * NE:(t + 1) * NE],
                                  k.sq[:, BEFORE if s == t else ONES, :], chosen[:, s, :],
                                  start=(s == 0), stop=(s == t))
                for s in range(NT):
                    mm = pe.matmul(k.bank(1)[:, NT * NE:(NT + 1) * NE], k.sq[:, ONES, :], chosen[:, s, :],
                                   start=(s == 0), stop=(s == NT - 1))
                mm.then_inc(rank_ps, 1)
                pe.wait_ge(gateT_ready, 1)
                for t in range(NT):
                    mm = pe.transpose(k.bank(2)[0:NE, t * P:(t + 1) * P], gate_e[:, t, :], ident)
                mm.then_inc(gateT_ps, 1)

            @block.scalar
            def _(act):
                def root(part, t):
                    chain(act.activation(rstd[:, part, t:t + 1], sumsq[:, part, t:t + 1], ACT.Sqrt,
                                         scale=1.0 / D, bias=k.eps[:, 0:1]))

                def evac(bank0, ps, ready, t):
                    for part in range(2):
                        act.wait_ge(ps, 2 * t + part + 1)
                        act.activation(turned[:, 4 * part:4 * part + 4, t * P:(t + 1) * P],
                                       k.bank(bank0 + part).rearrange("p (a b) -> p a b", b=P),
                                       ACT.Copy).then_inc(ready, 1)

                chain = k.act_chain.on(act)
                for t in range(NT + 1):
                    if t < NT:
                        evac(0, cat_ps, catT_ready, t)
                    if t < NT:
                        act.wait_ge(y_ps, t + 1)
                        chain(act.activation(junk[:], k.pp[1 + t % 2][:, :], ACT.Square,
                                             accum_out=sumsq[:, 0, t:t + 1]))
                        root(0, t)
                        act.sem_inc(y_sumsq, 1)
                        act.wait_ge(x_ready, t + 1)
                        chain(act.activation(junk[:], k.x[:, t, :], ACT.Square,
                                             accum_out=sumsq[:, 1, t:t + 1]))
                        root(1, t)
                        act.sem_inc(x_sumsq, 1)
                    if t:
                        evac(6, h2_ps, h2T_ready, t - 1)
                act.wait_ge(gate_diff, 1)
                act.activation(k.gates[:], k.gates[:], ACT.Exp).then_inc(gate_exp, 1)
                act.wait_ge(gateT_ps, 1)
                act.activation(k.gateT[:], k.bank(2)[0:NE, :], ACT.Copy)

            @block.vector
            def _(dve):
                chain = k.dve_chain.on(dve)
                for t in range(NT):
                    dve.wait_ge(y_sumsq, t + 1)
                    chain(dve.reciprocal(rstd[:, 0, t:t + 1], rstd[:, 0, t:t + 1]))
                    chain(dve.scalar_tensor_tensor(scaled[:], k.pp[1 + t % 2][:, :], rstd[:, 0, t:t + 1],
                                                   k.mod[:, 2, :], ALU.mult, ALU.mult))
                    dve.sem_inc(y_read, 1)
                    dve.tensor_tensor(k.x[:, t, :], k.x[:, t, :], scaled[:], ALU.add).then_inc(x_ready, 1)
                    dve.wait_ge(x_sumsq, t + 1)
                    chain(dve.reciprocal(rstd[:, 1, t:t + 1], rstd[:, 1, t:t + 1]))
                    chain(dve.scalar_tensor_tensor(h2[:, t, :], k.x[:, t, :], rstd[:, 1, t:t + 1],
                                                   k.mod[:, 4, :], ALU.mult, ALU.mult))
                    dve.tensor_tensor(h2[:, t, :], h2[:, t, :], k.mod[:, 3, :], ALU.add).then_inc(h2_ready, 1)
                dve.wait_ge(const_in, 64)
                dve.wait_ge(logits_ps, 1)
                over_t = lambda ap, n=NT: ap.unsqueeze(1).broadcast_to([P, n, NE])
                chain(dve.tensor_tensor(logits[:], k.bank(0)[:, 0:NT * NE].rearrange("p (t e) -> p t e", e=NE),
                                        over_t(b_router[:]), ALU.add))
                for t in range(NT):
                    ins = dve.max(top[:, t, :], logits[:, t, :])
                chain(ins)
                for t in range(NT):
                    ins = dve.max_index(index[:, t, :], top[:, t, :], logits[:, t, :])
                chain(ins)
                chain(dve.tensor_copy(indexf[:], index[:]))
                for t in range(NT):
                    ins = dve.tensor_tensor(onehot[:, t], over_t(count[:, 0:NE], TOPK),
                                            indexf[:, t, 0:TOPK].unsqueeze(2).broadcast_to([P, TOPK, NE]),
                                            ALU.is_equal)
                dve.tensor_tensor(k.gates[:], top[:, :, 0:TOPK], top[:, :, 0:1].broadcast_to([P, NT, TOPK]),
                                  ALU.subtract).then_inc(gate_diff, 1)
                chain(dve.memset(ones[:], 1.0))
                for t in range(NT):
                    ins = dve.tensor_reduce(chosen[:, t, :], onehot[:, t].rearrange("p c e -> p e c"), AX.X,
                                            ALU.add)
                ins.then_inc(chosen_ready, 1)
                dve.wait_ge(gate_exp, 1)
                chain(dve.tensor_reduce(gsum[:], k.gates[:], AX.X, ALU.add))
                chain(dve.reciprocal(gsum[:], gsum[:]))
                chain(dve.tensor_tensor(k.gates[:], k.gates[:],
                                        gsum[:].unsqueeze(2).broadcast_to([P, NT, TOPK]), ALU.mult))
                for t in range(NT):
                    ins = dve.tensor_tensor(work[:, t], onehot[:, t],
                                            k.gates[:, t, :].unsqueeze(2).broadcast_to([P, TOPK, NE]), ALU.mult)
                chain(ins)
                for t in range(NT):
                    ins = dve.tensor_reduce(gate_e[:, t, :], work[:, t].rearrange("p c e -> p e c"), AX.X,
                                            ALU.add)
                ins.then_inc(gateT_ready, 1)
                dve.wait_ge(rank_ps, 1)
                dve.tensor_copy(rank[:], k.bank(1)[:, 0:NT * NE].rearrange("p (t e) -> p t e", e=NE))
                total = k.bank(1)[:, NT * NE:(NT + 1) * NE]
                chain(dve.tensor_scalar(cnt[:, 0, :], total, 0.0, None, ALU.is_gt))
                for j in range(1, -(-S // SLOTS)):
                    chain(dve.scalar_tensor_tensor(cnt[:, 0, :], total, float(SLOTS * j), cnt[:, 0, :],
                                                   ALU.is_gt, ALU.add))
                chain(dve.tensor_scalar(cnt[:, 0, 0:1], cnt[:, 0, 0:1], 1.0, None, ALU.max))
                chain(dve.tensor_tensor_scan(cnt[:, 1, :], ones[:], cnt[:, 0, :], 0.0, ALU.mult, ALU.add))
                chain(dve.tensor_tensor(cnt[:, 2, :], cnt[:, 1, :], cnt[:, 0, :], ALU.subtract))
                for part, of_expert in enumerate((lambda t: rank[:, t, :], lambda t: cnt[:, 2, :])):
                    for t in range(NT):
                        ins = dve.tensor_tensor(work[:, t], onehot[:, t], over_t(of_expert(t), TOPK), ALU.mult)
                    chain(ins)
                    for t in range(NT):
                        ins = dve.tensor_reduce(destf[:, part, t, :], work[:, t], AX.X, ALU.add)
                    chain(ins)
                chain(dve.tensor_scalar(destf[:, 2], destf[:, 0], float(SLOTS), None, ALU.is_ge))
                for j in range(2, -(-S // SLOTS)):
                    chain(dve.scalar_tensor_tensor(destf[:, 2], destf[:, 0], float(SLOTS * j), destf[:, 2],
                                                   ALU.is_ge, ALU.add))
                chain(dve.scalar_tensor_tensor(destf[:, 0], destf[:, 2], -float(SLOTS), destf[:, 0],
                                               ALU.mult, ALU.add))
                chain(dve.tensor_tensor(destf[:, 1], destf[:, 1], destf[:, 2], ALU.add))
                chain(dve.scalar_tensor_tensor(listed[:], destf[:, 0], float(NBLK + 1), destf[:, 1],
                                               ALU.mult, ALU.add))
                dve.sem_inc(dest_ready, 1)
                dve.scalar_tensor_tensor(k.dest[:], destf[:, 1], float(SLOTS), destf[:, 0], ALU.mult, ALU.add)
                many = NBLK + 1
                chain(dve.tensor_tensor(cmp[:], cnt[:, 1, :].unsqueeze(1).broadcast_to([P, many, NE]),
                                        count[:].unsqueeze(2).broadcast_to([P, many, NE]), ALU.is_le))
                chain(dve.tensor_reduce(plan[:, 0:many], cmp[:], AX.X, ALU.add))
                chain(dve.tensor_scalar(plan[:, 0:many], plan[:, 0:many], float(NE - 1), None, ALU.min))
                dve.memset(plan[:, many:many + 1], 1.0)
                chain(dve.tensor_tensor(plan[:, many + 1:2 * many], plan[:, 1:many], plan[:, 0:many - 1],
                                        ALU.not_equal))
                chain(dve.tensor_scalar(plan[:, 2 * many:3 * many], plan[:, many:2 * many], 0.0, None,
                                        ALU.is_equal))
                chain(dve.tensor_scalar(plan[:, TABLE - 1:TABLE], cnt[:, 1, NE - 1:NE], float(NE), None,
                                        ALU.max))
                chain(dve.tensor_scalar(plan[:, TABLE - 2:TABLE - 1], plan[:, TABLE - 1:TABLE], -1.0, None,
                                        ALU.add))
                chain(dve.tensor_copy(k.table[:], plan[0:1, :]))


def stage_experts(k):
    nc, d = k.nc, k.d
    HALF = KT // 2 * UP
    with ExitStack() as ctx:
        sb = lambda n, s, dt=F32: k.sb(n, s, dt, at=ctx)
        sem = k.stage_semaphores(ctx)
        late = sb("wgu", [P, NM - k.n_early, KT * UP])
        wgu = [k.early_slab(m) if m < k.n_early else late[:, m - k.n_early, :] for m in range(NM)]
        wd = sb("wd", [P, NM, D])
        wgu_hi = sb("wgu_hi", [P, 2, KT * UP], F32R)
        wgu_lo = sb("wgu_lo", [P, 2, KT * UP], F32R)
        wd_hi = sb("wd_hi", [P, 2, D], F32R)
        wd_lo = sb("wd_lo", [P, 2, D], F32R)
        bias = sb("bias", [P, NM * UP], F32R)
        picked = sb("picked", [P, 1])
        pick = sb("pick", [P, P], F32R)
        slots = sb("slots", [SLOTS, NBLK + 1], I32)
        slot = sb("slot", [P, 1], I32)
        rows = sb("rows", [P, D])
        rowsT = sb("rowsT", [P, 2, KT, P], F32R)
        glu = sb("glu", [P, 2, P])
        lin = sb("lin", [P, 2, P])
        prod = sb("prod", [P, 2, P])
        sig = sb("sig", [P, 2, P])
        hidden = sb("hidden", [P, 2, P])
        hT = sb("hiddenT", [P, 2, 2, P], F32R)
        y = sb("y_rows", [P, D])
        gu_in = k.gu_in
        wd_in = [sem(f"wd_in{m}") for m in range(NM)]
        bias_in = sem("bias_in")
        bias_high = sem("bias_high")
        bias_ready = sem("bias_ready")
        slab_free = sem("slab_free")
        picked_in = sem("picked_in")
        pick_ready = sem("pick_ready")
        slots_in = sem("slots_in")
        slot_ready = sem("slot_ready")
        slot_seen = sem("slot_seen")
        rows_in = sem("rows_in")
        rows_ps = sem("rows_ps")
        rowsT_high = sem("rowsT_high")
        rowsT_ready = sem("rowsT_ready")
        gu_high = sem("gu_high")
        gu_ready = sem("gu_ready")
        wd_high = sem("wd_high")
        wd_ready = sem("wd_ready")
        half_up_ps = sem("half_up_ps")
        up_ps = sem("up_ps")
        up_read = sem("up_read")
        glu_ready = sem("glu_ready")
        sig_ready = sem("sig_ready")
        prod_ready = sem("prod_ready")
        hidden_ready = sem("hidden_ready")
        hiddenT_ps = sem("hiddenT_ps")
        hiddenT_high = sem("hiddenT_high")
        hiddenT_ready = sem("hiddenT_ready")
        down_ps = sem("down_ps")
        y_read = sem("expert_y_read")
        y_out = sem("expert_y_out")
        f = lambda ap: ap.bitcast(F32)
        raw_bias = wgu[NM - 1]

        def blocks_on(eng):
            return eng.value_load(k.table[0:1, TABLE - 1:TABLE], min_val=NE, max_val=NBLK)

        def last_on(eng):
            return eng.value_load(k.table[0:1, TABLE - 2:TABLE - 1], min_val=NE - 1, max_val=NBLK - 1)

        def after(eng, sem, n):
            if not isinstance(n, int) or n > 0:
                eng.wait_ge(sem, n)

        def begun(g):
            return not isinstance(g, int) or g >= 0

        with nc.Block() as block:
            @block.sync
            def _(sp):
                def load_picked(i, e):
                    after(sp, pick_ready, i)
                    sp.dma_start(picked[:], d["picked"][bass.ds(e * P, P), :]).then_inc(picked_in, 16)

                def slabs(i, load_gu, load_wd, store=False):
                    for m in range(NM + 1):
                        if m == NM - 1 and isinstance(i, int) and i == 0:
                            sp.wait_ge(bias_ready, 2)
                        if m < NM:
                            after(sp, gu_ready, 2 * (NM * (i - 1) + m + 1))
                            sp.sem_inc(slab_free, 1)
                            after(sp, gu_in[(m - 3) % NM], 16 * (i + (m >= 3)))
                            if not (isinstance(i, int) and i == 0 and m < k.n_early):
                                load_gu(m)
                        if m == 4 and store:
                            store_rows(i - 1)
                        if m:
                            after(sp, wd_ready, NM * (i - 1) + m)
                            load_wd(m - 1)

                def store_rows(n):
                    sp.wait_ge(y_read, n)
                    sp.dma_start(d["expert_rows"][bass.ds(n * SLOTS - SLOTS, SLOTS), :], y[:]).then_inc(y_out, 16)

                def load(i, e, store=True):
                    rows_of = lambda m: bass.ds((e * NM + m) * P, P)
                    slabs(i, lambda m: sp.dma_start(wgu[m], d["w_gate_up"][rows_of(m), :]
                                                    ).then_inc(gu_in[m], 16),
                          lambda m: sp.dma_start(wd[:, m, :], d["w_down"][rows_of(m), :]
                                                 ).then_inc(wd_in[m], 16), store)

                def expert(i):
                    return sp.value_load(k.table[0:1, bass.ds(i, 1)], min_val=0, max_val=NE - 1)

                sp.dma_start(slots[:], d["slot_token"].rearrange("(p n) one -> p (n one)", p=SLOTS)
                             ).then_inc(slots_in, 16)
                for part in range(2):
                    sp.dma_start(raw_bias[part * NE:(part + 1) * NE, :], d["b_gate_up"]).then_inc(bias_in, 16)
                blocks = blocks_on(sp)
                for i in range(2):
                    e = expert(i)
                    load_picked(i, e)
                    load(i, e, False)
                with sp.Fori(2, blocks) as i:
                    e = expert(i)
                    other = sp.value_load(k.table[0:1, bass.ds(i + (NBLK + 1), 1)], min_val=0, max_val=1)
                    same = sp.value_load(k.table[0:1, bass.ds(i + 2 * (NBLK + 1), 1)], min_val=0, max_val=1)
                    load_picked(i, e)
                    with sp.If(other > 0):
                        load(i, e)
                    with sp.If(same > 0):
                        slabs(i, lambda m: sp.sem_inc(gu_in[m], 16), lambda m: sp.sem_inc(wd_in[m], 16), True)
                load_picked(blocks, NE - 1)
                last = last_on(sp)
                sp.wait_ge(gu_ready, 2 * NM * last + 2)
                sp.sem_inc(gu_in[0], 16)
                store_rows(last)
                store_rows(last + 1)

            @block.gpsimd
            def _(pool):
                blocks = blocks_on(pool)

                def gather(i):
                    after(pool, rows_in, 16 * i)
                    pool.tensor_copy(slot[:], slots[:, bass.ds(i, 1)]).then_inc(slot_ready, 1)
                    after(pool, rows_ps, 2 * i)
                    pool.wait_ge(slot_ready, i + 1)
                    pool.sem_inc(slot_seen, 1)
                    pool.indirect_dma_start(
                        out=rows[:], out_offset=None, in_=d["h2"],
                        in_offset=bass.IndirectOffsetOnAxis(ap=slot[:, 0:1], axis=0)).then_inc(rows_in, 16)

                def split_wd(g, m):
                    if begun(g):
                        pool.wait_ge(wd_high, g + 1)
                        pool.tensor_tensor(wd_lo[:, m % 2, :], wd[:, m, :], f(wd_hi[:, m % 2, :]),
                                           ALU.subtract).then_inc(wd_ready, 1)

                def steps(i):
                    for m in range(NM):
                        split_wd(NM * i + m - 1, (m - 1) % NM)
                        if m == 0:
                            gather(i + 1)

                pool.wait_ge(slots_in, 16)
                gather(0)
                steps(0)
                with pool.Fori(1, blocks) as i:
                    steps(i)
                split_wd(NM * last_on(pool) + (NM - 1), NM - 1)
                pool.wait_ge(rows_in, 16 * blocks + 16)
                pool.wait_ge(picked_in, 16 * blocks + 16)
                pool.wait_ge(y_out, 16 * blocks + 16)

            @block.tensor
            def _(pe):
                blocks = blocks_on(pe)

                def turn_rows(i):
                    pe.wait_ge(rows_in, 16 * i + 16)
                    for q in range(KT):
                        mm = pe.transpose(k.bank(6 + q // 4)[:, (q % 4) * P:(q % 4 + 1) * P],
                                          rows[:, q * P:(q + 1) * P], k.sq[:, IDENT, :])
                        if q % 4 == 3:
                            mm.then_inc(rows_ps, 1)

                def up(g, m, i):
                    after(pe, up_read, g - 1)
                    out = k.bank(m % 2)[:, 0:UP]
                    pe.matmul(out, pick[:], bias[:, m * UP:(m + 1) * UP], start=True, stop=False)
                    for q in range(KT):
                        if q % (KT // 2) == 0:
                            pe.wait_ge(gu_ready, 2 * g + 1 + q // (KT // 2))
                            if m == 0:
                                pe.wait_ge(rowsT_ready, 2 * i + 1 + q // (KT // 2))
                        hi, lo = (w[:, m % 2, q * UP:(q + 1) * UP] for w in (wgu_hi, wgu_lo))
                        pe.matmul(out, rowsT[:, 0, q, :], hi, start=False, stop=False)
                        pe.matmul(out, rowsT[:, 0, q, :], lo, start=False, stop=False)
                        mm = pe.matmul(out, rowsT[:, 1, q, :], hi, start=False, stop=(q == KT - 1))
                        if q == KT // 2 - 1:
                            mm.then_inc(half_up_ps, 1)
                    mm.then_inc(up_ps, 1)

                def turn_hidden(g, m):
                    if begun(g):
                        pe.wait_ge(hidden_ready, g + 1)
                        after(pe, hiddenT_ready, g - 1)
                        pe.transpose(k.bank(2 + m % 2)[:, 0:P], hidden[:, m % 2, :],
                                     k.sq[:, IDENT, :]).then_inc(hiddenT_ps, 1)

                def down(g, m, i):
                    if begun(g):
                        pe.wait_ge(hiddenT_ready, g + 1)
                        pe.wait_ge(wd_ready, g + 1)
                        if m == 0:
                            after(pe, y_read, i)
                        for a, w in ((0, wd_hi), (0, wd_lo), (1, wd_hi)):
                            for n in range(2):
                                mm = pe.matmul(k.bank(4 + n), hT[:, m % 2, a, :],
                                               w[:, m % 2, n * 512:(n + 1) * 512],
                                               start=(m == 0 and a == 0 and w is wd_hi),
                                               stop=(m == NM - 1 and a == 1))
                        mm.then_inc(down_ps, 1)

                def steps(i):
                    pe.wait_ge(pick_ready, i + 1)
                    for m in range(NM):
                        g = NM * i + m
                        if m == NM - 1:
                            turn_rows(i + 1)
                        up(g, m, i)
                        turn_hidden(g - 1, (m - 1) % NM)
                        down(g - 2, (m - 2) % NM, i)

                turn_rows(0)
                pe.wait_ge(bias_ready, 2)
                steps(0)
                with pe.Fori(1, blocks) as i:
                    steps(i)
                last = NM * last_on(pe)
                turn_hidden(last + (NM - 1), NM - 1)
                down(last + (NM - 2), NM - 2, blocks)
                down(last + (NM - 1), NM - 1, blocks)

            @block.scalar
            def _(act):
                blocks = blocks_on(act)

                def sigmoid(g, m):
                    if begun(g):
                        act.wait_ge(glu_ready, g + 1)
                        after(act, hidden_ready, g - 1)
                        act.activation(sig[:, m % 2, :], glu[:, m % 2, :], ACT.Sigmoid,
                                       scale=ALPHA).then_inc(sig_ready, 1)

                def gu_highs(g, m, i):
                    act.wait_ge(gu_in[m], 16 * i + 16)
                    after(act, up_ps, g - 1)
                    for h in range(2):
                        act.activation(wgu_hi[:, m % 2, h * HALF:(h + 1) * HALF],
                                       wgu[m][:, h * HALF:(h + 1) * HALF], ACT.Copy).then_inc(gu_high, 1)

                def wd_highs(g, m, i):
                    if begun(g):
                        act.wait_ge(wd_in[m], 16 * i + 16)
                        after(act, down_ps, g - 1)
                        act.activation(wd_hi[:, m % 2, :], wd[:, m, :], ACT.Copy).then_inc(wd_high, 1)

                def row_highs(i, g=None):
                    for part in range(2):
                        if g is not None:
                            act.wait_ge(up_ps if part else half_up_ps, g + 1)
                        act.wait_ge(rows_ps, 2 * i + part + 1)
                        act.activation(rowsT[:, 0, 4 * part:4 * part + 4, :],
                                       k.bank(6 + part).rearrange("p (a b) -> p a b", b=P),
                                       ACT.Copy).then_inc(rowsT_high, 1)

                def hidden_high(g, m):
                    if begun(g):
                        act.wait_ge(hiddenT_ps, g + 1)
                        after(act, down_ps, g - 1)
                        act.activation(hT[:, m % 2, 0, :], k.bank(2 + m % 2)[:, 0:P],
                                       ACT.Copy).then_inc(hiddenT_high, 1)

                def read_y(i):
                    act.wait_ge(down_ps, NM * i + NM)
                    act.wait_ge(y_out, 16 * i + 16)
                    act.activation(y[:], k.pp[2][:, :], ACT.Copy).then_inc(y_read, 1)

                def steps(i):
                    for m in range(NM):
                        g = NM * i + m
                        before = (m - 1) % NM
                        sigmoid(g - 1, before)
                        if m == 2 and begun(i - 1):
                            read_y(i - 1)
                        gu_highs(g + 1, (m + 1) % NM, i + (m == NM - 1))
                        wd_highs(g - 1, before, i - (m == 0))
                        if m == NM - 1:
                            row_highs(i + 1, g)
                        hidden_high(g - 1, before)

                act.sem_inc(y_out, 16)
                act.wait_ge(bias_in, 32)
                act.wait_ge(bias_ready, 1)
                act.activation(bias[:], raw_bias, ACT.Copy).then_inc(bias_high, 1)
                gu_highs(0, 0, 0)
                row_highs(0)
                steps(0)
                with act.Fori(1, blocks) as i:
                    steps(i)
                last = last_on(act)
                end = NM * last + (NM - 1)
                sigmoid(end, NM - 1)
                wd_highs(end, NM - 1, last)
                hidden_high(end, NM - 1)
                read_y(last)

            @block.vector
            def _(dve):
                blocks = blocks_on(dve)

                def activate(g, m):
                    if begun(g):
                        dve.wait_ge(up_ps, g + 1)
                        dve.tensor_scalar(glu[:, m % 2, :], k.bank(m % 2)[:, 0:P], LIMIT, None,
                                          ALU.min).then_inc(glu_ready, 1)
                        dve.tensor_scalar(lin[:, m % 2, :], k.bank(m % 2)[:, P:UP], LIMIT, -LIMIT,
                                          ALU.min, ALU.max).then_inc(up_read, 1)
                        dve.wait_ge(glu_ready, g + 1)
                        dve.wait_ge(up_read, g + 1)
                        dve.scalar_tensor_tensor(prod[:, m % 2, :], lin[:, m % 2, :], 1.0,
                                                 glu[:, m % 2, :], ALU.add, ALU.mult).then_inc(prod_ready, 1)

                def finish_hidden(g, m):
                    if begun(g):
                        dve.wait_ge(prod_ready, g + 1)
                        dve.wait_ge(sig_ready, g + 1)
                        dve.tensor_tensor(hidden[:, m % 2, :], prod[:, m % 2, :], sig[:, m % 2, :],
                                          ALU.mult).then_inc(hidden_ready, 1)

                def gu_lows(g, m, h):
                    dve.wait_ge(gu_high, 2 * g + h + 1)
                    part = slice(h * HALF, (h + 1) * HALF)
                    dve.tensor_tensor(wgu_lo[:, m % 2, part], wgu[m][:, part], f(wgu_hi[:, m % 2, part]),
                                      ALU.subtract).then_inc(gu_ready, 1)

                def row_lows(i):
                    for part in range(2):
                        dve.wait_ge(rowsT_high, 2 * i + part + 1)
                        four = slice(4 * part, 4 * part + 4)
                        dve.tensor_tensor(rowsT[:, 1, four, :], k.bank(6 + part).rearrange(
                            "p (a b) -> p a b", b=P), f(rowsT[:, 0, four, :]),
                            ALU.subtract).then_inc(rowsT_ready, 1)

                def hidden_low(g, m):
                    if begun(g):
                        dve.wait_ge(hiddenT_high, g + 1)
                        dve.tensor_tensor(hT[:, m % 2, 1, :], k.bank(2 + m % 2)[:, 0:P],
                                          f(hT[:, m % 2, 0, :]), ALU.subtract).then_inc(hiddenT_ready, 1)

                def pick_expert(i):
                    dve.wait_ge(picked_in, 16 * i + 16)
                    dve.tensor_copy(pick[:], picked[:].broadcast_to([P, P])).then_inc(pick_ready, 1)

                def steps(i):
                    for m in range(NM):
                        g = NM * i + m
                        before = (m - 1) % NM
                        activate(g - 1, before)
                        finish_hidden(g - 1, before)
                        gu_lows(g + 1, (m + 1) % NM, 0)
                        gu_lows(g + 1, (m + 1) % NM, 1)
                        if m == NM - 1:
                            row_lows(i + 1)
                            dve.wait_ge(up_ps, g + 1)
                            pick_expert(i + 1)
                        hidden_low(g - 1, before)

                dve.memset(raw_bias[2 * NE:P, :], 0.0).then_inc(bias_ready, 1)
                dve.wait_ge(bias_high, 1)
                low = slice(NE, 2 * NE)
                dve.tensor_tensor(bias[low, :], raw_bias[low, :], f(bias[low, :]), ALU.subtract
                                  ).then_inc(bias_ready, 1)
                gu_lows(0, 0, 0)
                gu_lows(0, 0, 1)
                pick_expert(0)
                row_lows(0)
                steps(0)
                with dve.Fori(1, blocks) as i:
                    steps(i)
                last = NM * last_on(dve) + (NM - 1)
                activate(last, NM - 1)
                finish_hidden(last, NM - 1)
                hidden_low(last, NM - 1)


def stage_combine(k):
    nc, d = k.nc, k.d
    with ExitStack() as ctx:
        sb = lambda n, s, dt=F32: k.sb(n, s, dt, at=ctx)
        sem = k.stage_semaphores(ctx)
        choice = sb("choice", [P, NT, TOPK, D])
        b_down = sb("b_down", [NE, D])
        acc = sb("acc", [P, 2, D])
        junk = sb("combine_junk", [P, D])
        sumsq = sb("combine_sumsq", [P, NT])
        rstd = sb("combine_rstd", [P, NT])
        b_in = sem("b_down_in")
        choice_in = [sem(f"choice_in{t}") for t in range(NT)]
        bias_ps = sem("bias_ps")
        bias_read = sem("bias_read")
        acc_ready = sem("acc_ready")
        acc_sumsq = sem("acc_sumsq")

        with nc.Block() as block:
            @block.sync
            def _(sp):
                sp.dma_start(b_down[:], d["b_down"]).then_inc(b_in, 16)

            @block.gpsimd
            def _(pool):
                for t in range(NT):
                    for c in range(TOPK):
                        pool.indirect_dma_start(
                            out=choice[:, t, c, :], out_offset=None, in_=d["expert_rows"],
                            in_offset=bass.IndirectOffsetOnAxis(ap=k.dest[:, t, c:c + 1], axis=0)
                        ).then_inc(choice_in[t], 16)

            @block.tensor
            def _(pe):
                pe.wait_ge(b_in, 16)
                for t in range(NT):
                    for n in range(2):
                        mm = pe.matmul(k.pp[t][:, n * 512:(n + 1) * 512], k.gateT[:, t * P:(t + 1) * P],
                                       b_down[:, n * 512:(n + 1) * 512], start=True, stop=True)
                    mm.then_inc(bias_ps, 1)

            @block.scalar
            def _(act):
                chain = k.act_chain.on(act)
                for t in range(NT):
                    act.wait_ge(acc_ready, t + 1)
                    chain(act.activation(junk[:], acc[:, t % 2, :], ACT.Square, accum_out=sumsq[:, t:t + 1]))
                    act.activation(rstd[:, t:t + 1], sumsq[:, t:t + 1], ACT.Sqrt, scale=1.0 / D,
                                   bias=k.eps[:, 0:1]).then_inc(acc_sumsq, 1)

            @block.vector
            def _(dve):
                chain = k.dve_chain.on(dve)
                for t in range(NT):
                    a = acc[:, t % 2, :]
                    dve.wait_ge(bias_ps, t + 1)
                    dve.wait_ge(choice_in[t], 16 * TOPK)
                    for c in range(TOPK):
                        ins = dve.scalar_tensor_tensor(a, choice[:, t, c, :], k.gates[:, t, c:c + 1],
                                                       a if c else k.pp[t][:, :], ALU.mult, ALU.add)
                        if c < TOPK - 1:
                            chain(ins)
                    ins.then_inc(acc_ready, 1)
                    dve.wait_ge(acc_sumsq, t + 1)
                    chain(dve.reciprocal(rstd[:, t:t + 1], rstd[:, t:t + 1]))
                    chain(dve.scalar_tensor_tensor(a, a, rstd[:, t:t + 1], k.gate2[:], ALU.mult, ALU.mult))
                    chain(dve.tensor_tensor(k.x[:, t, :], k.x[:, t, :], a, ALU.add))


U_A, G_A, R_F, K_F, V_F, LR_F, G_B = 0, 4, 8, 12, 16, 20, 21
HR = 8
NCH = S // CH
FEATURE_ORDER = (*range(LR_F, NF2), *range(U_A, G_A), *range(K_F, LR_F), *range(R_F, K_F),
                 *range(G_A, R_F))
POOL_AT = (10, 13, 16, 19)


def stage_second(k, scope):
    nc, d = k.nc, k.d
    k.cols = k.sb("cols", [P, NCOL])
    k.silu_b = k.sb("silu_b", [P, 4, S])
    k.y_pool = k.sb("y_pool", [P, 4, S])
    k.alpha = k.sb("alpha", [P, 4, S])
    k.beta = k.sb("beta", [P, 4, S])
    k.kappa = k.sb("kappa", [P, 4, S])
    k.rho = k.sb("rho", [P, 4, S])
    k.bonus = k.sb("bonus", [P, 4, S])
    k.last = k.sb("last_decay", [P, 4, NCH])
    k.v_tok = k.sb("v_tok", [P, NT, 4 * P])
    k.z2 = k.sb("z2", [P, 21, S + 1], at=scope)
    z2 = k.z2
    tiles = FEATURE_ORDER
    arrival = {f: n for n, f in enumerate(tiles)}
    with ExitStack() as ctx:
        sb = lambda n, s, dt=F32: k.sb(n, s, dt, at=ctx)
        sem = k.stage_semaphores(ctx)
        hT = sb("h3T", [P, 2, KT, S], F32R)
        stage = sb("stage2", [P, 3, KT, P])
        w_hi = sb("w_in_2_hi", [P, 2, KT, P], F32R)
        w_lo = sb("w_in_2_lo", [P, 2, KT, P], F32R)
        gain = flat(k.y_pool[:])[:, 0:D]
        h = lambda t: z2[:, 2 * t:2 * t + 2, 1:S + 1]
        diff = sb("diff", [P, S])
        sumsq = sb("s2_sumsq", [P, NT])
        rstd = sb("s2_rstd", [P, NT])
        inv = sb("pool_inv", [P, 4, 16])
        w_pool = sb("w_pool", [P, 4, P])
        sums = sb("sums", [P, 2, 16 + S])
        pooled = sb("pooled", [P, S])
        small_in = sem("s2_small_in")
        gain_in = sem("s2_gain_in")
        stage_in = [sem(f"s2_stage_in{n}") for n in range(3)]
        w_high = sem("s2_w_high")
        w_ready = sem("s2_w_ready")
        sumsq_done = sem("s2_sumsq_done")
        root_ready = sem("s2_root")
        h_ready = sem("s2_h_ready")
        h_ps = sem("s2_h_ps")
        hT_high = sem("s2_hT_high")
        hT_ready = sem("s2_hT_ready")
        z_ps = sem("z_ps")
        z_ready = sem("z_ready")
        sums_set = sem("sums_set")
        pooled_ready = sem("pooled_ready")
        pool_ps = sem("pool_ps")
        pool_read = sem("pool_read")

        with nc.Block() as block:
            @block.sync
            def _(sp):
                sp.dma_start(k.cols[:], d["cols"]).then_inc(small_in, 16)
                sp.dma_start(gain, row(d["norm_gain_2"][0:1, :])).then_inc(gain_in, 16)
                sp.dma_start(inv[:], d["pool_inverse"]).then_inc(small_in, 16)
                sp.dma_start(w_pool[:], d["pool_w_2"].rearrange("g c n -> c g n")).then_inc(small_in, 16)
                w = d["w_in_2"].rearrange("(k p) n -> p k n", p=P)
                for n, f in enumerate(tiles):
                    if n >= 3:
                        sp.wait_ge(w_ready, n - 2)
                    sp.dma_start(stage[:, n % 3], w[:, :, f * P:(f + 1) * P]).then_inc(stage_in[n % 3], 16)

            @block.tensor
            def _(pe):
                for t in range(NT):
                    pe.wait_ge(h_ready, t + 1)
                    for q in range(KT):
                        if t and q % 4 == 0:
                            pe.wait_ge(hT_ready, 2 * t - 1 + q // 4)
                        mm = pe.transpose(k.bank(6 + q // 4)[:, (q % 4) * P:(q % 4 + 1) * P],
                                          h(t)[:, q // 4, (q % 4) * P:(q % 4 + 1) * P], k.sq[:, IDENT, :])
                        if q % 4 == 3:
                            mm.then_inc(h_ps, 1)
                pe.wait_ge(hT_ready, 2 * NT)
                pe.wait_ge(small_in, 48)
                for n in range(NF2):
                    if n in POOL_AT:
                        g = POOL_AT.index(n)
                        pe.wait_ge(pooled_ready, g + 1)
                        pe.matmul(k.bank(4 + g), w_pool[:, g, :], pooled[:], start=True, stop=True
                                  ).then_inc(pool_ps, 1)
                    pe.wait_ge(w_ready, n + 1)
                    if n >= 4:
                        pe.wait_ge(z_ready, n - 3)
                    for q in range(KT):
                        for a, w, b in ((0, w_hi, 0), (1, w_hi, 1), (2, w_lo, 0)):
                            mm = pe.matmul(k.bank(n % 4), w[:, n % 2, q, :], hT[:, b, q, :],
                                           start=(q == 0 and a == 0), stop=(q == KT - 1 and a == 2))
                    mm.then_inc(z_ps, 1)

            @block.scalar
            def _(act):
                chain = k.act_chain.on(act)
                for t in range(NT):
                    act.activation(h(t), k.x[:, t, :].rearrange(
                        "p (a n) -> p a n", a=2), ACT.Square, accum_out=sumsq[:, t:t + 1]).then_inc(sumsq_done, 1)
                act.wait_ge(sumsq_done, NT)
                act.activation(rstd[:], sumsq[:], ACT.Sqrt, scale=1.0 / D, bias=k.eps[:, 0:1]
                               ).then_inc(root_ready, 1)

                def high(n):
                    act.wait_ge(stage_in[n % 3], 16 * (n // 3 + 1))
                    if n >= 2:
                        act.wait_ge(z_ps, n - 1)
                    act.activation(w_hi[:, n % 2], stage[:, n % 3], ACT.Copy).then_inc(w_high, 1)

                for t in range(NT):
                    for part in range(2):
                        act.wait_ge(h_ps, 2 * t + part + 1)
                        act.activation(hT[:, 0, 4 * part:4 * part + 4, t * P:(t + 1) * P],
                                       k.bank(6 + part).rearrange("p (a b) -> p a b", b=P),
                                       ACT.Copy).then_inc(hT_high, 1)
                    if t in (1, 3):
                        high(t // 2)
                for n, f in enumerate(tiles):
                    act.wait_ge(z_ps, n + 1)
                    out = k.silu_b[:, f - G_B, :] if f >= G_B else z2[:, f, 1:S + 1]
                    act.activation(out, k.bank(n % 4), ACT.Silu if f >= G_B or G_A <= f < G_A + 4
                                   else ACT.Copy).then_inc(z_ready, 1)
                    if n + 2 < NF2:
                        high(n + 2)

            @block.gpsimd
            def _(pool):
                chain = k.pool_chain.on(pool)
                chain(pool.memset(sums[:], 0.0))
                pool.wait_ge(small_in, 48)
                for g, w in enumerate(WINDOWS):
                    u = z2[:, U_A + g, 1:S + 1]
                    pool.wait_ge(z_ready, arrival[U_A + g] + 1)
                    chain(pool.tensor_copy(sums[:, 0, 16:], u))
                    for n in range(g + 1):
                        s = 1 << n
                        chain(pool.tensor_tensor(sums[:, (n + 1) % 2, 16:], sums[:, n % 2, 16:],
                                                 sums[:, n % 2, 16 - s:16 + S - s], ALU.add))
                    src = sums[:, (g + 1) % 2, 16:]
                    if g:
                        pool.wait_ge(pool_ps, g)
                    pool.tensor_scalar(pooled[:, 16:], src[:, 16:], 1.0 / w, None, ALU.mult)
                    chain(pool.tensor_tensor(pooled[:, 0:16], src[:, 0:16], inv[:, g, :], ALU.mult))
                    pool.tensor_tensor(pooled[:], pooled[:], u, ALU.subtract).then_inc(pooled_ready, 1)
                    pool.wait_ge(pooled_ready, g + 1)

            @block.vector
            def _(dve):
                chain = k.dve_chain.on(dve)
                dve.wait_ge(root_ready, 1)
                dve.memset(z2[:, :, 0:1], 0.0)
                chain(dve.reciprocal(rstd[:], rstd[:]))
                dve.wait_ge(gain_in, 16)

                def low(n):
                    dve.wait_ge(w_high, n + 1)
                    dve.tensor_tensor(w_lo[:, n % 2], stage[:, n % 3], w_hi[:, n % 2].bitcast(F32),
                                      ALU.subtract).then_inc(w_ready, 1)

                def make_h(t):
                    two = lambda ap: ap.rearrange("p (a n) -> p a n", a=2)
                    dve.scalar_tensor_tensor(h(t), two(k.x[:, t, :]), rstd[:, t:t + 1], two(gain), ALU.mult,
                                             ALU.mult).then_inc(h_ready, 1)

                make_h(0)
                for t in range(NT):
                    if t + 1 < NT:
                        make_h(t + 1)
                    for part in range(2):
                        dve.wait_ge(hT_high, 2 * t + part + 1)
                        at = (slice(4 * part, 4 * part + 4), slice(t * P, (t + 1) * P))
                        dve.tensor_tensor(hT[:, 1, at[0], at[1]],
                                          k.bank(6 + part).rearrange("p (a b) -> p a b", b=P),
                                          hT[:, 0, at[0], at[1]].bitcast(F32), ALU.subtract
                                          ).then_inc(hT_ready, 1)
                    if t in (1, 3):
                        low(t // 2)
                dve.wait_ge(small_in, 48)
                for n, f in enumerate(tiles):
                    if n + 2 < NF2:
                        low(n + 2)
                    if not R_F <= f <= LR_F:
                        continue
                    dve.wait_ge(z_ready, n + 1)
                    chain(dve.tensor_tensor(diff[:], z2[:, f, 0:S], z2[:, f, 1:S + 1], ALU.subtract))
                    c = MU0 + f - R_F
                    chain(dve.scalar_tensor_tensor(z2[:, f, 1:S + 1], diff[:], k.cols[:, c:c + 1],
                                                   z2[:, f, 1:S + 1], ALU.mult, ALU.add))
                for g in range(4):
                    dve.wait_ge(z_ready, arrival[G_A + g] + 1)
                    dve.wait_ge(pool_ps, g + 1)
                    dve.scalar_tensor_tensor(k.y_pool[:, g, :], k.bank(4 + g), k.cols[:, PS0 + g:PS0 + g + 1],
                                             z2[:, G_A + g, 1:S + 1], ALU.mult, ALU.mult).then_inc(pool_read, 1)


def rwkv_features(k):
    nc, d, z2 = k.nc, k.d, k.z2
    r = z2[:, R_F:R_F + 4, 1:S + 1]
    key = z2[:, K_F:K_F + 4, 1:S + 1]
    v = z2[:, V_F:V_F + 4, 1:S + 1]
    with ExitStack() as ctx:
        sb = lambda n, s, dt=F32: k.sb(n, s, dt, at=ctx)
        sem = k.stage_semaphores(ctx)
        w_lora = sb("w_lora", [P, 4 * P])
        rate = sb("rate", [P, 4, S])
        sigw = sb("sigw", [P, 4, S])
        cum = sb("cum", [P, 4, S])
        grow = sb("decay_grow", [P, 4, S])
        kk = sb("kk", [P, 4, S])
        root = sb("kk_root", [P, 4, S])
        keep = sb("keep", [P, S])
        one_less = sb("one_less", [P, 4])
        lora_in = sem("lora_in")
        tanh_ready = sem("tanh_ready")
        lora_ps = sem("lora_ps")
        sigw_ready = sem("sigw_ready")
        rate_ready = sem("rate_ready")
        cum_ready = sem("cum_ready")
        prev_ready = sem("prev_ready")
        decay_ready = sem("decay_ready")
        kk_ready = sem("kk_ready")
        square_ready = sem("square_ready")
        norm_ps = sem("norm_ps")
        norm_clamped = sem("norm_clamped")
        norm_root = sem("norm_root")
        pair_ready = sem("rk_ready")
        bonus_ps = sem("bonus_ps")

        with nc.Block() as block:
            @block.sync
            def _(sp):
                sp.dma_start(w_lora[0:64, :], d["w_up_2"]).then_inc(lora_in, 16)
                sp.dma_start(w_lora[64:128, :], d["a_up_2"]).then_inc(lora_in, 16)

            @block.tensor
            def _(pe):
                pe.wait_ge(lora_in, 32)
                for j in range(4):
                    mm = pe.matmul(k.bank(4 + j), w_lora[64:128, j * P:(j + 1) * P],
                                   z2[64:128, LR_F, 1:S + 1], start=True, stop=True)
                mm.then_inc(lora_ps, 1)
                pe.wait_ge(tanh_ready, 1)
                for j in range(4):
                    mm = pe.matmul(k.bank(j), w_lora[0:64, j * P:(j + 1) * P],
                                   z2[0:64, LR_F, 1:S + 1], start=True, stop=True)
                mm.then_inc(lora_ps, 1)
                pe.wait_ge(square_ready, 1)
                pe.wait_ge(rate_ready, 4)
                for j in range(4):
                    mm = pe.matmul(k.bank(4 + j), k.sq[:, BLOCK, :], root[:, j, :], start=True, stop=True)
                mm.then_inc(norm_ps, 1)
                pe.wait_ge(pair_ready, 1)
                pe.wait_ge(sigw_ready, 4)
                for j in range(4):
                    mm = pe.matmul(k.bank(j), k.sq[:, BLOCK, :], k.bonus[:, j, :], start=True, stop=True)
                mm.then_inc(bonus_ps, 1)

            @block.scalar
            def _(act):
                act.activation(z2[0:64, LR_F, 1:S + 1], z2[0:64, LR_F, 1:S + 1], ACT.Tanh).then_inc(tanh_ready, 1)
                act.wait_ge(kk_ready, 1)
                act.activation(root[:], kk[:], ACT.Square).then_inc(square_ready, 1)
                act.wait_ge(lora_ps, 1)
                for j in range(4):
                    act.activation(rate[:, j, :], k.bank(4 + j), ACT.Sigmoid,
                                   bias=k.cols[:, A00 + j:A00 + j + 1]).then_inc(rate_ready, 1)
                act.wait_ge(lora_ps, 2)
                for j in range(4):
                    act.activation(sigw[:, j, :], k.bank(j), ACT.Sigmoid,
                                   bias=k.cols[:, W00 + j:W00 + j + 1]).then_inc(sigw_ready, 1)
                act.wait_ge(norm_clamped, 1)
                act.activation(root[:], root[:], ACT.Sqrt).then_inc(norm_root, 1)
                act.wait_ge(cum_ready, 4)
                act.activation(grow[:], cum[:], ACT.Exp, scale=LOG_DECAY).then_inc(decay_ready, 1)
                act.activation(k.rho[:], cum[:], ACT.Exp, scale=-LOG_DECAY).then_inc(decay_ready, 1)
                act.wait_ge(prev_ready, 1)
                act.activation(k.alpha[:], k.alpha[:], ACT.Exp, scale=-LOG_DECAY).then_inc(decay_ready, 1)

            @block.vector
            def _(dve):
                chain = k.dve_chain.on(dve)
                col = lambda c, j: k.cols[:, c + j:c + j + 1]
                for j in range(4):
                    ins = dve.tensor_scalar(kk[:, j, :], key[:, j, :], col(KK0, j), None, ALU.mult)
                ins.then_inc(kk_ready, 1)
                dve.tensor_scalar(one_less[:], k.cols[:, KA0:KA0 + 4], -1.0, 1.0, ALU.mult, ALU.add)
                chain(dve.memset(keep[:], 1.0))
                chain(dve.memset(keep[:, 0:S:CH], 0.0))
                dve.wait_ge(rate_ready, 4)
                for j in range(4):
                    ins = dve.tensor_scalar(k.kappa[:, j, :], rate[:, j, :], col(KA0, j), one_less[:, j:j + 1],
                                            ALU.mult, ALU.add)
                chain(ins)
                chain(dve.tensor_tensor(k.kappa[:], k.kappa[:], key, ALU.mult))
                for j in range(4):
                    ins = dve.scalar_tensor_tensor(k.bonus[:, j, :], r[:, j, :], col(RK0, j), k.kappa[:, j, :],
                                                   ALU.mult, ALU.mult)
                ins.then_inc(pair_ready, 1)
                for j in range(4):
                    dve.wait_ge(sigw_ready, j + 1)
                    dve.tensor_tensor_scan(cum[:, j, :], keep[:], sigw[:, j, :], 0.0, ALU.mult,
                                           ALU.add).then_inc(cum_ready, 1)
                dve.wait_ge(cum_ready, 4)
                dve.tensor_tensor(k.alpha[:], cum[:], sigw[:], ALU.subtract).then_inc(prev_ready, 1)
                dve.wait_ge(norm_ps, 1)
                for j in range(4):
                    ins = dve.tensor_scalar(root[:, j, :], k.bank(4 + j), 1e-24, None, ALU.max)
                ins.then_inc(norm_clamped, 1)
                dve.wait_ge(norm_root, 1)
                chain(dve.reciprocal(root[:], root[:]))
                chain(dve.tensor_tensor(kk[:], kk[:], root[:], ALU.mult))
                chain(dve.tensor_tensor(k.beta[:], kk[:], rate[:], ALU.mult))
                dve.wait_ge(decay_ready, 1)
                chain(dve.tensor_tensor(k.beta[:], k.beta[:], grow[:], ALU.mult))
                chain(dve.tensor_tensor(k.kappa[:], k.kappa[:], grow[:], ALU.mult))
                dve.wait_ge(decay_ready, 2)
                chain(dve.tensor_copy(k.last[:], k.rho[:, :, CH - 1:S:CH]))
                chain(dve.tensor_tensor(k.rho[:], k.rho[:], r, ALU.mult))
                dve.wait_ge(decay_ready, 3)
                chain(dve.scalar_tensor_tensor(k.alpha[:], kk[:], -1.0, k.alpha[:], ALU.mult, ALU.mult))
                dve.wait_ge(bonus_ps, 1)
                for j in range(4):
                    ins = dve.tensor_tensor(k.bonus[:, j, :], k.bank(j), v[:, j, :], ALU.mult)
                chain(ins)


def rwkv_turn(k, name, pairs):
    nc = k.nc
    with ExitStack() as ctx:
        sem = k.stage_semaphores(ctx)
        turn_ps = sem(name + "_tok_ps")
        turn_read = sem(name + "_tok_read")
        jobs = [(dst, src, t) for dst, src in pairs for t in range(NT)]
        with nc.Block() as block:
            @block.tensor
            def _(pe):
                for n, (dst, src, t) in enumerate(jobs):
                    if n >= 8:
                        pe.wait_ge(turn_read, n - 7)
                    for j in range(4):
                        mm = pe.transpose(k.bank(n % 8)[:, j * P:(j + 1) * P], src[:, j, t * P:(t + 1) * P],
                                          k.sq[:, IDENT, :])
                    mm.then_inc(turn_ps, 1)

            @block.scalar
            def _(act):
                for n, (dst, src, t) in enumerate(jobs):
                    act.wait_ge(turn_ps, n + 1)
                    act.activation(dst[:, t, :], k.bank(n % 8), ACT.Copy).then_inc(turn_read, 1)


def rwkv_inverse(k, v_tok, solveT, out_sa, r_v, y_v):
    nc = k.nc
    with ExitStack() as ctx:
        sb = lambda n, s, dt=F32: k.sb(n, s, dt, at=ctx)
        sem = k.stage_semaphores(ctx)
        masks = sb("level_masks", [P, NSQ - LEVEL0, P])
        mT = sb("mT", [P, 2, HR, P])
        level = sb("level", [P, 2, HR, P])
        solve = sb("solve", [P, 2, HR, P])
        product = sb("product", [P, 2, HR, P])
        alpha_m = sb("alpha_m", [P, 4, 2, P])
        rho_m = sb("rho_m", [P, 4, 2, P])
        masked_zero = sem("masked_zero")
        alpha_masked = sem("alpha_masked")
        rho_masked = sem("rho_masked")
        mask_in = sem("mask_in")
        prod_ps = sem("mat_ps")
        prod_read = sem("mat_read")
        m_ready = sem("m_ready")
        level_ready = sem("level_ready")
        p_ps = sem("p_ps")
        p_ready = sem("p_ready")
        x_ps = sem("x_ps")
        x_ready = sem("solve_ready")
        v_ps = sem("vpart_ps")
        v_read = sem("vpart_read")
        heads = lambda ap: ap.rearrange("p (h n) -> p h n", h=HR)
        over_heads = lambda m: m.unsqueeze(1).broadcast_to([P, HR, P])
        NL = 5
        kinds = (("beta", "alpha"), ("alpha", "beta"), ("kappa", "alpha"), ("kappa", "rho"), ("beta", "rho"))

        with nc.Block() as block:
            @block.sync
            def _(sp):
                sp.dma_start(masks[:], k.d["square"][:, LEVEL0:NSQ, :]).then_inc(mask_in, 16)

            @block.tensor
            def _(pe):
                n = 0
                for pair in range(NT // 2):
                    for e in range(2):
                        t = 2 * pair + e
                        for m, (a, b) in enumerate(kinds):
                            if n >= 4:
                                pe.wait_ge(prod_read, n - 3)
                            pe.wait_ge(alpha_masked if m < 3 else rho_masked, 2 * t + 2)
                            tile = slice(t * P, (t + 1) * P)
                            for j in range(4):
                                if a == "alpha":
                                    for half in range(2):
                                        c = (2 * j + half) * P
                                        mm = pe.matmul(k.pp[n % 4][:, c:c + P], alpha_m[:, j, half, :],
                                                       k.beta[:, j, tile], start=True, stop=True)
                                else:
                                    left = {"beta": k.beta, "kappa": k.kappa}[a]
                                    right = {"alpha": alpha_m, "rho": rho_m}[b]
                                    mm = pe.matmul(k.pp[n % 4][:, 2 * j * P:(2 * j + 2) * P],
                                                   left[:, j, tile], right[:, j].rearrange("p a n -> p (a n)"),
                                                   start=True, stop=True)
                            mm.then_inc(prod_ps, 1)
                            n += 1
                            if m in (2, 3):
                                pe.wait_ge(prod_read, n)
                                for h in range(HR):
                                    pair_v = h // 2 * P
                                    mm = pe.matmul(k.pp[(n - 1) % 4][:, h * P:(h + 1) * P],
                                                   product[:, m - 2, h, :],
                                                   v_tok[:, t, pair_v:pair_v + P], start=True, stop=True)
                                mm.then_inc(v_ps, 1)
                                pe.wait_ge(v_read, 2 * (2 * t + m - 1))
                    for s in range(NL):
                        for e in range(2):
                            t = 2 * pair + e
                            at = (pair * NL + s) * 2 + e
                            pe.wait_ge(level_ready, at + 1)
                            pe.wait_ge(x_ready, 2 * (NL + 1) * pair + 2 * s + e + 1)
                            pe.wait_ge(prod_read, n)
                            for h in range(HR):
                                mm = pe.matmul(k.pp[2 * e][:, h * P:(h + 1) * P], level[:, e, h, :],
                                               solve[:, e, h, :], start=True, stop=True)
                            mm.then_inc(p_ps, 1)
                        for e in range(2):
                            t = 2 * pair + e
                            at = (pair * NL + s) * 2 + e
                            pe.wait_ge(p_ready, at + 1)
                            for h in range(HR):
                                mm = pe.matmul(k.pp[2 * e + 1][:, h * P:(h + 1) * P], product[:, e, h, :],
                                               solveT[:, t, h, :], start=True, stop=True)
                            if s < NL - 1:
                                for h in range(HR):
                                    mm = pe.matmul(k.pp[2 * e][:, h * P:(h + 1) * P], solveT[:, t, h, :],
                                                   product[:, e, h, :], start=True, stop=True)
                            mm.then_inc(x_ps, 1)
                    pe.wait_ge(x_ready, 2 * (NL + 1) * (pair + 1))

            @block.gpsimd
            def _(pool):
                pool.memset(alpha_m[:], 0.0).then_inc(masked_zero, 1)
                pool.memset(rho_m[:], 0.0).then_inc(masked_zero, 1)
                pool.wait_ge(mask_in, 16)
                for pair in range(NT // 2):
                    for s in range(NL):
                        for e in range(2):
                            at = (pair * NL + s) * 2 + e
                            pool.wait_ge(m_ready, 2 * pair + e + 1)
                            if at >= 2:
                                pool.wait_ge(p_ps, at - 1)
                            pool.tensor_tensor(level[:, e], mT[:, e], over_heads(masks[:, s, :]),
                                               ALU.mult).then_inc(level_ready, 1)

            @block.scalar
            def _(act):
                def masked(dst, src, t, done):
                    for half in range(2):
                        rows = slice(half * CH, (half + 1) * CH)
                        act.activation(dst[rows, :, half, :], src[rows, :, t * P:(t + 1) * P],
                                       ACT.Copy).then_inc(done, 1)

                act.wait_ge(masked_zero, 2)
                masked(alpha_m, k.alpha, 0, alpha_masked)
                masked(rho_m, k.rho, 0, rho_masked)
                for pair in range(NT // 2):
                    for e in range(2):
                        t = 2 * pair + e
                        act.wait_ge(prod_ps, 5 * t + 1)
                        if pair:
                            act.wait_ge(level_ready, 2 * NL)
                        act.activation(mT[:, e], heads(k.pp[(5 * t) % 4][:, :]), ACT.Copy).then_inc(m_ready, 1)
                        for m in range(2):
                            act.wait_ge(v_ps, 2 * t + m + 1)
                            both = k.pp[(5 * t + 2 + m) % 4][:, :].rearrange("p (j h n) -> p j h n", j=4, h=2)
                            for half in range(2):
                                out = (r_v, y_v)[m][:, t, :].rearrange("p (j h n) -> p j h n", j=4, h=2)
                                act.activation(out[:, :, half, :], both[:, :, half, half * CH:(half + 1) * CH],
                                               ACT.Copy).then_inc(v_read, 1)
                            if t + 1 < NT and m == 0:
                                act.wait_ge(prod_ps, 5 * t + 3)
                                masked(alpha_m, k.alpha, t + 1, alpha_masked)
                        if t + 1 < NT:
                            act.wait_ge(prod_ps, 5 * t + 5)
                            masked(rho_m, k.rho, t + 1, rho_masked)
                    for s in range(NL):
                        for e in range(2):
                            at = (pair * NL + s) * 2 + e
                            act.wait_ge(p_ps, at + 1)
                            act.activation(product[:, e], heads(k.pp[2 * e][:, :]), ACT.Copy).then_inc(p_ready, 1)

            @block.vector
            def _(dve):
                chain = k.dve_chain.on(dve)
                dve.wait_ge(mask_in, 16)
                for pair in range(NT // 2):
                    for e in range(2):
                        t = 2 * pair + e
                        for m in range(5):
                            n = 5 * t + m
                            dve.wait_ge(prod_ps, n + 1)
                            src = heads(k.pp[n % 4][:, :])
                            if m < 2:
                                out = (solveT[:, t], solve[:, e])[m]
                                if m == 0:
                                    dve.wait_ge(m_ready, t + 1)
                                    src = mT[:, e]
                                chain(dve.tensor_tensor(out, src, over_heads(masks[:, NL + m, :]), ALU.mult))
                                chain(dve.tensor_tensor(out, out, over_heads(k.sq[:, IDENT, :]), ALU.add))
                                dve.sem_inc(prod_read, 1)
                                if m == 1:
                                    dve.sem_inc(x_ready, 1)
                            elif m < 4:
                                if t:
                                    dve.wait_ge(v_ps, 2 * t - 2 + m - 1)
                                dve.tensor_tensor(product[:, m - 2], src, over_heads(
                                    k.sq[:, (LT, LE)[m - 2], :]), ALU.mult).then_inc(prod_read, 1)
                            else:
                                dve.tensor_tensor(out_sa[:, t], src, over_heads(k.sq[:, LE, :]),
                                                  ALU.mult).then_inc(prod_read, 1)
                    for s in range(NL):
                        for e in range(2):
                            t = 2 * pair + e
                            at = (pair * NL + s) * 2 + e
                            dve.wait_ge(x_ps, at + 1)
                            ins = dve.tensor_tensor(solveT[:, t], solveT[:, t], heads(k.pp[2 * e + 1][:, :]), ALU.add)
                            if s < NL - 1:
                                ins = dve.tensor_tensor(solve[:, e], solve[:, e], heads(k.pp[2 * e][:, :]), ALU.add)
                            ins.then_inc(x_ready, 1)
                            dve.wait_ge(x_ready, 2 * (NL + 1) * pair + 2 + 2 * s + e + 1)


def stage_rwkv(k):
    nc, d, v_tok = k.nc, k.d, k.v_tok
    with ExitStack() as ctx:
        sb = lambda n, s, dt=F32: k.sb(n, s, dt, at=ctx)
        beta_tok = sb("beta_tok", [P, NT, 4 * P])
        kappa_tok = sb("kappa_tok", [P, NT, 4 * P])
        solveT = sb("solveT", [P, NT, HR, P])
        out_sa = sb("out_sa", [P, NT, HR, P])
        y_v = sb("y_v", [P, NT, HR * CH])
        with ExitStack() as inner:
            known = k.sb("known", [P, NT, 2, HR, CH], at=inner)
            part = lambda n: known[:, :, n].rearrange("p t h n -> p t (h n)")
            rwkv_turn(k, "bk", ((beta_tok, k.beta), (kappa_tok, k.kappa), (part(1), k.alpha)))
            rwkv_inverse(k, v_tok, solveT, out_sa, part(0), y_v)
            solved = k.sb("solved", [P, NT, 2, HR, CH], at=inner)
            rwkv_fold(k, solveT, out_sa, known, solved, y_v)
            rwkv_states(k, v_tok, beta_tok, kappa_tok, solved, y_v)
        output(k, y_v)


def rwkv_fold(k, solveT, out_sa, known, solved, y_v):
    nc = k.nc
    with ExitStack() as ctx:
        sem = k.stage_semaphores(ctx)
        out_w = k.sb("out_w", [P, NT, HR, CH], at=ctx)
        solved_ps = sem("solved_ps")
        solved_ready = sem("solved_ready")
        out_ps = sem("fold_out_ps")
        out_w_ready = sem("out_w_ready")
        y_added = sem("y_added")
        w_ps = sem("fold_w_ps")
        w_copied = sem("fold_w_copied")
        rho_ps = sem("fold_rho_ps")
        by_head = lambda ap: ap.rearrange("p (h two n) -> p two h n", two=2, n=CH)
        by_tile = lambda ap: ap.rearrange("p (j n) -> p j n", j=4)

        with nc.Block() as block:
            @block.tensor
            def _(pe):
                def products(bank2, left, t, right):
                    for h in range(HR):
                        mm = pe.matmul(bank2[:, h * P:(h + 1) * P].rearrange("p (two n) -> p two n", two=2),
                                       left[:, t, h, :], right[:, t, :, h, :], start=True, stop=True)
                    return mm

                def turn(bank, src):
                    flat_src = src.rearrange("p h n -> p (h n)")
                    for j in range(4):
                        mm = pe.transpose(bank[:, j * P:(j + 1) * P], flat_src[:, j * P:(j + 1) * P],
                                          k.sq[:, IDENT, :])
                    return mm

                for t in range(NT):
                    if t >= 2:
                        pe.wait_ge(solved_ready, t - 1)
                    products(k.pp[t % 2], solveT, t, known).then_inc(solved_ps, 1)
                for t in range(NT):
                    pe.wait_ge(solved_ready, t + 1)
                    if t >= 2:
                        pe.wait_ge(y_added, t - 1)
                    products(k.pp[2 + t % 2], out_sa, t, solved).then_inc(out_ps, 1)
                for t in range(NT):
                    turn(k.bank(t), solved[:, t, 1]).then_inc(w_ps, 1)
                for t in range(NT):
                    pe.wait_ge(y_added, min(t + 3, NT))
                    turn(k.bank(4 + t), out_w[:, t]).then_inc(rho_ps, 1)

            @block.scalar
            def _(act):
                for t in range(NT):
                    act.wait_ge(solved_ps, t + 1)
                    act.activation(solved[:, t], by_head(k.pp[t % 2][:, :]), ACT.Copy).then_inc(solved_ready, 1)
                for t in range(NT):
                    act.wait_ge(out_ps, t + 1)
                    act.activation(out_w[:, t], by_head(k.pp[2 + t % 2][:, :])[:, 1], ACT.Copy
                                   ).then_inc(out_w_ready, 1)
                for t in range(NT):
                    act.wait_ge(w_ps, t + 1)
                    act.activation(k.alpha[:, :, t * P:(t + 1) * P], by_tile(k.bank(t)), ACT.Copy
                                   ).then_inc(w_copied, 1)

            @block.vector
            def _(dve):
                for t in range(NT):
                    dve.wait_ge(out_w_ready, t + 1)
                    y = y_v[:, t, :].rearrange("p (h n) -> p h n", h=HR)
                    dve.tensor_tensor(y, y, by_head(k.pp[2 + t % 2][:, :])[:, 0], ALU.add).then_inc(y_added, 1)
                for t in range(NT):
                    dve.wait_ge(rho_ps, t + 1)
                    rho = k.rho[:, :, t * P:(t + 1) * P]
                    dve.tensor_tensor(rho, rho, by_tile(k.bank(4 + t)), ALU.add)


def rwkv_states(k, v_tok, beta_tok, kappa_tok, solved, y_v):
    nc = k.nc
    with ExitStack() as ctx:
        sb = lambda n, s, dt=F32: k.sb(n, s, dt, at=ctx)
        sem = k.stage_semaphores(ctx)
        state = sb("rwkv_state", [P, 4, P])
        sa = sb("sa", [P, HR * CH])
        state_ready = sem("rwkv_state_ready")
        sa_ps = sem("sa_ps")
        sa_ready = sem("sa_ready")
        y_ps = sem("rwkv_y_ps")
        y_read = sem("rwkv_y_read")
        next_ps = sem("next_ps")
        halves = [slice(0, CH), slice(CH, P)]

        with nc.Block() as block:
            @block.tensor
            def _(pe):
                def outer(c, left, right, start, stop):
                    rows = halves[c % 2]
                    for h in range(HR):
                        mm = pe.matmul(k.bank(2 + c % 2)[halves[h % 2], h // 2 * CH:(h // 2 + 1) * CH],
                                       left[rows, c // 2, h * CH:(h + 1) * CH], right(rows, h),
                                       start=(start and h < 2), stop=(stop and h >= HR - 2),
                                       skip_group_check=True)
                    return mm

                def with_v(c):
                    outer(c, kappa_tok, lambda rows, h: v_tok[rows, c // 2, h * CH:(h + 1) * CH], True, False)

                with_v(0)
                for c in range(NCH):
                    rows = halves[c % 2]
                    pe.wait_ge(state_ready, c + 1)
                    for j in range(4):
                        mm = pe.matmul(k.bank(0)[rows, j * P:(j + 1) * P], k.alpha[:, j, c * CH:(c + 1) * CH],
                                       state[:, j, :], start=True, stop=True)
                    mm.then_inc(sa_ps, 1)
                    if c:
                        pe.wait_ge(y_read, c)
                    for j in range(4):
                        mm = pe.matmul(k.bank(1)[rows, j * P:(j + 1) * P], k.rho[:, j, c * CH:(c + 1) * CH],
                                       state[:, j, :], start=True, stop=True)
                    mm.then_inc(y_ps, 1)
                    pe.wait_ge(sa_ready, c + 1)
                    outer(c, beta_tok, lambda rows, h: sa[rows, h * CH:(h + 1) * CH], False, True
                          ).then_inc(next_ps, 1)
                    if c + 1 < NCH:
                        with_v(c + 1)

            @block.vector
            def _(dve):
                chain = k.dve_chain.on(dve)
                dve.memset(state[:], 0.0).then_inc(state_ready, 1)
                for c in range(NCH):
                    t, rows = c // 2, halves[c % 2]
                    dve.wait_ge(sa_ps, c + 1)
                    dve.tensor_tensor(sa[rows], k.bank(0)[rows, :], solved[rows, t, 0].rearrange(
                        "p h n -> p (h n)"), ALU.add).then_inc(sa_ready, 1)
                    dve.wait_ge(next_ps, c + 1)
                    dve.wait_ge(state_ready, c + 1)
                    for half in halves:
                        own = state[half, :, half]
                        ins = dve.tensor_tensor(own, own, k.bank(2 + c % 2)[half, 0:4 * CH].rearrange(
                            "p (j n) -> p j n", j=4), ALU.add)
                    chain(ins)
                    for half in halves:
                        own = state[half, :, half]
                        ins = dve.tensor_tensor(own, own, k.last[half, :, c:c + 1].broadcast_to([CH, 4, CH]),
                                                ALU.mult)
                    ins.then_inc(state_ready, 1)
                    dve.wait_ge(y_ps, c + 1)
                    dve.tensor_tensor(y_v[rows, t, :], y_v[rows, t, :], k.bank(1)[rows, :], ALU.add
                                      ).then_inc(y_read, 1)


def output(k, y):
    nc, d = k.nc, k.d
    k.w_out2_in = k.sem("w_out2_in")
    with ExitStack() as ctx:
        sb = lambda n, s, dt=F32: k.sb(n, s, dt, at=ctx)
        sem = k.stage_semaphores(ctx)
        w_out2 = sb("w_out2", [P, KT, D])
        square = sb("gn_square", [P, HR * CH])
        mean = sb("gn_mean", [P, HR])
        var = sb("gn_var", [P, HR])
        normed = sb("normed", [P, 2, HR * CH])
        final = sb("final", [P, 2, D])
        gain = sb("final_gain", [P, D])
        junk = flat(k.alpha[:])[:, 0:D]
        sumsq = sb("final_sumsq", [P, NT])
        rstd = sb("final_rstd", [P, NT])
        w_in = sem("final_w_in")
        centred = sem("centred")
        squared = sem("squared")
        var_ready = sem("var_ready")
        gn_root = sem("gn_root")
        normed_ready = sem("normed_ready")
        turned_ps = sem("gn_turned_ps")
        y_ready = sem("y_rwkv_ready")
        out_ps = sem("out_ps")
        sum_ready = sem("sum_ready")
        final_root = sem("final_root")
        final_ready = sem("final_ready")
        out_done = sem("out_done")
        yb = k.beta
        heads = lambda ap: ap.rearrange("p (h n) -> p h n", h=HR)

        with nc.Block() as block:
            @block.sync
            def _(sp):
                sp.dma_start(w_out2[:], d["w_out_2"].rearrange("(k p) n -> p k n", p=P)).then_inc(w_in, 16)
                sp.dma_start(gain[:], row(d["final_gain_2"][0:1, :])).then_inc(w_in, 16)
                for t in range(NT):
                    sp.wait_ge(final_ready, t + 1)
                    sp.dma_start(d["out"][t * P:(t + 1) * P, :], final[:, t % 2, :]).then_inc(out_done, 16)
                    sp.wait_ge(out_done, 16 * (t + 1))

            @block.tensor
            def _(pe):
                for t in range(NT):
                    pe.wait_ge(normed_ready, t + 1)
                    for j in range(4):
                        mm = pe.transpose(k.bank(j)[:, t * P:(t + 1) * P], normed[:, t % 2, j * P:(j + 1) * P],
                                          k.sq[:, IDENT, :])
                    mm.then_inc(turned_ps, 1)
                pe.wait_ge(w_in, 32)
                for t in range(NT):
                    if t >= 2:
                        pe.wait_ge(sum_ready, t - 1)
                    for n in range(2):
                        for q in range(KT):
                            if q == 4 and t == 0 and n == 0:
                                pe.wait_ge(y_ready, 1)
                            src = k.y_pool[:, q, :] if q < 4 else yb[:, q - 4, :]
                            mm = pe.matmul(k.pp[2 + t % 2][:, n * 512:(n + 1) * 512], src[:, t * P:(t + 1) * P],
                                           w_out2[:, q, n * 512:(n + 1) * 512],
                                           start=(q == 0), stop=(q == KT - 1))
                    mm.then_inc(out_ps, 1)

            @block.scalar
            def _(act):
                chain = k.act_chain.on(act)
                for t in range(NT):
                    act.wait_ge(centred, t + 1)
                    act.activation(square[:], y[:, t, :], ACT.Square).then_inc(squared, 1)
                    act.wait_ge(var_ready, t + 1)
                    act.activation(var[:], var[:], ACT.Sqrt, scale=1.0 / CH, bias=k.eps[:, 1:2]).then_inc(gn_root, 1)
                for t in range(NT):
                    act.wait_ge(sum_ready, t + 1)
                    chain(act.activation(junk, k.x[:, t, :], ACT.Square, accum_out=sumsq[:, t:t + 1]))
                    act.activation(rstd[:, t:t + 1], sumsq[:, t:t + 1], ACT.Sqrt, scale=1.0 / D,
                                   bias=k.eps[:, 0:1]).then_inc(final_root, 1)

            @block.vector
            def _(dve):
                chain = k.dve_chain.on(dve)
                for t in range(NT):
                    yt = heads(y[:, t, :])
                    chain(dve.tensor_reduce(mean[:], yt, AX.X, ALU.add))
                    chain(dve.tensor_scalar(mean[:], mean[:], 1.0 / CH, None, ALU.mult))
                    dve.tensor_tensor(yt, yt, mean[:].unsqueeze(2).broadcast_to([P, HR, CH]),
                                      ALU.subtract).then_inc(centred, 1)
                    dve.wait_ge(squared, t + 1)
                    dve.tensor_reduce(var[:], heads(square[:]), AX.X, ALU.add).then_inc(var_ready, 1)
                    dve.wait_ge(gn_root, t + 1)
                    chain(dve.reciprocal(var[:], var[:]))
                    if t >= 2:
                        dve.wait_ge(turned_ps, t - 1)
                    dve.tensor_tensor(heads(normed[:, t % 2, :]), yt, var[:].unsqueeze(2).broadcast_to(
                        [P, HR, CH]), ALU.mult).then_inc(normed_ready, 1)
                    dve.wait_ge(normed_ready, t + 1)
                dve.wait_ge(turned_ps, NT)
                for j in range(4):
                    ins = dve.tensor_scalar(yb[:, j, :], k.bank(j), k.cols[:, GG0 + j:GG0 + j + 1],
                                            k.cols[:, GB0 + j:GB0 + j + 1], ALU.mult, ALU.add)
                chain(ins)
                chain(dve.tensor_tensor(yb[:], yb[:], k.bonus[:], ALU.add))
                dve.tensor_tensor(yb[:], yb[:], k.silu_b[:], ALU.mult).then_inc(y_ready, 1)
                dve.wait_ge(w_in, 32)
                for t in range(NT):
                    dve.wait_ge(out_ps, t + 1)
                    dve.tensor_tensor(k.x[:, t, :], k.x[:, t, :], k.pp[2 + t % 2][:, :], ALU.add
                                      ).then_inc(sum_ready, 1)
                    dve.wait_ge(final_root, t + 1)
                    chain(dve.reciprocal(rstd[:, t:t + 1], rstd[:, t:t + 1]))
                    if t >= 2:
                        dve.wait_ge(out_done, 16 * (t - 1))
                    dve.scalar_tensor_tensor(final[:, t % 2, :], k.x[:, t, :], rstd[:, t:t + 1], gain[:],
                                             ALU.mult, ALU.mult).then_inc(final_ready, 1)
                    dve.wait_ge(final_ready, t + 1)


def build(nc, dram):
    with ExitStack() as ctx:
        k = Core(nc, ctx, dram)
        persistent(k)
        with ExitStack() as weights:
            early_weights(k, weights)
            with ExitStack() as front:
                stage_front(k, front)
                stage_mixers(k, front)
                stage_router(k, front)
            stage_experts(k)
        stage_combine(k)
        with ExitStack() as scope:
            stage_second(k, scope)
            rwkv_features(k)
            rwkv_turn(k, "v", ((k.v_tok, k.z2[:, V_F:V_F + 4, 1:S + 1]),))
        stage_rwkv(k)


def packed_columns(a):
    names = ["shift_mu_2", "w0_2", "a0_2", "k_k_2", "k_a_2", "r_k_2", "gn_gain_2", "gn_bias_2",
             "pool_scale_2", "c"]
    return np.ascontiguousarray(np.concatenate([np.asarray(a[n]).reshape(-1, P) for n in names]).T)


def kernel(**inputs):
    import concourse.bacc as bacc
    from concourse.bass_utils import run_bass_kernel_spmd

    a = {n: np.asarray(v) for n, v in inputs.items()}
    arrays = {
        "x": a["x"][0],
        "cols": packed_columns(a),
        "w_gate_up": a["w_gate_up"][0].reshape(NE, KT, P, NM, P, 2).transpose(0, 3, 2, 1, 5, 4).reshape(
            NE * NM * P, KT * 2 * P),
        "w_down": a["w_down"][0].reshape(NE * NM * P, D),
        "b_gate_up": a["b_gate_up"][0].reshape(NE, NM, P, 2).transpose(0, 1, 3, 2).reshape(NE, NM * 2 * P),
        "picked": picked_constant(),
        "square": square_constants(),
        "log_count": attention_constant(),
        "rope": rope_constant(),
        "count": count_constant(),
        "pool_inverse": pool_constant(),
        "token": np.ascontiguousarray(np.arange(S, dtype=np.int32).reshape(NT, P).T),
        "w_gate_lr": np.concatenate([a["w_gate_lr"][0], a["b_gate"]]),
    }
    for n in ("w_mod", "w_in", "w_out", "router_w", "b_down", "w_in_2", "pool_w_2", "w_up_2", "a_up_2",
              "w_out_2"):
        arrays[n] = a[n][0]
    for n in ("b_mod", "g_pre_mix", "g_gla", "g_post_mix", "g_pre_ffn", "router_b", "g_post_ffn",
              "norm_gain_2", "final_gain_2"):
        arrays[n] = a[n].reshape(1, -1)

    nc = bacc.Bacc("TRN2", target_bir_lowering=False, num_devices=1)
    dram, sent = {}, {}
    for n, v in arrays.items():
        v = np.ascontiguousarray(v)
        sent["in_" + n] = v
        dram[n] = nc.dram_tensor("in_" + n, v.shape, mybir.dt.from_np(v.dtype), kind="ExternalInput").ap()
    dram["out"] = nc.dram_tensor("out", [S, D], F32, kind="ExternalOutput").ap()
    dram["h2"] = nc.dram_tensor("h2_rows", [S, D], F32, kind="Internal").ap()
    dram["slot_token"] = nc.dram_tensor("slot_token", [(NBLK + 1) * SLOTS, 1], I32, kind="Internal").ap()
    dram["expert_rows"] = nc.dram_tensor("expert_rows", [NBLK * SLOTS, D], F32, kind="Internal").ap()
    build(nc, dram)
    result = run_bass_kernel_spmd(nc, [sent], core_ids=[0])
    return result.results[0]["out"].reshape(1, S, D)
```
